# Optimizing a Trainium2 kernel written in Bass

```python
import jax, jax.numpy as jnp
from jax import lax
import numpy as np

D_MODEL = 1024
BATCH = 1
SEQ = 1024
DEPTH = 1

CHUNK = 64
N_META = 16
Q_BLOCK = 128
C_CONV = D_MODEL // 2
CONV_K = 31
N_HEADS = D_MODEL // 128
QK_NOPE = 64
QK_ROPE = 32
V_DIM = 64
Q_LORA = 3 * D_MODEL // 8
KV_LORA = D_MODEL // 4
ROPE_THETA = 10000.0
D_ATTN = N_HEADS * V_DIM
D_MIX = C_CONV + D_ATTN
N_IN = 2 * C_CONV + Q_LORA + KV_LORA + QK_ROPE
N_GROUPS = 4
EXPERTS_PER_GROUP = 8
N_EXPERTS = N_GROUPS * EXPERTS_PER_GROUP
TOP_K = 2
D_EXPERT = D_MODEL // 4
MOE_BLOCK = 128
DEEPNORM_ALPHA = (2.0 * DEPTH) ** 0.25
DEEPNORM_BETA = (8.0 * DEPTH) ** -0.25
EPS = 1e-5
NEG_INF = -1e30

kernel_name = 'hybrid_conv_mla_hmoe_deepnorm'

def _layer_norm(x, g, b):
    xf = x.astype(jnp.float32)
    mu = jnp.mean(xf, axis=-1, keepdims=True)
    var = jnp.mean(jnp.square(xf - mu), axis=-1, keepdims=True)
    return ((xf - mu) * lax.rsqrt(var + EPS)).astype(x.dtype) * g + b

def _rms_norm(x, g):
    xf = x.astype(jnp.float32)
    return (xf * lax.rsqrt(jnp.mean(xf * xf, axis=-1, keepdims=True) + EPS)).astype(x.dtype) * g

def _chunk_id(pos):
    return jnp.where(pos < N_META, 0, (pos - N_META) // CHUNK + 1)

def _rope_tables(length, dtype):
    half = QK_ROPE // 2
    inv_freq = ROPE_THETA ** (-jnp.arange(half, dtype=jnp.float32) / half)
    ang = jnp.arange(length, dtype=jnp.float32)[:, None] * inv_freq[None, :]
    return jnp.cos(ang).astype(dtype), jnp.sin(ang).astype(dtype)

def _apply_rope(x, cos, sin):
    x1, x2 = jnp.split(x, 2, axis=-1)
    return jnp.concatenate([x1 * cos - x2 * sin, x1 * sin + x2 * cos], axis=-1)

def _causal_depthwise_conv(u, w, b):
    y = lax.conv_general_dilated(u, w[:, None, :], window_strides=(1,), padding=[(CONV_K - 1, 0)],
                                 dimension_numbers=('NWC', 'WIO', 'NWC'), feature_group_count=u.shape[-1])
    return y + b

def _chunk_causal_mla(q_nope, q_rope, k_nope, k_rope, v):
    B, L, H, _ = q_nope.shape
    n_blk = -(-L // Q_BLOCK)
    lp = n_blk * Q_BLOCK

    def to_blocks(t):
        t = jnp.pad(t, [(0, 0), (0, lp - L)] + [(0, 0)] * (t.ndim - 2))
        return jnp.swapaxes(t.reshape((B, n_blk, Q_BLOCK) + t.shape[2:]), 0, 1)

    qn_b, qr_b = to_blocks(q_nope), to_blocks(q_rope)
    q_pos = jnp.arange(lp, dtype=jnp.int32).reshape(n_blk, Q_BLOCK)
    k_chunk = _chunk_id(jnp.arange(L, dtype=jnp.int32))
    scale = (QK_NOPE + QK_ROPE) ** -0.5

    def attend(args):
        qn, qr, qp = args
        s = (jnp.einsum('bqhd,bkhd->bhqk', qn, k_nope)
             + jnp.einsum('bqhd,bkd->bhqk', qr, k_rope)).astype(jnp.float32) * scale
        visible = k_chunk[None, :] <= _chunk_id(qp)[:, None]
        p = jax.nn.softmax(jnp.where(visible, s, NEG_INF), axis=-1).astype(v.dtype)
        return jnp.einsum('bhqk,bkhd->bqhd', p, v)

    o = lax.map(attend, (qn_b, qr_b, q_pos))
    return jnp.swapaxes(o, 0, 1).reshape(B, lp, H, V_DIM)[:, :L]

def _mixer(h, cos, sin, w_in, conv_w, conv_b, conv_ln_g, conv_ln_b, q_norm_g, w_uq,
           kv_norm_g, w_ukv, conv_out_g, attn_out_g, w_o):
    B, L, _ = h.shape
    z = h @ w_in
    c1 = C_CONV
    c2 = 2 * C_CONV
    c3 = c2 + Q_LORA
    c4 = c3 + KV_LORA
    a, gate, cq, ckv, kr = jnp.split(z, [c1, c2, c3, c4], axis=-1)
    u = a * jax.nn.sigmoid(gate)
    c = jax.nn.silu(_layer_norm(_causal_depthwise_conv(u, conv_w, conv_b), conv_ln_g, conv_ln_b))
    q = (_rms_norm(cq, q_norm_g) @ w_uq).reshape(B, L, N_HEADS, QK_NOPE + QK_ROPE)
    q_nope = q[..., :QK_NOPE]
    q_rope = _apply_rope(q[..., QK_NOPE:], cos[:, None, :], sin[:, None, :])
    kv = (_rms_norm(ckv, kv_norm_g) @ w_ukv).reshape(B, L, N_HEADS, QK_NOPE + V_DIM)
    k_nope, v = kv[..., :QK_NOPE], kv[..., QK_NOPE:]
    k_rope = _apply_rope(kr, cos, sin)
    o = _chunk_causal_mla(q_nope, q_rope, k_nope, k_rope, v).reshape(B, L, D_ATTN)
    merged = jnp.concatenate([_rms_norm(c, conv_out_g), _rms_norm(o, attn_out_g)], axis=-1)
    return merged @ w_o

def _hier_moe(h, w_rg, b_rg, w_re, b_re, w_gate, w_up, w_down):
    B, L, D = h.shape
    T = B * L
    xt = h.reshape(T, D)
    g_logits = (xt @ w_rg).astype(jnp.float32) + b_rg.astype(jnp.float32)
    g_prob = jax.nn.softmax(g_logits, axis=-1)
    g_idx = jnp.argmax(g_logits, axis=-1).astype(jnp.int32)
    g_w = jnp.take_along_axis(g_prob, g_idx[:, None], axis=1)[:, 0]
    e_logits = ((xt @ w_re).astype(jnp.float32) + b_re.astype(jnp.float32)).reshape(T, N_GROUPS, EXPERTS_PER_GROUP)
    e_in = jnp.take_along_axis(e_logits, g_idx[:, None, None], axis=1)[:, 0]
    top_v, top_i = lax.top_k(e_in, TOP_K)
    comb = g_w[:, None] * jax.nn.softmax(top_v, axis=-1)
    eid = (g_idx[:, None] * EXPERTS_PER_GROUP + top_i).reshape(-1).astype(jnp.int32)
    A = T * TOP_K
    tok = jnp.repeat(jnp.arange(T, dtype=jnp.int32), TOP_K)
    order = jnp.argsort(eid)
    e_sorted = eid[order]
    counts = jnp.bincount(eid, length=N_EXPERTS).astype(jnp.int32)
    padded = (counts + MOE_BLOCK - 1) // MOE_BLOCK * MOE_BLOCK
    pad_end = jnp.cumsum(padded)
    pad_start = pad_end - padded
    start = jnp.cumsum(counts) - counts
    dest = pad_start[e_sorted] + (jnp.arange(A, dtype=jnp.int32) - start[e_sorted])
    n_blocks = -(-A // MOE_BLOCK) + N_EXPERTS
    R = n_blocks * MOE_BLOCK
    tok_buf = jnp.zeros((R,), jnp.int32).at[dest].set(tok[order])
    w_buf = jnp.zeros((R,), h.dtype).at[dest].set(comb.reshape(-1)[order].astype(h.dtype))
    blk_e = jnp.clip(jnp.searchsorted(pad_end, jnp.arange(n_blocks, dtype=jnp.int32) * MOE_BLOCK, side='right'),
                     0, N_EXPERTS - 1)
    x_buf = xt[tok_buf].reshape(n_blocks, MOE_BLOCK, D)

    def expert_block(args):
        xb, e = args
        act = jax.nn.silu(xb @ w_gate[e]) * (xb @ w_up[e])
        return act @ w_down[e]

    y_buf = lax.map(expert_block, (x_buf, blk_e)).reshape(R, D)
    out = jnp.zeros((T, D), h.dtype).at[tok_buf].add(y_buf * w_buf[:, None])
    return out.reshape(B, L, D)

def setup_inputs(seed: int = 0) -> dict:
    key = jax.random.key(seed)
    ks = jax.random.split(key, 32)
    f32 = jnp.float32

    def nrm(k, shape, scale):
        return jax.random.normal(k, shape, f32) * scale

    def gain(k, shape):
        return 1.0 + 0.05 * jax.random.normal(k, shape, f32)

    beta = DEEPNORM_BETA
    in_scale = jnp.concatenate([jnp.full((C_CONV,), beta, f32), jnp.ones((N_IN - C_CONV,), f32)])
    kv_scale = jnp.tile(jnp.concatenate([jnp.ones((QK_NOPE,), f32), jnp.full((V_DIM,), beta, f32)]), N_HEADS)
    return {
        'x': nrm(ks[0], (BATCH, SEQ, D_MODEL), 1.0),
        'meta_tokens': nrm(ks[1], (N_META, D_MODEL), 1.0),
        'ln_in_g': gain(ks[2], (D_MODEL,)),
        'ln_in_b': nrm(ks[3], (D_MODEL,), 0.01),
        'w_in': nrm(ks[4], (DEPTH, D_MODEL, N_IN), D_MODEL ** -0.5) * in_scale,
        'conv_w': nrm(ks[5], (DEPTH, CONV_K, C_CONV), CONV_K ** -0.5),
        'conv_b': nrm(ks[6], (DEPTH, C_CONV), 0.01),
        'conv_ln_g': gain(ks[7], (DEPTH, C_CONV)),
        'conv_ln_b': nrm(ks[8], (DEPTH, C_CONV), 0.01),
        'q_norm_g': gain(ks[9], (DEPTH, Q_LORA)),
        'w_uq': nrm(ks[10], (DEPTH, Q_LORA, N_HEADS * (QK_NOPE + QK_ROPE)), Q_LORA ** -0.5),
        'kv_norm_g': gain(ks[11], (DEPTH, KV_LORA)),
        'w_ukv': nrm(ks[12], (DEPTH, KV_LORA, N_HEADS * (QK_NOPE + V_DIM)), KV_LORA ** -0.5) * kv_scale,
        'conv_out_g': gain(ks[13], (DEPTH, C_CONV)),
        'attn_out_g': gain(ks[14], (DEPTH, D_ATTN)),
        'w_o': nrm(ks[15], (DEPTH, D_MIX, D_MODEL), D_MIX ** -0.5 * beta),
        'ln1_g': gain(ks[16], (DEPTH, D_MODEL)),
        'ln1_b': nrm(ks[17], (DEPTH, D_MODEL), 0.01),
        'w_rg': nrm(ks[18], (DEPTH, D_MODEL, N_GROUPS), D_MODEL ** -0.5),
        'b_rg': nrm(ks[19], (DEPTH, N_GROUPS), 0.01),
        'w_re': nrm(ks[20], (DEPTH, D_MODEL, N_EXPERTS), D_MODEL ** -0.5),
        'b_re': nrm(ks[21], (DEPTH, N_EXPERTS), 0.01),
        'w_gate': nrm(ks[22], (DEPTH, N_EXPERTS, D_MODEL, D_EXPERT), D_MODEL ** -0.5),
        'w_up': nrm(ks[23], (DEPTH, N_EXPERTS, D_MODEL, D_EXPERT), D_MODEL ** -0.5 * beta),
        'w_down': nrm(ks[24], (DEPTH, N_EXPERTS, D_EXPERT, D_MODEL), D_EXPERT ** -0.5 * beta),
        'ln2_g': gain(ks[25], (DEPTH, D_MODEL)),
        'ln2_b': nrm(ks[26], (DEPTH, D_MODEL), 0.01),
    }

def reference(x, meta_tokens, ln_in_g, ln_in_b, w_in, conv_w, conv_b, conv_ln_g, conv_ln_b,
              q_norm_g, w_uq, kv_norm_g, w_ukv, conv_out_g, attn_out_g, w_o, ln1_g, ln1_b,
              w_rg, b_rg, w_re, b_re, w_gate, w_up, w_down, ln2_g, ln2_b):
    B = x.shape[0]
    meta = jnp.broadcast_to(meta_tokens.astype(x.dtype)[None], (B, N_META, x.shape[-1]))
    h = _layer_norm(jnp.concatenate([meta, x], axis=1), ln_in_g, ln_in_b)
    cos, sin = _rope_tables(h.shape[1], h.dtype)
    for l in range(DEPTH):
        y = _mixer(h, cos, sin, w_in[l], conv_w[l], conv_b[l], conv_ln_g[l], conv_ln_b[l],
                   q_norm_g[l], w_uq[l], kv_norm_g[l], w_ukv[l], conv_out_g[l], attn_out_g[l], w_o[l])
        h = _layer_norm(DEEPNORM_ALPHA * h + y, ln1_g[l], ln1_b[l])
        y = _hier_moe(h, w_rg[l], b_rg[l], w_re[l], b_re[l], w_gate[l], w_up[l], w_down[l])
        h = _layer_norm(DEEPNORM_ALPHA * h + y, ln2_g[l], ln2_b[l])
    return h[:, N_META:]


_drawn_inputs = setup_inputs


def setup_inputs(seed=0):
    import zlib

    import numpy as np

    out = dict(_drawn_inputs(seed))
    spreads = {}
    factors = {'conv_b': 4.579,
     'conv_ln_g': 2.727,
     'conv_ln_b': 24.283,
     'q_norm_g': 3.318,
     'conv_out_g': 3.232,
     'attn_out_g': 3.422,
     'ln1_b': 4.737,
     'b_rg': 35.871,
     'b_re': 37.419,
     'ln2_b': 5.614,
     'ln_in_b': 2.774}
    for name, (base, spread) in spreads.items():
        noise = np.random.default_rng([zlib.crc32(name.encode()), seed]).standard_normal(out[name].shape)
        drawn = base * np.exp(spread * noise) if base else spread * noise
        out[name] = __import__('jax').numpy.asarray(drawn.astype(out[name].dtype))
    for name, factor in factors.items():
        out[name] = (out[name] * factor).astype(out[name].dtype)
    return out
```

```python
import concourse.bass as bass
from concourse import mybir
from contextlib import ExitStack
import numpy as np

F32 = mybir.dt.float32
I32 = mybir.dt.int32
ALU = mybir.AluOpType
ACT = mybir.ActivationFunctionType
AX = mybir.AxisListType

P = 128
D = 1024
T = 1024
NT = T // P
META = 16
KD = D // P
C = 512
NC4 = C // P
TAPS = 31
CHUNK = 64
H = 8
NOPE, ROPE, VD = 64, 32, 64
QK = NOPE + ROPE
QL, KVL = 384, 256
ZR = QL + KVL + ROPE
G, EG, E = 4, 8, 32
F = 256
MAXB = E + 2 * T // P - 1
ALPHA = float(np.float32(2.0 ** 0.25))
EPS = 1e-5
PAD = TAPS - 1 - META
UW = PAD + META + T
WGU, WDN = KD * 2 * F, (F // P) * D
WE = WGU + WDN
RING = 4

K_ID = 0
K_TRI = K_ID + P
K_ONE = K_TRI + P
K_COS = K_ONE + P
K_SIN = K_COS + (NT + 1) * ROPE
K_IOTA = K_SIN + (NT + 1) * ROPE
K_MASK = K_IOTA + P
K_NEG = K_MASK + P
K_TOK = K_NEG + CHUNK
K_DESC = K_TOK + NT
K_MH = K_DESC + EG
K_EPS = K_MH + NT
K_END = K_EPS + 1


def constants():
    t = np.zeros((P, K_END), np.float32)
    t[:, K_ID:K_ID + P] = np.eye(P)
    t[:, K_TRI:K_TRI + P] = np.triu(np.ones((P, P)), 1)
    t[:, K_ONE:K_ONE + P] = 1.0
    half = ROPE // 2
    freq = (np.float32(10000.0) ** (-np.arange(half, dtype=np.float32) / np.float32(half))).astype(np.float32)
    ang = np.arange(META + T, dtype=np.float32)[:, None] * freq[None, :]
    for name, f in ((K_COS, np.cos), (K_SIN, np.sin)):
        v = f(ang).astype(np.float32)
        v = np.concatenate([v, v], 1)
        t[:META, name:name + ROPE] = v[:META]
        t[:, name + ROPE:name + (NT + 1) * ROPE] = v[META:].reshape(NT, P, ROPE).transpose(1, 0, 2).reshape(P, -1)
    t[:, K_IOTA:K_IOTA + P] = np.arange(P)
    t[0, K_MASK:K_MASK + P] = np.arange(P) < CHUNK
    t[0, K_NEG:K_NEG + CHUNK] = -1e30
    t[:, K_TOK:K_TOK + NT] = np.arange(T).reshape(NT, P).T
    t[:, K_DESC:K_DESC + EG] = np.arange(EG, 0, -1)
    t[:, K_MH:K_MH + NT] = -0.5
    t[:, K_EPS] = EPS
    return t


class Chain:

    def __init__(self, engine, semaphore):
        self.engine, self.semaphore, self.count = engine, semaphore, 0

    def __call__(self, instruction):
        self.count += 1
        instruction.then_inc(self.semaphore, 1)
        self.engine.wait_ge(self.semaphore, self.count)


def inverse_root(pool, chain, const, out, var, scale):
    r, n = out.shape
    chain(pool.tensor_scalar(out, var, scale, EPS, ALU.mult, ALU.add))
    return pool.tensor_tensor(out, out, const[:r, K_MH:K_MH + n], ALU.pow)


def rows(t):
    return META if t == 0 else P


def col(t):
    return 0 if t == 0 else META + P * (t - 1)


def input_block(nc, a, ps, const, hT, u, h_dram, y_dram):
    ctx = ExitStack()
    with ctx:
        sb = lambda n, s, d=F32: ctx.enter_context(nc.sbuf_tensor(n, s, d))
        sem = lambda n: ctx.enter_context(nc.semaphore(n))
        x_t = sb("x_t", [P, 2, D])
        h_t = sb("h_t", [P, 2, D])
        g_in = sb("g_in", [P, D])
        b_in = sb("b_in", [P, D])
        w_c = sb("w_c", [P, NC4, KD * 2 * P])
        sg = sb("sg", [P, 2, 512])
        stats = sb("stats", [P, 2, 12])
        mv = sb("mv", [P, 2, 2])
        rstd = sb("rstd", [P, 2, 1])
        zeros = sb("zeros", [P, D])
        ident = const[:, K_ID:K_ID + P]

        consts_in, w_in = sem("a_consts_in"), [sem(f"a_w_in{c}") for c in range(NC4)]
        x_in = [sem("a_x_in0"), sem("a_x_in1")]
        stats_done, rstd_done, normed, scaled, h_done = (sem("a_" + n) for n in ("stats", "rstd", "normed", "scaled", "h"))
        h_out = [sem("a_h_out0"), sem("a_h_out1")]
        transposed, hT_act, hT_dve = (sem("a_" + n) for n in ("transposed", "hT_act", "hT_dve"))
        gate_done, sig_done, u_done, link = (sem("a_" + n) for n in ("gate", "sig", "u", "link"))
        zeroed, plink, zeros_out = sem("a_zeroed"), sem("a_plink"), sem("a_zeros_out")
        block = ctx.enter_context(nc.Block())
        units = [(0, 0)] + [(n, c) for n in range(2) for c in range(NC4)]

        @block.sync
        def _(sp):
            sp.dma_start(const[:, :], a["consts"]).then_inc(consts_in, 16)
            for t in range(NT + 1):
                if t >= 2:
                    sp.wait_ge(normed, t - 1)
                src = a["meta_tokens"] if t == 0 else a["x"][0, P * (t - 1):P * t, :]
                sp.dma_start(x_t[:rows(t), t % 2, :], src).then_inc(x_in[t % 2], 16)
                if t == 0:
                    sp.dma_start(g_in[:, :], a["ln_in_g"].rearrange("(a n) -> a n", a=1).broadcast_to([P, D])).then_inc(consts_in, 16)
                    sp.dma_start(b_in[:, :], a["ln_in_b"].rearrange("(a n) -> a n", a=1).broadcast_to([P, D])).then_inc(consts_in, 16)
                if t >= 2:
                    sp.wait_ge(h_done, t - 1)
                    if t >= 3:
                        sp.dma_start(h_dram[P * (t - 3):P * (t - 2), :], h_t[:, t % 2, :]).then_inc(h_out[t % 2], 16)
            for t in (NT - 1, NT):
                sp.wait_ge(h_done, t + 1)
                sp.dma_start(h_dram[P * (t - 1):P * t, :], h_t[:, t % 2, :]).then_inc(h_out[t % 2], 16)
            sp.wait_ge(h_out[0], 16 * (NT // 2))
            sp.wait_ge(h_out[1], 16 * (NT // 2))

        @block.gpsimd
        def _(pool):
            chain = Chain(pool, plink)
            pool.memset(u[:, :, 0:PAD], 0.0).then_inc(zeroed, 1)
            pool.memset(zeros[:, :], 0.0).then_inc(zeroed, 1)
            pool.wait_ge(consts_in, 48)
            for t in range(NT + 1):
                r = rows(t)
                pool.wait_ge(stats_done, t + 1)
                inverse_root(pool, chain, const, rstd[:r, t % 2, :], mv[:r, t % 2, 1:2], 1.0).then_inc(rstd_done, 1)
                pool.wait_ge(scaled, t + 1)
                pool.tensor_tensor(h_t[:r, t % 2, :], h_t[:r, t % 2, :], b_in[:r, :], ALU.add).then_inc(h_done, 1)

        def take(eng, ns, t, half, done):
            r = rows(t)
            eng.wait_ge(transposed, t + 1)
            src = ps[:, half, :].rearrange("p (k t) -> p k t", t=P)[:, :, 0:r]
            dst = hT[:, 4 * half:4 * half + 4, col(t):col(t) + r]
            if half:
                ns.tensor_copy(dst, src).then_inc(done, 1)
            else:
                ns.activation(dst, src, ACT.Copy).then_inc(done, 1)

        @block.vector
        def _(dve):
            chain = Chain(dve, link)

            def gated(j):
                n, c = units[j]
                dve.wait_ge(sig_done, j + 1)
                if j == 0:
                    nc.vector.tensor_tensor(u[:, :, PAD:PAD + META], ps[:, 2, 0:64].rearrange("p (c t) -> p c t", t=META),
                                            sg[:, 0, 0:64].rearrange("p (c t) -> p c t", t=META), ALU.mult).then_inc(u_done, 1)
                else:
                    at = PAD + META + 512 * n
                    nc.vector.tensor_tensor(u[:, c, at:at + 512], ps[:, 2 + 2 * (j % 2), :], sg[:, j % 2, :],
                                            ALU.mult).then_inc(u_done, 1)

            for t in range(NT + 1):
                r = rows(t)
                dve.wait_ge(x_in[t % 2], 16 * (t // 2 + 1))
                chain(nc.vector.bn_stats(stats[:r, t % 2, 0:6], x_t[:r, t % 2, 0:512]))
                chain(nc.vector.bn_stats(stats[:r, t % 2, 6:12], x_t[:r, t % 2, 512:1024]))
                nc.vector.bn_aggr(mv[:r, t % 2, :], stats[:r, t % 2, :]).then_inc(stats_done, 1)
                dve.wait_ge(rstd_done, t + 1)
                dve.wait_ge(stats_done, t + 1)
                if t >= 3:
                    dve.wait_ge(h_out[t % 2], 16 * ((t - 1) // 2))
                if t >= 2:
                    dve.wait_ge(transposed, t - 1)
                nc.vector.tensor_scalar(h_t[:r, t % 2, :], x_t[:r, t % 2, :], mv[:r, t % 2, 0:1], rstd[:r, t % 2, :],
                                        ALU.subtract, ALU.mult).then_inc(normed, 1)
                if t == 0:
                    dve.wait_ge(consts_in, 48)
                dve.wait_ge(normed, t + 1)
                nc.vector.tensor_tensor(h_t[:r, t % 2, :], h_t[:r, t % 2, :], g_in[:r, :], ALU.mult).then_inc(scaled, 1)
                if t >= 1:
                    take(dve, nc.vector, t - 1, 1, hT_dve)
            take(dve, nc.vector, NT, 1, hT_dve)
            for j in range(len(units)):
                gated(j)

        @block.scalar
        def _(act):
            for c in range(NC4):
                act.dma_start(w_c[:, c, :], a["w_conv_in"][:, c, :]).then_inc(w_in[c], 16)
            act.wait_ge(zeroed, 2)
            act.dma_start(y_dram[E * P:MAXB * P, :].rearrange("(b p) d -> p b d", p=P),
                          zeros[:, :].unsqueeze(1).broadcast_to([P, MAXB - E, D])).then_inc(zeros_out, 16)
            for t in range(NT + 1):
                take(act, nc.scalar, t, 0, hT_act)
            for j in range(len(units)):
                act.wait_ge(gate_done, j + 1)
                if j >= 2:
                    act.wait_ge(u_done, j - 1)
                src, dst = (ps[:, 3, 0:64], sg[:, 0, 0:64]) if j == 0 else (ps[:, 3 + 2 * (j % 2), :], sg[:, j % 2, :])
                nc.scalar.activation(dst, src, ACT.Sigmoid).then_inc(sig_done, 1)
            act.wait_ge(zeros_out, 16)

        @block.tensor
        def _(pe):
            pe.wait_ge(consts_in, 48)
            for t in range(NT + 1):
                r = rows(t)
                pe.wait_ge(h_done, t + 1)
                if t >= 1:
                    pe.wait_ge(hT_act, t)
                    pe.wait_ge(hT_dve, t)
                for k in range(KD):
                    last = nc.tensor.transpose(ps[:, k // 4, (k % 4) * P:(k % 4) * P + r], h_t[:r, t % 2, k * P:(k + 1) * P],
                                               ident[:r, :r])
                last.then_inc(transposed, 1)
            pe.wait_ge(hT_act, NT + 1)
            pe.wait_ge(hT_dve, NT + 1)
            for j, (n, c) in enumerate(units):
                if j >= 2:
                    pe.wait_ge(u_done, j - 1)
                    pe.wait_ge(sig_done, j - 1)
                if j == 0:
                    for c0 in range(NC4):
                        pe.wait_ge(w_in[c0], 16)
                        for part in range(2):
                            for k in range(KD):
                                w = w_c[:, c0, k * 2 * P + part * P:k * 2 * P + (part + 1) * P]
                                last = nc.tensor.matmul(ps[:, 2 + part, c0 * META:(c0 + 1) * META], w, hT[:, k, 0:META],
                                                        start=(k == 0), stop=(k == KD - 1))
                else:
                    at = META + 512 * n
                    for part in range(2):
                        for k in range(KD):
                            w = w_c[:, c, k * 2 * P + part * P:k * 2 * P + (part + 1) * P]
                            last = nc.tensor.matmul(ps[:, 2 + 2 * (j % 2) + part, :], w, hT[:, k, at:at + 512],
                                                    start=(k == 0), stop=(k == KD - 1))
                last.then_inc(gate_done, 1)


def tap(nc, chain, u, acc, cw, c, k):
    if k == 0:
        chain(nc.vector.tensor_scalar(acc[:, c, :], u[:, c, 0:T], cw[:, c, 0:1], cw[:, c, TAPS:TAPS + 1], ALU.mult, ALU.add))
    else:
        chain(nc.vector.scalar_tensor_tensor(acc[:, c, :], u[:, c, k:k + T], cw[:, c, k:k + 1], acc[:, c, :], ALU.mult, ALU.add))


def mixer_block(nc, a, ps, const, hT, u, acc, cw, qT, kT, v_all, v_meta, z, zT, q_t, k_t):
    ctx = ExitStack()
    with ctx:
        sb = lambda n, s, d=F32: ctx.enter_context(nc.sbuf_tensor(n, s, d))
        sem = lambda n: ctx.enter_context(nc.semaphore(n))
        w_z = sb("w_z", [P, KD, ZR])
        w_q = sb("w_q", [P, 3, H * QK])
        w_kv = acc[:, 2:4, :]
        qg = sb("qg", [P, 5])
        ssq = sb("ssq", [P, 2, 2])
        rr = sb("rr", [P, 2, 2])
        ra = sb("ra", [P, H, ROPE])
        rb = sb("rb", [P, H, ROPE])
        ka = sb("ka", [P, ROPE])
        kb = sb("kb", [P, ROPE])
        ident = const[:, K_ID:K_ID + P]

        w_ready, wz_ready, vm_in = sem("b_w"), sem("b_wz"), sem("b_vm")
        folded, z_mm, z_sq, z_copied, z_cp2, r_done = (sem("b_" + n) for n in ("folded", "z", "z_sq", "z_cp", "z_cp2", "r"))
        zT_mm, zT_a, zT_d = (sem("b_" + n) for n in ("zT_mm", "zT_a", "zT_d"))
        q_mm, kv_mm, q_ev, k_ev, v_ev, roped = (sem("b_" + n) for n in ("q_mm", "kv_mm", "q_ev", "k_ev", "v_ev", "roped"))
        tq_mm, tk_mm, tq_ev, tk_ev, pl, vl = (sem("b_" + n) for n in ("tq_mm", "tk_mm", "tq_ev", "tk_ev", "pl", "vl"))
        block = ctx.enter_context(nc.Block())
        NS = NT + 1

        @block.sync
        def _(sp):
            sp.dma_start(w_z[:, :, :], a["w_z"]).then_inc(wz_ready, 16)
            sp.dma_start(w_q[:, :, :], a["w_q"]).then_inc(w_ready, 16)
            sp.dma_start(w_kv[:, :, :], a["w_kv"]).then_inc(w_ready, 16)
            sp.dma_start(qg[:, :], a["qkv_g"]).then_inc(w_ready, 16)
            sp.dma_start(cw[:, :, :], a["conv_wb"]).then_inc(w_ready, 16)
            for h in range(H):
                if h == 0:
                    sp.wait_ge(v_ev, 1)
                    sp.wait_ge(folded, 6)
                sp.dma_start(v_meta[META * h:META * (h + 1), VD * h:VD * (h + 1)],
                             v_all[:META, 0, VD * h:VD * (h + 1)]).then_inc(vm_in, 16)
            sp.wait_ge(vm_in, 16 * H)

        @block.gpsimd
        def _(pool):
            pool.wait_ge(w_ready, 64)
            for k in range(3):
                pool.tensor_scalar(w_q[:, k, :], w_q[:, k, :], qg[:, k:k + 1], None, ALU.mult).then_inc(folded, 1)
            for k in range(2):
                pool.tensor_scalar(w_kv[:, k, :], w_kv[:, k, :], qg[:, 3 + k:4 + k], None, ALU.mult).then_inc(folded, 1)
            pool.memset(v_meta[:, :], 0.0).then_inc(folded, 1)
            chain = Chain(pool, pl)
            for t in range(NS):
                r = rows(t)
                c2 = const[:r, K_COS + ROPE * t:K_COS + ROPE * (t + 1)]
                s2 = const[:r, K_SIN + ROPE * t:K_SIN + ROPE * (t + 1)]
                half = ROPE // 2
                pool.wait_ge(z_sq, t + 1)
                for part, width in ((0, QL), (1, KVL)):
                    if part or t:
                        ins = inverse_root(pool, chain, const, rr[:r, t % 2, part:part + 1], ssq[:r, t % 2, part:part + 1], 1.0 / width)
                ins.then_inc(r_done, 1)
                pool.wait_ge(z_cp2, t + 1)
                kr = z[:r, QL + KVL:ZR]
                pool.tensor_tensor(ka[:r, :], kr, c2, ALU.mult)
                chain(pool.tensor_tensor(kb[:r, :], kr, s2, ALU.mult))
                if t >= 1:
                    pool.wait_ge(tk_mm, t)
                one = lambda x, lo: x[:r, lo:lo + half].unsqueeze(1).broadcast_to([r, H, half])
                pool.tensor_tensor(k_t[:r, :, NOPE:NOPE + half], one(ka, 0), one(kb, half), ALU.subtract)
                pool.tensor_tensor(k_t[:r, :, NOPE + half:QK], one(kb, 0), one(ka, half), ALU.add).then_inc(roped, 1)
                if t >= 1:
                    pool.wait_ge(q_ev, 2 * t)
                    qr = q_t[:r, :, NOPE:QK]
                    many = lambda x: x.unsqueeze(1).broadcast_to([r, H, ROPE])
                    pool.tensor_tensor(ra[:r, :, :], qr, many(c2), ALU.mult)
                    chain(pool.tensor_tensor(rb[:r, :, :], qr, many(s2), ALU.mult))
                    pool.tensor_tensor(q_t[:r, :, NOPE:NOPE + half], ra[:r, :, 0:half], rb[:r, :, half:ROPE], ALU.subtract)
                    pool.tensor_tensor(q_t[:r, :, NOPE + half:QK], rb[:r, :, 0:half], ra[:r, :, half:ROPE], ALU.add).then_inc(roped, 1)

        @block.scalar
        def _(act):
            for t in range(NS + 1):
                if t < NS:
                    r = rows(t)
                    act.wait_ge(z_mm, t + 1)
                    if t:
                        act.wait_ge(zT_mm, t)
                        act.wait_ge(roped, 1 if t == 1 else 2 * t - 2)
                        nc.scalar.activation(z[:r, 0:QL], ps[:r, 0, 0:QL], ACT.Copy).then_inc(z_copied, 1)
                        act.wait_ge(z_copied, t)
                        nc.scalar.activation(ps[:r, 0, 0:QL], ps[:r, 0, 0:QL], ACT.Square, accum_out=ssq[:r, t % 2, 0:1])
                    nc.scalar.activation(z[:r, QL:ZR], ps[:r, 1, 0:KVL + ROPE], ACT.Copy).then_inc(z_cp2, 1)
                    act.wait_ge(z_cp2, t + 1)
                    nc.scalar.activation(ps[:r, 1, 0:KVL], ps[:r, 1, 0:KVL], ACT.Square, accum_out=ssq[:r, t % 2, 1:2]).then_inc(z_sq, 1)
                if t >= 1:
                    e = t - 1
                    r = rows(e)
                    act.wait_ge(r_done, e + 1)
                    if e:
                        act.wait_ge(q_mm, e)
                        if e >= 2:
                            act.wait_ge(tq_mm, e - 1)
                        for b in range(2):
                            nc.scalar.activation(q_t[:r, 4 * b:4 * b + 4, :].rearrange("p h d -> p (h d)"), ps[:r, 4 + b, 0:4 * QK],
                                                 ACT.Copy, scale=rr[:r, e % 2, 0:1]).then_inc(q_ev, 1)
                    act.wait_ge(kv_mm, e + 1)
                    if e:
                        act.wait_ge(tk_mm, e)
                    nc.scalar.activation(k_t[:r, :, 0:NOPE], ps[:r, 6, :].rearrange("p (h d) -> p h d", d=NOPE), ACT.Copy,
                                         scale=rr[:r, e % 2, 1:2]).then_inc(k_ev, 1)
                    nc.scalar.activation(v_all[:r, e, :], ps[:r, 7, :], ACT.Copy, scale=rr[:r, e % 2, 1:2]).then_inc(v_ev, 1)

        taps = [(c, k) for c in range(2) for k in range(TAPS)]

        @block.vector
        def _(dve):
            done = 0
            dve.wait_ge(w_ready, 64)
            dve.wait_ge(wz_ready, 16)
            chain = Chain(dve, vl)
            for t in range(NS + 1):
                if t < NS:
                    r = rows(t)
                    dve.wait_ge(zT_mm, t + 1)
                    if t >= 1:
                        dve.wait_ge(kv_mm, t)
                    if t:
                        nc.vector.tensor_copy(zT[:, 0:3, 0:r], ps[:, 2, 0:3 * P].rearrange("p (k t) -> p k t", t=P)[:, :, 0:r]).then_inc(zT_d, 1)
                    nc.vector.tensor_copy(zT[:, 3:5, 0:r], ps[:, 3, 0:2 * P].rearrange("p (k t) -> p k t", t=P)[:, :, 0:r]).then_inc(zT_a, 1)
                if t >= 1 and t <= NS:
                    e = t - 1
                    r = rows(e)
                    if e:
                        dve.wait_ge(tq_mm, e)
                        for b in range(2):
                            nc.vector.tensor_copy(qT[:, 4 * b:4 * b + 4, P * (e - 1):P * e],
                                                  ps[:QK, 2 + b, :].rearrange("p (h t) -> p h t", t=P)).then_inc(tq_ev, 1)
                    dve.wait_ge(tk_mm, e + 1)
                    for b in range(2):
                        nc.vector.tensor_copy(kT[:, 4 * b:4 * b + 4, col(e):col(e) + r],
                                              ps[:QK, 6 + b, :].rearrange("p (h t) -> p h t", t=P)[:, :, 0:r]).then_inc(tk_ev, 1)
                upto = len(taps) * (t + 1) // (NS + 1)
                while done < upto:
                    tap(nc, chain, u, acc, cw, *taps[done])
                    done += 1

        @block.tensor
        def _(pe):
            pe.wait_ge(wz_ready, 16)
            for s in range(NS + 1):
                if s < NS:
                    r, at = rows(s), col(s)
                    if s:
                        pe.wait_ge(z_sq, s)
                        for k in range(KD):
                            nc.tensor.matmul(ps[:r, 0, 0:QL], hT[:, k, at:at + r], w_z[:, k, 0:QL], start=(k == 0), stop=(k == KD - 1))
                    for k in range(KD):
                        last = nc.tensor.matmul(ps[:r, 1, 0:KVL + ROPE], hT[:, k, at:at + r], w_z[:, k, QL:ZR],
                                                start=(k == 0), stop=(k == KD - 1))
                    last.then_inc(z_mm, 1)
                if s >= 1:
                    e = s - 1
                    r = rows(e)
                    if e == 0:
                        pe.wait_ge(folded, 5)
                    if e:
                        pe.wait_ge(zT_d, e)
                        if e >= 2:
                            pe.wait_ge(q_ev, 2 * (e - 1))
                        for b in range(2):
                            for k in range(3):
                                last = nc.tensor.matmul(ps[:r, 4 + b, 0:4 * QK], zT[:, k, 0:r], w_q[:, k, 4 * QK * b:4 * QK * (b + 1)],
                                                        start=(k == 0), stop=(k == 2))
                        last.then_inc(q_mm, 1)
                    pe.wait_ge(zT_a, e + 1)
                    if e:
                        pe.wait_ge(tk_ev, 2 * e)
                    for b in range(2):
                        for k in range(2):
                            last = nc.tensor.matmul(ps[:r, 6 + b, :], zT[:, 3 + k, 0:r], w_kv[:, k, 512 * b:512 * (b + 1)],
                                                    start=(k == 0), stop=(k == 1))
                    last.then_inc(kv_mm, 1)
                if s < NS:
                    r = rows(s)
                    if s >= 3:
                        pe.wait_ge(tq_ev, 2 * (s - 2))
                    if s:
                        pe.wait_ge(z_copied, s)
                        for k in range(3):
                            nc.tensor.transpose(ps[:, 2, k * P:k * P + r], z[:r, k * P:(k + 1) * P], ident[:r, :r])
                    pe.wait_ge(z_cp2, s + 1)
                    for k in range(2):
                        last = nc.tensor.transpose(ps[:, 3, k * P:k * P + r], z[:r, QL + k * P:QL + (k + 1) * P], ident[:r, :r])
                    last.then_inc(zT_mm, 1)
                if s >= 1:
                    e = s - 1
                    r = rows(e)
                    pe.wait_ge(roped, 1 if e == 0 else 2 * e + 1)
                    if s < NS:
                        pe.wait_ge(zT_a, s + 1)
                        pe.wait_ge(zT_d, s)
                    if e:
                        pe.wait_ge(q_ev, 2 * e)
                        for h in range(H):
                            last = nc.tensor.transpose(ps[:QK, 2 + h // 4, (h % 4) * P:(h % 4 + 1) * P], q_t[:r, h, :], ident[:r, :r])
                        last.then_inc(tq_mm, 1)
                    pe.wait_ge(k_ev, e + 1)
                    pe.wait_ge(v_ev, e + 1)
                    for h in range(H):
                        last = nc.tensor.transpose(ps[:QK, 6 + h // 4, (h % 4) * P:(h % 4) * P + r], k_t[:r, h, :], ident[:r, :r])
                    last.then_inc(tk_mm, 1)


def attention_block(nc, ps, const, u, acc, cw, qT, kT, v_all, v_meta, o_all, p, pT):
    ctx = ExitStack()
    with ctx:
        sb = lambda n, s, d=F32: ctx.enter_context(nc.sbuf_tensor(n, s, d))
        sem = lambda n: ctx.enter_context(nc.semaphore(n))
        m_s = sb("m_s", [P, H, META])
        m_p = sb("m_p", [P, H, META])
        m_pT = sb("m_pT", [P, P])
        m_max = sb("m_max", [P, H])
        r_max = sb("r_max", [P, 2])
        bias = sb("bias", [P, H])
        sums = sb("sums", [P, 2, H])
        m_sums = sb("m_sums", [P, H])
        inv = sb("inv", [P, H])
        scale = float(np.float32(QK ** -0.5))
        ident = const[:, K_ID:K_ID + P]
        units = [(i, h) for i in range(NT) for h in range(H)]
        NU = len(units)

        (m_mm, m_copied, m_maxed, s_mm, biased, exp_done, t_mm, ev_act, ev_dve, pv_mm, m_arg, m_exp, m_t, m_tc, o_mm,
         o_done, link) = (sem("c_" + n) for n in ("m_mm", "m_copied", "m_maxed", "s_mm", "biased", "exp", "t_mm", "ev_act",
                                                  "ev_dve", "pv_mm", "m_arg", "m_exp", "m_t", "m_tc", "o_mm", "o_done", "link"))
        block = ctx.enter_context(nc.Block())

        def dve_evacs(n):
            return sum(i >= 4 for i, _ in units[:n])

        @block.tensor
        def _(pe):
            def scores(n):
                i, h = units[n]
                if n >= 2:
                    pe.wait_ge(exp_done, n - 1)
                keys = P * (i + 1)
                for lo in range(0, keys, 512):
                    hi = min(lo + 512, keys)
                    bank = 2 * (n % 2) + lo // 512
                    last = nc.tensor.matmul(ps[:, bank, 0:hi - lo], qT[:, h, P * i:P * (i + 1)], kT[:, h, META + lo:META + hi],
                                            start=True, stop=(hi < keys))
                    if hi == keys:
                        last = nc.tensor.matmul(ps[:, bank, hi - lo - CHUNK:hi - lo], const[0:1, K_MASK:K_MASK + P],
                                                const[0:1, K_NEG:K_NEG + CHUNK], start=False, stop=True)
                last.then_inc(s_mm, 1)

            def meta_scores(i):
                if i >= 2:
                    pe.wait_ge(m_tc, i - 1)
                for h in range(H):
                    last = nc.tensor.matmul(ps[:, 7, META * h:META * (h + 1)], qT[:, h, P * i:P * (i + 1)], kT[:, h, 0:META],
                                            start=True, stop=True)
                last.then_inc(m_mm, 1)

            def transposes(n):
                i, h = units[n]
                pe.wait_ge(exp_done, n + 1)
                if n >= 1:
                    pe.wait_ge(ev_act, n)
                    if dve_evacs(n):
                        pe.wait_ge(ev_dve, dve_evacs(n))
                for k in range(i + 1):
                    last = nc.tensor.transpose(ps[:, 4 + k // 4, (k % 4) * P:(k % 4 + 1) * P], p[:, n % 2, k * P:(k + 1) * P], ident)
                last.then_inc(t_mm, 1)

            def values(n):
                i, h = units[n]
                pe.wait_ge(ev_act, n + 1)
                if i >= 4:
                    pe.wait_ge(ev_dve, dve_evacs(n + 1))
                if h == 0 and i >= 1:
                    pe.wait_ge(o_done, i)
                for k in range(i + 1):
                    last = nc.tensor.matmul(ps[:, 6, VD * h:VD * (h + 1)], pT[:, n % 2, k, :], v_all[:, k + 1, VD * h:VD * (h + 1)],
                                            start=(h == 0 and k == 0), stop=False, skip_group_check=True)
                last.then_inc(pv_mm, 1)
                if h == H - 1:
                    pe.wait_ge(m_exp, i + 1)
                    pe.wait_ge(m_copied, min(i + 2, NT))
                    nc.tensor.transpose(ps[:, 7, 0:P], m_p[:, :, :].rearrange("p h k -> p (h k)"), ident).then_inc(m_t, 1)
                    pe.wait_ge(m_tc, i + 1)
                    nc.tensor.matmul(ps[:, 6, :], m_pT[:, :], v_meta[:, :], start=False, stop=True,
                                     skip_group_check=True).then_inc(o_mm, 1)

            meta_scores(0)
            scores(0)
            for n, (i, h) in enumerate(units):
                if h == H - 1 and i + 1 < NT:
                    meta_scores(i + 1)
                if n + 1 < NU:
                    scores(n + 1)
                transposes(n)
                if n >= 1:
                    values(n - 1)
            values(NU - 1)

        @block.scalar
        def _(act):
            for n, (i, h) in enumerate(units):
                if h == 0:
                    act.wait_ge(m_mm, i + 1)
                    if i >= 1:
                        act.wait_ge(m_arg, i)
                    nc.scalar.activation(m_s[:, :, :], ps[:, 7, 0:P].rearrange("p (h k) -> p h k", k=META), ACT.Copy).then_inc(m_copied, 1)
                    if i >= 2:
                        act.wait_ge(o_done, i - 1)
                act.wait_ge(biased, n + 1)
                if n >= 2:
                    act.wait_ge(t_mm, n - 1)
                keys = P * (i + 1)
                src = ps[:, 2 * (n % 2):2 * (n % 2) + 2, :].rearrange("p b n -> p (b n)")[:, 0:keys]
                nc.scalar.activation(p[:, n % 2, 0:keys], src, ACT.Exp, bias=bias[:, h:h + 1], scale=scale,
                                     accum_out=sums[:, i % 2, h:h + 1]).then_inc(exp_done, 1)
                if h == H - 1:
                    act.wait_ge(m_arg, i + 1)
                    nc.scalar.activation(m_p[:, :, :], m_p[:, :, :], ACT.Exp).then_inc(m_exp, 1)
                act.wait_ge(t_mm, n + 1)
                if n >= 2:
                    act.wait_ge(pv_mm, n - 1)
                m = min(4, i + 1)
                nc.scalar.activation(pT[:, n % 2, 0:m, :].rearrange("p k t -> p (k t)"), ps[:, 4, 0:m * P], ACT.Copy).then_inc(ev_act, 1)
                if h == 0 and i >= 1:
                    act.wait_ge(m_t, i)
                    nc.scalar.activation(m_pT[:, :], ps[:, 7, 0:P], ACT.Copy).then_inc(m_tc, 1)
            act.wait_ge(m_t, NT)
            nc.scalar.activation(m_pT[:, :], ps[:, 7, 0:P], ACT.Copy).then_inc(m_tc, 1)

        taps = [(c, k) for c in (2, 3) for k in range(TAPS)]

        @block.vector
        def _(dve):
            chain = Chain(dve, link)

            def finish(i):
                dve.wait_ge(m_exp, i + 1)
                chain(nc.vector.reduce_sum(m_sums[:, :], m_p[:, :, :], AX.X))
                dve.wait_ge(exp_done, H * (i + 1))
                chain(nc.vector.tensor_tensor(m_sums[:, :], m_sums[:, :], sums[:, i % 2, :], ALU.add))
                chain(nc.vector.reciprocal(inv[:, :], m_sums[:, :]))
                dve.wait_ge(o_mm, i + 1)
                nc.vector.tensor_tensor(o_all[:, i, :].rearrange("p (h d) -> p h d", d=VD),
                                        ps[:, 6, :].rearrange("p (h d) -> p h d", d=VD),
                                        inv[:, :].unsqueeze(2).broadcast_to([P, H, VD]), ALU.mult).then_inc(o_done, 1)

            def evacuate(n):
                i, h = units[n]
                if i >= 4:
                    dve.wait_ge(t_mm, n + 1)
                    if n >= 2:
                        dve.wait_ge(pv_mm, n - 1)
                    nc.vector.tensor_copy(pT[:, n % 2, 4:i + 1, :].rearrange("p k t -> p (k t)"), ps[:, 5, 0:(i - 3) * P]).then_inc(ev_dve, 1)

            done = 0
            for n, (i, h) in enumerate(units):
                if h == 0:
                    dve.wait_ge(m_copied, i + 1)
                    nc.vector.reduce_max(m_max[:, :], m_s[:, :, :], AX.X).then_inc(m_maxed, 1)
                dve.wait_ge(s_mm, n + 1)
                keys = P * (i + 1)
                src = ps[:, 2 * (n % 2):2 * (n % 2) + 2, :].rearrange("p b n -> p (b n)")[:, 0:keys]
                chain(nc.vector.reduce_max(r_max[:, n % 2:n % 2 + 1], src, AX.X))
                if h == 0:
                    dve.wait_ge(m_maxed, i + 1)
                    if i >= 1:
                        dve.wait_ge(exp_done, n)
                nc.vector.tensor_scalar(bias[:, h:h + 1], r_max[:, n % 2:n % 2 + 1], m_max[:, h:h + 1], -scale,
                                        ALU.max, ALU.mult).then_inc(biased, 1)
                if h == H - 1:
                    dve.wait_ge(biased, n + 1)
                    nc.vector.scalar_tensor_tensor(m_p[:, :, :], m_s[:, :, :], scale, bias[:, :].unsqueeze(2).broadcast_to([P, H, META]),
                                                   ALU.mult, ALU.add).then_inc(m_arg, 1)
                if n >= 1:
                    evacuate(n - 1)
                if h == 2 and i >= 1:
                    finish(i - 1)
                upto = len(taps) * (n + 1) // NU
                while done < upto:
                    tap(nc, chain, u, acc, cw, *taps[done])
                    done += 1
            evacuate(NU - 1)
            finish(NT - 1)


def merge_block(nc, a, ps, const, acc, o_all, h_dram, h1, h1_dram, logits):
    ctx = ExitStack()
    with ctx:
        sb = lambda n, s, d=F32: ctx.enter_context(nc.sbuf_tensor(n, s, d))
        sem = lambda n: ctx.enter_context(nc.semaphore(n))
        w_o = sb("wo", [P, KD, D])
        g_o = sb("g_o", [P, KD])
        cg = sb("cg", [P, 2, NC4])
        w_r = sb("w_r", [P, KD, G + E])
        g1 = sb("g1", [P, D])
        b1 = sb("b1", [P, D])
        sq = sb("sq", [P, NC4, 512])
        rs = sb("rs", [P, 2, 512])
        rc = sb("rc", [P, NT])
        ra = sb("ra_o", [P, NT])
        res = sb("res", [P, D])
        y_t = sb("y_t", [P, D])
        oT = sb("oT", [P, NC4, P])
        hT1 = sb("hT1", [P, KD, P])
        stats = sb("stats1", [P, 12])
        mv = sb("mv1", [P, 2])
        rstd = sb("rstd1", [P, 1])
        ident, ones = const[:, K_ID:K_ID + P], const[:, K_ONE:K_ONE + P]

        w_in, wo_folded = sem("d_w"), sem("d_folded")
        (sum_mm, centred, squared, var_mm, var_ev, rs_done, scaled, silu, c_sq, csum_mm, rc_ev, rc_done, o_sq,
         oT_mm, oT_ev, yc_mm, ya_mm, res_done, y_done, stats_done, rstd_done, normed, gained, h1_done, hT_mm, hT_a, hT_d,
         lg_mm, lg_ev, link) = (sem("d_" + n) for n in
                                ("sum_mm", "centred", "squared", "var_mm", "var_ev", "rs", "scaled", "silu", "c_sq", "csum_mm",
                                 "rc_ev", "rc", "o_sq", "oT_mm", "oT_ev", "yc_mm", "ya_mm", "res", "y", "stats", "rstd",
                                 "normed", "gained", "h1", "hT_mm", "hT_a", "hT_d", "lg_mm", "lg_ev", "link"))
        h_in, h1_out, plink = sem("d_h_in"), sem("d_h1_out"), sem("d_plink")
        block = ctx.enter_context(nc.Block())

        @block.sync
        def _(sp):
            sp.dma_start(cg[:, :, :], a["conv_ln"]).then_inc(w_in, 16)
            sp.dma_start(g_o[:, :], a["out_g"]).then_inc(w_in, 16)
            sp.dma_start(w_o[:, :, :], a["w_o"]).then_inc(w_in, 16)
            sp.dma_start(w_r[:, :, :], a["w_r"]).then_inc(w_in, 16)
            sp.dma_start(g1[:, :], a["ln1_g"].broadcast_to([P, D])).then_inc(w_in, 16)
            sp.dma_start(b1[:, :], a["ln1_b"].broadcast_to([P, D])).then_inc(w_in, 16)
            for t in range(NT):
                if t >= 1:
                    sp.wait_ge(y_done, 2 * t)
                sp.dma_start(res[:, :], h_dram[P * t:P * (t + 1), :]).then_inc(h_in, 16)
                if t >= 1:
                    sp.wait_ge(h1_done, t)
                    if t >= 2:
                        sp.wait_ge(h1_out, 16 * (t - 1))
                    sp.dma_start(h1_dram[P * (t - 1):P * t, :], h1[:, t - 1, :]).then_inc(h1_out, 16)
            sp.wait_ge(h1_done, NT)
            sp.wait_ge(h1_out, 16 * (NT - 1))
            sp.dma_start(h1_dram[P * (NT - 1):P * NT, :], h1[:, NT - 1, :]).then_inc(h1_out, 16)
            sp.wait_ge(h1_out, 16 * NT)

        @block.gpsimd
        def _(pool):
            chain = Chain(pool, plink)
            pool.wait_ge(w_in, 96)
            for k in range(KD):
                pool.tensor_scalar(w_o[:, k, :], w_o[:, k, :], g_o[:, k:k + 1], None, ALU.mult).then_inc(wo_folded, 1)
            pool.wait_ge(rc_ev, 2)
            inverse_root(pool, chain, const, rc[:, :], rc[:, :], 1.0 / C).then_inc(rc_done, 1)
            pool.wait_ge(o_sq, NT)
            inverse_root(pool, chain, const, ra[:, :], ra[:, :], 1.0 / C).then_inc(rc_done, 1)
            for t in range(NT):
                pool.wait_ge(h_in, 16 * (t + 1))
                pool.tensor_scalar(res[:, :], res[:, :], ALPHA, None, ALU.mult).then_inc(res_done, 1)
                pool.wait_ge(stats_done, t + 1)
                inverse_root(pool, chain, const, rstd[:, :], mv[:, 1:2], 1.0).then_inc(rstd_done, 1)
                pool.wait_ge(gained, t + 1)
                pool.tensor_tensor(h1[:, t, :], h1[:, t, :], b1[:, :], ALU.add).then_inc(h1_done, 1)

        @block.vector
        def _(dve):
            chain = Chain(dve, link)
            for n in range(2):
                at = slice(512 * n, 512 * (n + 1))
                dve.wait_ge(sum_mm, n + 1)
                for c in range(NC4):
                    nc.vector.scalar_tensor_tensor(acc[:, c, at], ps[:, n, :], -1.0 / C, acc[:, c, at], ALU.mult, ALU.add).then_inc(centred, 1)
            for n in range(2):
                at = slice(512 * n, 512 * (n + 1))
                dve.wait_ge(var_ev, n + 1)
                nc.vector.reciprocal(rs[:, n, :], rs[:, n, :]).then_inc(rs_done, 1)
                dve.wait_ge(rs_done, n + 1)
                for c in range(NC4):
                    dve.wait_ge(centred, NC4 * n + c + 1)
                    nc.vector.tensor_tensor(acc[:, c, at], acc[:, c, at], rs[:, n, :], ALU.mult).then_inc(scaled, 1)
                dve.wait_ge(csum_mm, n + 1)
                nc.vector.tensor_copy(rc[:, 4 * n:4 * n + 4], ps[:, 4, 4 * n:4 * n + 4]).then_inc(rc_ev, 1)
            for t in range(NT + 1):
                if t < NT:
                    if t == 0:
                        dve.wait_ge(rc_done, 2)
                    dve.wait_ge(yc_mm, t + 1)
                    dve.wait_ge(res_done, t + 1)
                    if t >= 1:
                        dve.wait_ge(normed, t)
                    for b in range(2):
                        nc.vector.scalar_tensor_tensor(y_t[:, 512 * b:512 * (b + 1)], ps[:, b, :], rc[:, t:t + 1],
                                                       res[:, 512 * b:512 * (b + 1)], ALU.mult, ALU.add).then_inc(y_done, 1)
                    dve.wait_ge(ya_mm, t + 1)
                    dve.wait_ge(y_done, 2 * (t + 1))
                    for b in range(2):
                        chain(nc.vector.scalar_tensor_tensor(y_t[:, 512 * b:512 * (b + 1)], ps[:, 2 + b, :], ra[:, t:t + 1],
                                                             y_t[:, 512 * b:512 * (b + 1)], ALU.mult, ALU.add))
                    for b in range(2):
                        chain(nc.vector.bn_stats(stats[:, 6 * b:6 * b + 6], y_t[:, 512 * b:512 * (b + 1)]))
                    nc.vector.bn_aggr(mv[:, :], stats[:, :]).then_inc(stats_done, 1)
                    dve.wait_ge(rstd_done, t + 1)
                    nc.vector.tensor_scalar(h1[:, t, :], y_t[:, :], mv[:, 0:1], rstd[:, :], ALU.subtract, ALU.mult).then_inc(normed, 1)
                    dve.wait_ge(normed, t + 1)
                    nc.vector.tensor_tensor(h1[:, t, :], h1[:, t, :], g1[:, :], ALU.mult).then_inc(gained, 1)
                if t >= 1:
                    dve.wait_ge(hT_mm, t)
                    if t >= 2:
                        dve.wait_ge(lg_mm, t - 1)
                    nc.vector.tensor_copy(hT1[:, 4:8, :].rearrange("p k t -> p (k t)"), ps[:, 6, :]).then_inc(hT_d, 1)
                    dve.wait_ge(lg_mm, t)
                    nc.vector.tensor_copy(logits[:, t - 1, :], ps[:, 7, 0:G + E]).then_inc(lg_ev, 1)

        @block.scalar
        def _(act):
            act.wait_ge(w_in, 96)
            for n in range(2):
                at = slice(512 * n, 512 * (n + 1))
                for c in range(NC4):
                    act.wait_ge(centred, NC4 * n + c + 1)
                    if n:
                        act.wait_ge(var_mm, n)
                    nc.scalar.activation(sq[:, c, :], acc[:, c, at], ACT.Square).then_inc(squared, 1)
                act.wait_ge(var_mm, n + 1)
                nc.scalar.activation(rs[:, n, :], ps[:, 2 + n, :], ACT.Sqrt, scale=1.0 / C,
                                     bias=const[:, K_EPS:K_EPS + 1]).then_inc(var_ev, 1)
            for t in range(NT):
                if t >= NC4:
                    act.wait_ge(o_sq, t - 3)
                nc.scalar.activation(sq[:, t % NC4, :], o_all[:, t, :], ACT.Square, accum_out=ra[:, t:t + 1]).then_inc(o_sq, 1)
            for n in range(2):
                at = slice(512 * n, 512 * (n + 1))
                for c in range(NC4):
                    act.wait_ge(scaled, NC4 * n + c + 1)
                    nc.scalar.activation(acc[:, c, at], acc[:, c, at], ACT.Silu, scale=cg[:, 0, c:c + 1], bias=cg[:, 1, c:c + 1]).then_inc(silu, 1)
                for c in range(NC4):
                    act.wait_ge(silu, NC4 * n + c + 1)
                    if n:
                        act.wait_ge(csum_mm, n)
                    if n == 0 and c == 0:
                        act.wait_ge(o_sq, NT)
                    nc.scalar.activation(sq[:, c, :], acc[:, c, at], ACT.Square).then_inc(c_sq, 1)
            for t in range(NT + 1):
                if t < NT:
                    act.wait_ge(oT_mm, t + 1)
                    if t >= 1:
                        act.wait_ge(ya_mm, t)
                    nc.scalar.activation(oT[:, :, :].rearrange("p k t -> p (k t)"), ps[:, 4, :], ACT.Copy).then_inc(oT_ev, 1)
                if t >= 1:
                    act.wait_ge(hT_mm, t)
                    if t >= 2:
                        act.wait_ge(lg_mm, t - 1)
                    nc.scalar.activation(hT1[:, 0:4, :].rearrange("p k t -> p (k t)"), ps[:, 5, :], ACT.Copy).then_inc(hT_a, 1)

        @block.tensor
        def _(pe):
            pe.wait_ge(w_in, 96)
            for n in range(2):
                at = slice(512 * n, 512 * (n + 1))
                for c in range(NC4):
                    last = nc.tensor.matmul(ps[:, n, :], ones, acc[:, c, at], start=(c == 0), stop=(c == NC4 - 1))
                last.then_inc(sum_mm, 1)
            for n in range(2):
                for c in range(NC4):
                    pe.wait_ge(squared, NC4 * n + c + 1)
                    last = nc.tensor.matmul(ps[:, 2 + n, :], ones, sq[:, c, :], start=(c == 0), stop=(c == NC4 - 1))
                last.then_inc(var_mm, 1)
            for n in range(2):
                pe.wait_ge(c_sq, NC4 * (n + 1))
                for j in range(4):
                    for c in range(NC4):
                        last = nc.tensor.matmul(ps[:, 4, 4 * n + j:4 * n + j + 1], sq[:, c, P * j:P * (j + 1)], ones[:, 0:1],
                                                start=(c == 0), stop=(c == NC4 - 1))
                last.then_inc(csum_mm, 1)
            pe.wait_ge(wo_folded, KD)
            pe.wait_ge(silu, 2 * NC4)
            pe.wait_ge(rc_ev, 2)
            for t in range(NT + 1):
                if t < NT:
                    if t >= 1:
                        pe.wait_ge(oT_ev, t)
                    for k in range(NC4):
                        last = nc.tensor.transpose(ps[:, 4, k * P:(k + 1) * P], o_all[:, t, k * P:(k + 1) * P], ident)
                    last.then_inc(oT_mm, 1)
                    if t == 0:
                        pe.wait_ge(var_ev, 2)
                        pe.wait_ge(centred, 2 * NC4)
                    if t >= 1:
                        pe.wait_ge(y_done, 2 * t)
                    for b in range(2):
                        for k in range(NC4):
                            last = nc.tensor.matmul(ps[:, b, :], acc[:, k, P * t:P * (t + 1)], w_o[:, k, 512 * b:512 * (b + 1)],
                                                    start=(k == 0), stop=(k == NC4 - 1))
                    last.then_inc(yc_mm, 1)
                    pe.wait_ge(oT_ev, t + 1)
                    if t >= 1:
                        pe.wait_ge(stats_done, t)
                    for b in range(2):
                        for k in range(NC4):
                            last = nc.tensor.matmul(ps[:, 2 + b, :], oT[:, k, :], w_o[:, NC4 + k, 512 * b:512 * (b + 1)],
                                                    start=(k == 0), stop=(k == NC4 - 1))
                    last.then_inc(ya_mm, 1)
                if t >= 1:
                    pe.wait_ge(h1_done, t)
                    if t >= 2:
                        pe.wait_ge(hT_a, t - 1)
                        pe.wait_ge(hT_d, t - 1)
                    for k in range(KD):
                        last = nc.tensor.transpose(ps[:, 5 + k // 4, (k % 4) * P:(k % 4 + 1) * P], h1[:, t - 1, k * P:(k + 1) * P], ident)
                    last.then_inc(hT_mm, 1)
                    pe.wait_ge(hT_a, t)
                    pe.wait_ge(hT_d, t)
                    if t >= 2:
                        pe.wait_ge(lg_ev, t - 1)
                    for k in range(KD):
                        last = nc.tensor.matmul(ps[:, 7, 0:G + E], hT1[:, k, :], w_r[:, k, :], start=(k == 0), stop=(k == KD - 1))
                    last.then_inc(lg_mm, 1)


def route_block(nc, a, ps, const, logits, comb, dest, token_of, expert_of, n_blocks):
    ctx = ExitStack()
    with ctx:
        sb = lambda n, s, d=F32: ctx.enter_context(nc.sbuf_tensor(n, s, d))
        sem = lambda n: ctx.enter_context(nc.semaphore(n))
        rb = sb("rb_", [P, G + E])
        w1 = sb("w1", [P, NT])
        gmax = sb("gmax", [P, NT])
        keyg = sb("keyg", [P, NT, G])
        ohg = sb("ohg", [P, NT, G])
        expo = sb("expo", [P, NT, G + 1])
        gsum = sb("gsum", [P, NT])
        pick = sb("pick", [P, NT, G, EG])
        e_in = sb("e_in", [P, NT, EG])
        key = sb("key", [P, NT, EG])
        oh = sb("oh", [P, 2, NT, EG])
        v12 = sb("v12", [P, 2, NT])
        A = sb("A", [P, 2, NT, G, EG])
        M = sb("M", [P, NT, E])
        rank = sb("rank", [P, NT, E])
        base = sb("base", [P, NT + 1, E])
        over = sb("over", [P, E, 7])
        nover = sb("nover", [P, E])
        pre = sb("pre", [P, 2, E])
        excl = sb("excl", [P, E])
        tmp = sb("tmp", [P, NT, E])
        stat = sb("stat", [P, 3, NT])
        q7 = sb("q7", [P, NT, 7])
        qq = sb("qq", [P, NT])
        pp = sb("pp", [P, 2, NT])
        bb = sb("bb", [P, 2, NT])
        sel = sb("sel", [P, 2, P])
        blk = sb("blk", [P, 2, MAXB + 1])
        of = sb("of", [1, 16, E])
        of1 = sb("of1", [1, MAXB + 1])

        bias_in, link, args, exps, mset, counted, made, used, idx_mm = (sem("e_" + n) for n in
            ("bias", "link", "args", "exps", "M", "counted", "made", "used", "idx_mm"))
        block = ctx.enter_context(nc.Block())
        io = lambda n: const[:, K_IOTA:K_IOTA + n]

        @block.sync
        def _(sp):
            sp.dma_start(rb[:, :], a["b_r"].broadcast_to([P, G + E])).then_inc(bias_in, 16)
            sp.wait_ge(bias_in, 16)

        @block.scalar
        def _(act):
            act.wait_ge(args, 2)
            nc.scalar.activation(expo[:, :, :], expo[:, :, :], ACT.Exp).then_inc(exps, 1)

        @block.tensor
        def _(pe):
            pe.wait_ge(mset, 1)
            flat = M[:, :, :].rearrange("p t e -> p (t e)")
            nc.tensor.matmul(ps[:, 0, 0:NT * E], const[:, K_TRI:K_TRI + P], flat, start=True, stop=True)
            nc.tensor.matmul(ps[:, 1, 0:NT * E], const[:, K_ONE:K_ONE + P], flat, start=True, stop=True).then_inc(counted, 1)
            for n in range(2 * NT):
                pe.wait_ge(made, n + 1)
                last = nc.tensor.matmul(ps[:, 2, 0:MAXB + 1], sel[:, n % 2, :], blk[:, n % 2, :], start=(n == 0), stop=(n == 2 * NT - 1))
                last.then_inc(used, 1)

        @block.vector
        def _(dve):
            v = nc.vector
            chain = Chain(dve, link)
            tt = lambda o, x, y, op: chain(v.tensor_tensor(o, x, y, op))
            one = lambda x, n: x.unsqueeze(len(x.shape)).broadcast_to(list(x.shape) + [n])
            dve.wait_ge(bias_in, 16)
            tt(logits[:, :, :], logits[:, :, :], rb[:, :].unsqueeze(1).broadcast_to([P, NT, G + E]), ALU.add)
            lg, le = logits[:, :, 0:G], logits[:, :, G:G + E].rearrange("p t (g e) -> p t g e", e=EG)

            def first_max(out_max, out_hot, x, keys, n):
                desc = const[:, K_DESC + EG - n:K_DESC + EG].unsqueeze(1).broadcast_to([P, NT, n])
                chain(v.reduce_max(out_max, x, AX.X))
                tt(keys, x, one(out_max, n), ALU.is_equal)
                tt(keys, keys, desc, ALU.mult)
                chain(v.reduce_max(w1[:, :], keys, AX.X))
                tt(out_hot, keys, one(w1[:, :], n), ALU.is_equal)

            first_max(gmax[:, :], ohg[:, :, :], lg, keyg[:, :, :], G)
            v.tensor_tensor(expo[:, :, 0:G], lg, one(gmax[:, :], G), ALU.subtract).then_inc(args, 1)
            tt(pick[:, :, :, :], le, one(ohg[:, :, :], EG), ALU.mult)
            chain(v.reduce_sum(e_in[:, :, :], pick[:, :, :, :].rearrange("p t g e -> p t e g"), AX.X))
            first_max(v12[:, 0, :], oh[:, 0, :, :], e_in[:, :, :], key[:, :, :], EG)
            chain(v.scalar_tensor_tensor(e_in[:, :, :], oh[:, 0, :, :], -1e30, e_in[:, :, :], ALU.mult, ALU.add))
            first_max(v12[:, 1, :], oh[:, 1, :, :], e_in[:, :, :], key[:, :, :], EG)
            v.tensor_tensor(expo[:, :, G], v12[:, 1, :], v12[:, 0, :], ALU.subtract).then_inc(args, 1)
            for j in range(2):
                for g in range(G):
                    tt(A[:, j, :, g, :], oh[:, j, :, :], ohg[:, :, g:g + 1].broadcast_to([P, NT, EG]), ALU.mult)
            Af = lambda j: A[:, j, :, :, :].rearrange("p t g e -> p t (g e)")
            v.tensor_tensor(M[:, :, :], Af(0), Af(1), ALU.add).then_inc(mset, 1)
            dve.wait_ge(exps, 1)
            chain(v.reduce_sum(gsum[:, :], expo[:, :, 0:G], AX.X))
            chain(v.tensor_scalar(qq[:, :], expo[:, :, G], 1.0, None, ALU.add))
            tt(gsum[:, :], gsum[:, :], qq[:, :], ALU.mult)
            chain(v.reciprocal(comb[:, 0, :], gsum[:, :]))
            tt(comb[:, 1, :], comb[:, 0, :], expo[:, :, G], ALU.mult)
            dve.wait_ge(counted, 1)
            chain(v.memset(base[:, 0, :], 0.0))
            for t in range(NT):
                tt(base[:, t + 1, :], base[:, t, :], ps[:, 1, E * t:E * (t + 1)], ALU.add)
            tt(rank[:, :, :], base[:, 0:NT, :], ps[:, 0, 0:NT * E].rearrange("p (t e) -> p t e", e=E), ALU.add)
            total = base[:, NT, :]
            chain(v.scalar_tensor_tensor(over[:, :, :], const[:, K_IOTA + 1:K_IOTA + 8].unsqueeze(1).broadcast_to([P, E, 7]), float(P),
                                         one(total, 7), ALU.mult, ALU.is_lt))
            chain(v.reduce_sum(nover[:, :], over[:, :, :], AX.X))
            src = nover
            cur = nover[:, :]
            step, n = 1, 0
            while step < E:
                nxt = pre[:, n % 2, :]
                chain(v.tensor_copy(nxt[:, 0:step], cur[:, 0:step]))
                tt(nxt[:, step:E], cur[:, step:E], cur[:, 0:E - step], ALU.add)
                cur, step, n = nxt, 2 * step, n + 1
            incl = cur
            tt(excl[:, :], incl, nover[:, :], ALU.subtract)
            for j in range(2):
                for m, table in enumerate((rank[:, :, :], excl[:, :].unsqueeze(1).broadcast_to([P, NT, E]),
                                           io(E).unsqueeze(1).broadcast_to([P, NT, E]))):
                    tt(tmp[:, :, :], Af(j), table, ALU.mult)
                    chain(v.reduce_sum(stat[:, m, :], tmp[:, :, :], AX.X))
                chain(v.scalar_tensor_tensor(q7[:, :, :], const[:, K_IOTA + 1:K_IOTA + 8].unsqueeze(1).broadcast_to([P, NT, 7]),
                                             float(P), one(stat[:, 0, :], 7), ALU.mult, ALU.is_le))
                chain(v.reduce_sum(qq[:, :], q7[:, :, :], AX.X))
                chain(v.scalar_tensor_tensor(pp[:, j, :], qq[:, :], -float(P), stat[:, 0, :], ALU.mult, ALU.add))
                tt(stat[:, 1, :], stat[:, 1, :], qq[:, :], ALU.add)
                tt(stat[:, 1, :], stat[:, 1, :], stat[:, 2, :], ALU.subtract)
                chain(v.tensor_scalar(qq[:, :], qq[:, :], 1.0, None, ALU.min))
                chain(v.scalar_tensor_tensor(stat[:, 1, :], stat[:, 1, :], float(E - 1), qq[:, :], ALU.add, ALU.mult))
                tt(bb[:, j, :], stat[:, 2, :], stat[:, 1, :], ALU.add)
                chain(v.scalar_tensor_tensor(dest[:, j, :], bb[:, j, :], float(P), pp[:, j, :], ALU.mult, ALU.add))
            for n in range(2 * NT):
                j, t = n // NT, n % NT
                if n >= 2:
                    dve.wait_ge(used, n - 1)
                v.tensor_scalar(sel[:, n % 2, :], io(P), pp[:, j, t:t + 1], None, ALU.is_equal)
                v.tensor_scalar(blk[:, n % 2, :], io(MAXB + 1), bb[:, j, t:t + 1], const[:, K_TOK + t:K_TOK + t + 1],
                                ALU.is_equal, ALU.mult).then_inc(made, 1)
            chain(v.tensor_copy(of1[0:1, 0:E], const[0:1, K_IOTA:K_IOTA + E]))
            tt(of[0:1, :, :], incl[0:1, :].unsqueeze(1).broadcast_to([1, 16, E]),
               const[0:1, K_IOTA:K_IOTA + 16].unsqueeze(2).broadcast_to([1, 16, E]), ALU.is_le)
            chain(v.reduce_sum(of1[0:1, E:E + 16], of[0:1, :, :], AX.X))
            chain(v.tensor_scalar(expert_of[0:1, :], of1[0:1, :], float(E - 1), None, ALU.min))
            chain(v.tensor_scalar(n_blocks[0:1, 0:1], incl[0:1, E - 1:E], float(E - 2), None, ALU.add))
            dve.wait_ge(used, 2 * NT)
            chain(v.tensor_copy(token_of[:, :], ps[:, 2, 0:MAXB + 1]))


def expert_block(nc, a, ps, const, h1_dram, y_dram, token_of, expert_of, n_blocks):
    ctx = ExitStack()
    with ctx:
        sb = lambda n, s, d=F32: ctx.enter_context(nc.sbuf_tensor(n, s, d))
        sem = lambda n: ctx.enter_context(nc.semaphore(n))
        gu_w = sb("gu_w", [P, RING * WGU])
        dn_w = sb("dn_w", [P, RING * WDN])
        x = sb("x_rows", [P, D])
        xT = sb("xT", [P, KD, P])
        sg = sb("sg_e", [P, F])
        hh = sb("hh", [P, F])
        hT = sb("hT_e", [P, 2, P])
        y = sb("y_rows", [P, D])
        ident = const[:, K_ID:K_ID + P]
        (gu_in, dn_in, x_in, y_out, tx_mm, xT_a, xT_d, gu_mm, sg_done, hh_done, th_mm, hT_ev, dn_mm, y_a, y_d) = (
            sem("f_" + n) for n in ("gu_in", "dn_in", "x_in", "y_out", "tx_mm", "xT_a", "xT_d", "gu_mm", "sg", "hh", "th_mm",
                                    "hT_ev", "dn_mm", "y_a", "y_d"))
        block = ctx.enter_context(nc.Block())
        ds = bass.ds
        blocks = lambda eng: eng.value_load(n_blocks[0:1, 0:1], min_val=E - 2, max_val=MAXB - 2)

        @block.sync
        def _(sp):
            m = blocks(sp)

            def load(e, at):
                sp.dma_start(gu_w[:, ds(at, WGU)], a["w_gate_up"][ds(e, 1), :, :].rearrange("a p n -> p (a n)")).then_inc(gu_in, 16)

            def load_down(e, at):
                sp.dma_start(dn_w[:, ds(at, WDN)], a["w_down_t"][ds(e, 1), :, :].rearrange("a p n -> p (a n)")).then_inc(dn_in, 16)

            for b in range(RING):
                if b:
                    sp.wait_ge(gu_in, 16 * b)
                load(b, b * WGU)
                if b:
                    sp.wait_ge(dn_in, 16 * b)
                load_down(b, b * WDN)
            with sp.Fori(1, m + 2 - (RING - 1)) as used:
                b = used + (RING - 1)
                e = sp.value_load(expert_of[0:1, ds(b, 1)], min_val=0, max_val=E - 1)
                slot = sp.snap(b % RING)
                sp.wait_ge(gu_in, b * 16)
                sp.wait_ge(gu_mm, used)
                load(e, slot * WGU)
                sp.wait_ge(dn_in, b * 16)
                sp.wait_ge(dn_mm, used)
                load_down(e, slot * WDN)

        @block.gpsimd
        def _(pool):
            m = blocks(pool)

            def gather(b):
                if b:
                    pool.wait_ge(tx_mm, b)
                pool.indirect_dma_start(out=x[:, :], out_offset=None, in_=h1_dram,
                                        in_offset=bass.IndirectOffsetOnAxis(ap=token_of[:, b:b + 1], axis=0)).then_inc(x_in, 16)

            for b in range(E):
                gather(b)
            for b in range(E, MAXB):
                with pool.If(m > b - 2):
                    gather(b)
            pool.wait_ge(y_out, m * 16 + 32)

        @block.scalar
        def _(act):
            m = blocks(act)

            def x_part(b):
                act.wait_ge(tx_mm, b + 1)
                nc.scalar.activation(xT[:, 0:4, :].rearrange("p k t -> p (k t)"), ps[:, 1, :], ACT.Copy).then_inc(xT_a, 1)

            def h_part(b):
                act.wait_ge(th_mm, b + 1)
                nc.scalar.activation(hT[:, :, :].rearrange("p k t -> p (k t)"), ps[:, 3, 0:2 * P], ACT.Copy).then_inc(hT_ev, 1)

            def y_part(b, first):
                act.wait_ge(dn_mm, b + 1)
                if not first:
                    act.wait_ge(y_out, b * 16)
                nc.scalar.activation(y[:, 0:512], ps[:, 4, :], ACT.Copy).then_inc(y_a, 1)
                act.wait_ge(y_a, b + 1)
                act.wait_ge(y_d, b + 1)
                act.dma_start(y_dram[ds(b * P, P), :], y[:, :]).then_inc(y_out, 16)

            def silu(b):
                act.wait_ge(gu_mm, b + 1)
                nc.scalar.activation(sg[:, :], ps[:, 0, 0:F], ACT.Silu).then_inc(sg_done, 1)

            x_part(0)
            silu(0)
            x_part(1)
            h_part(0)
            act.wait_ge(hh_done, 1)
            silu(1)
            x_part(2)
            y_part(0, True)
            h_part(1)
            act.wait_ge(hh_done, 2)
            silu(2)
            with act.Fori(3, m + 2) as b:
                x_part(b)
                y_part(b - 2, False)
                h_part(b - 1)
                act.wait_ge(hh_done, b)
                silu(b)
            y_part(m, False)
            h_part(m + 1)
            y_part(m + 1, False)

        @block.vector
        def _(dve):
            m = blocks(dve)

            def x_part(b):
                dve.wait_ge(tx_mm, b + 1)
                nc.vector.tensor_copy(xT[:, 4:8, :].rearrange("p k t -> p (k t)"), ps[:, 2, :]).then_inc(xT_d, 1)

            def y_part(b, first):
                dve.wait_ge(dn_mm, b + 1)
                if not first:
                    dve.wait_ge(y_out, b * 16)
                nc.vector.tensor_copy(y[:, 512:1024], ps[:, 5, :]).then_inc(y_d, 1)

            def hidden(b, first):
                dve.wait_ge(sg_done, b + 1)
                if not first:
                    dve.wait_ge(th_mm, b)
                nc.vector.tensor_tensor(hh[:, :], sg[:, :], ps[:, 0, F:2 * F], ALU.mult).then_inc(hh_done, 1)

            x_part(0)
            hidden(0, True)
            x_part(1)
            hidden(1, False)
            x_part(2)
            y_part(0, True)
            hidden(2, False)
            with dve.Fori(3, m + 2) as b:
                x_part(b)
                y_part(b - 2, False)
                hidden(b, False)
            y_part(m, False)
            y_part(m + 1, False)

        @block.tensor
        def _(pe):
            m = blocks(pe)

            def turn_x(b):
                pe.wait_ge(x_in, b * 16 + 16)
                for k in range(KD):
                    last = nc.tensor.transpose(ps[:, 1 + k // 4, (k % 4) * P:(k % 4 + 1) * P], x[:, k * P:(k + 1) * P], ident)
                last.then_inc(tx_mm, 1)

            def gate_up(b, slot, first):
                pe.wait_ge(gu_in, b * 16 + 16)
                pe.wait_ge(xT_a, b + 1)
                pe.wait_ge(xT_d, b + 1)
                if not first:
                    pe.wait_ge(hh_done, b)
                for k in range(KD):
                    last = nc.tensor.matmul(ps[:, 0, :], xT[:, k, :], gu_w[:, ds(slot * WGU + k * 2 * F, 2 * F)],
                                            start=(k == 0), stop=(k == KD - 1))
                last.then_inc(gu_mm, 1)

            def turn_h(b):
                pe.wait_ge(hh_done, b + 1)
                for k in range(2):
                    last = nc.tensor.transpose(ps[:, 3, k * P:(k + 1) * P], hh[:, k * P:(k + 1) * P], ident)
                last.then_inc(th_mm, 1)

            def down(b, slot, first):
                pe.wait_ge(dn_in, b * 16 + 16)
                pe.wait_ge(hT_ev, b + 1)
                if not first:
                    pe.wait_ge(y_a, b)
                    pe.wait_ge(y_d, b)
                for half in range(2):
                    for k in range(2):
                        last = nc.tensor.matmul(ps[:, 4 + half, :], hT[:, k, :], dn_w[:, ds(slot * WDN + k * D + 512 * half, 512)],
                                                start=(k == 0), stop=(k == 1))
                last.then_inc(dn_mm, 1)

            turn_x(0)
            gate_up(0, 0, True)
            turn_x(1)
            turn_h(0)
            gate_up(1, 1, False)
            turn_x(2)
            down(0, 0, True)
            turn_h(1)
            gate_up(2, 2, False)
            with pe.Fori(3, m + 2) as b:
                turn_x(b)
                down(b - 2, (b - 2) % RING, False)
                turn_h(b - 1)
                gate_up(b, b % RING, False)
            down(m, m % RING, False)
            turn_h(m + 1)
            down(m + 1, (m + 1) % RING, False)


def final_block(nc, a, ps, const, h1, y_dram, comb, dest, out):
    ctx = ExitStack()
    with ctx:
        sb = lambda n, s, d=F32: ctx.enter_context(nc.sbuf_tensor(n, s, d))
        sem = lambda n: ctx.enter_context(nc.semaphore(n))
        g2 = sb("g2", [P, D])
        b2 = sb("b2", [P, D])
        yy = sb("yy", [P, NT, 2, D])
        stats = sb("stats2", [P, 12])
        mv = sb("mv2", [P, 2])
        rstd = sb("rstd2", [P, 1])
        g_in, link, stats_done, rstd_done, gained, done, out_s, ah = (sem("g_" + n) for n in
            ("g_in", "link", "stats", "rstd", "gained", "done", "out", "ah"))
        y_in = [sem(f"g_y{t}") for t in range(NT)]
        plink = sem("g_plink")
        block = ctx.enter_context(nc.Block())

        @block.sync
        def _(sp):
            sp.dma_start(g2[:, :], a["ln2_g"].broadcast_to([P, D])).then_inc(g_in, 16)
            sp.dma_start(b2[:, :], a["ln2_b"].broadcast_to([P, D])).then_inc(g_in, 16)
            for t in range(NT):
                sp.wait_ge(done, t + 1)
                sp.dma_start(out[0, P * t:P * (t + 1), :], h1[:, t, :]).then_inc(out_s, 16)
            sp.wait_ge(out_s, 16 * NT)

        @block.gpsimd
        def _(pool):
            for t in range(NT):
                for j in range(2):
                    pool.indirect_dma_start(out=yy[:, t, j, :], out_offset=None, in_=y_dram,
                                            in_offset=bass.IndirectOffsetOnAxis(ap=dest[:, j, t:t + 1], axis=0)).then_inc(y_in[t], 16)
            chain = Chain(pool, plink)
            pool.wait_ge(g_in, 32)
            for t in range(NT):
                pool.wait_ge(stats_done, t + 1)
                inverse_root(pool, chain, const, rstd[:, :], mv[:, 1:2], 1.0).then_inc(rstd_done, 1)
                pool.wait_ge(gained, t + 1)
                pool.tensor_tensor(h1[:, t, :], h1[:, t, :], b2[:, :], ALU.add).then_inc(done, 1)

        @block.scalar
        def _(act):
            for t in range(NT):
                nc.scalar.activation(h1[:, t, :], h1[:, t, :], ACT.Copy, scale=ALPHA).then_inc(ah, 1)

        @block.vector
        def _(dve):
            v = nc.vector
            chain = Chain(dve, link)
            dve.wait_ge(g_in, 32)
            for t in range(NT):
                dve.wait_ge(y_in[t], 32)
                dve.wait_ge(ah, t + 1)
                chain(v.scalar_tensor_tensor(h1[:, t, :], yy[:, t, 0, :], comb[:, 0, t:t + 1], h1[:, t, :], ALU.mult, ALU.add))
                chain(v.scalar_tensor_tensor(h1[:, t, :], yy[:, t, 1, :], comb[:, 1, t:t + 1], h1[:, t, :], ALU.mult, ALU.add))
                for b in range(2):
                    chain(v.bn_stats(stats[:, 6 * b:6 * b + 6], h1[:, t, 512 * b:512 * (b + 1)]))
                v.bn_aggr(mv[:, :], stats[:, :]).then_inc(stats_done, 1)
                dve.wait_ge(rstd_done, t + 1)
                chain(v.tensor_scalar(h1[:, t, :], h1[:, t, :], mv[:, 0:1], rstd[:, :], ALU.subtract, ALU.mult))
                v.tensor_tensor(h1[:, t, :], h1[:, t, :], g2[:, :], ALU.mult).then_inc(gained, 1)


def program(nc, a, out):
    h_dram = nc.dram_tensor("h_dram", [T, D], F32, kind="Internal").ap()
    h1_dram = nc.dram_tensor("h1_dram", [T, D], F32, kind="Internal").ap()
    y_dram = nc.dram_tensor("y_dram", [MAXB * P, D], F32, kind="Internal").ap()
    ps = nc.alloc_psum_tensor("ps", [P, 8, 512], F32)
    with (nc.sbuf_tensor("const", [P, K_END], F32) as const, nc.sbuf_tensor("logits", [P, NT, G + E], F32) as logits,
          nc.sbuf_tensor("h1", [P, NT, D], F32) as h1):
        early, at = h1[:, :, :].rearrange("p t d -> p (t d)"), 0

        def piece(*dims):
            nonlocal at
            size = int(np.prod(dims))
            v = early[:, at:at + size]
            at += size
            if len(dims) == 2:
                v = v.rearrange("p (a b) -> p a b", a=dims[0])
            return v

        u, cw, v_meta = piece(NC4, UW), piece(NC4, TAPS + 1), piece(H * VD)
        z, zT, q_t, k_t = piece(ZR), piece(5, P), piece(H, QK), piece(H, QK)
        assert at <= NT * D
        with nc.sbuf_tensor("acc", [P, NC4, T], F32) as acc, nc.sbuf_tensor("hT", [P, KD, META + T], F32) as hT:
            flat = hT[:, :, :].rearrange("p k t -> p (k t)")
            o_all = flat[:, 0:NT * C].rearrange("p (t c) -> p t c", c=C)
            p = flat[:, NT * C:NT * C + 2 * T].rearrange("p (b n) -> p b n", b=2)
            pT = flat[:, NT * C + 2 * T:NT * C + 4 * T].rearrange("p (b k n) -> p b k n", b=2, n=P)
            input_block(nc, a, ps, const, hT, u, h_dram, y_dram)
            with (nc.sbuf_tensor("qT", [QK, H, T], F32) as qT, nc.sbuf_tensor("kT", [QK, H, META + T], F32) as kT,
                  nc.sbuf_tensor("v_all", [P, NT + 1, H * VD], F32) as v_all):
                mixer_block(nc, a, ps, const, hT, u, acc, cw, qT, kT, v_all, v_meta, z, zT, q_t, k_t)
                attention_block(nc, ps, const, u, acc, cw, qT, kT, v_all, v_meta, o_all, p, pT)
            merge_block(nc, a, ps, const, acc, o_all, h_dram, h1, h1_dram, logits)
        with (nc.sbuf_tensor("comb", [P, 2, NT], F32) as comb,
              nc.sbuf_tensor("dest", [P, 2, NT], I32) as dest, nc.sbuf_tensor("token_of", [P, MAXB + 1], I32) as token_of,
              nc.sbuf_tensor("expert_of", [1, MAXB + 1], I32) as expert_of, nc.sbuf_tensor("n_blocks", [1, 1], I32) as n_blocks):
            route_block(nc, a, ps, const, logits, comb, dest, token_of, expert_of, n_blocks)
            expert_block(nc, a, ps, const, h1_dram, y_dram, token_of, expert_of, n_blocks)
            final_block(nc, a, ps, const, h1, y_dram, comb, dest, out)


def kernel(**inputs):
    import numpy as _np
    import concourse.bacc as _bacc
    from concourse import mybir as _mybir
    from concourse.bass_utils import run_bass_kernel_spmd as _run

    i = {k: _np.asarray(v) for k, v in inputs.items()}
    tile = lambda w: w.reshape(w.shape[0] // P, P, -1).transpose(1, 0, 2)
    w_in = i["w_in"][0]
    conv = tile(w_in[:, :2 * C]).reshape(P, KD, 2, NC4, P).transpose(0, 3, 1, 2, 4).reshape(P, NC4, KD * 2 * P)
    kv = i["w_ukv"][0].reshape(KVL, H, 2, NOPE).transpose(0, 2, 1, 3).reshape(KVL, 2 * H * NOPE)
    experts = lambda w: w.reshape(E, w.shape[1] // P, P, w.shape[2]).transpose(0, 2, 1, 3)
    arrays = {
        "x": i["x"], "meta_tokens": i["meta_tokens"], "ln_in_g": i["ln_in_g"], "ln_in_b": i["ln_in_b"],
        "ln1_g": i["ln1_g"], "ln1_b": i["ln1_b"], "ln2_g": i["ln2_g"], "ln2_b": i["ln2_b"],
        "consts": constants(),
        "w_conv_in": conv,
        "w_z": tile(w_in[:, 2 * C:]),
        "w_q": tile(i["w_uq"][0]),
        "w_kv": tile(kv),
        "qkv_g": _np.concatenate([i["q_norm_g"][0].reshape(3, P).T, i["kv_norm_g"][0].reshape(2, P).T], 1),
        "conv_wb": _np.concatenate([i["conv_w"][0].reshape(TAPS, NC4, P), i["conv_b"][0].reshape(1, NC4, P)]).transpose(2, 1, 0),
        "conv_ln": _np.stack([i["conv_ln_g"][0].reshape(NC4, P), i["conv_ln_b"][0].reshape(NC4, P)]).transpose(2, 0, 1),
        "out_g": _np.concatenate([i["conv_out_g"][0], i["attn_out_g"][0]]).reshape(KD, P).T,
        "w_o": tile(i["w_o"][0]),
        "w_r": tile(_np.concatenate([i["w_rg"][0], i["w_re"][0]], 1)),
        "b_r": _np.concatenate([i["b_rg"], i["b_re"]], 1),
        "w_gate_up": _np.concatenate([experts(i["w_gate"][0]), experts(i["w_up"][0])], 3).reshape(E, P, WGU),
        "w_down_t": experts(i["w_down"][0]).reshape(E, P, WDN),
    }
    arrays = {k + "_in": _np.ascontiguousarray(v) for k, v in arrays.items()}
    nc = _bacc.Bacc("TRN2", target_bir_lowering=False, num_devices=1)
    aps = {k[:-3]: nc.dram_tensor(k, v.shape, _mybir.dt.from_np(v.dtype), kind="ExternalInput").ap() for k, v in arrays.items()}
    out = nc.dram_tensor("out_0", (1, T, D), _mybir.dt.float32, kind="ExternalOutput").ap()
    program(nc, aps, out)
    r = _run(nc, [arrays], core_ids=[0])
    return r.results[0]["out_0"]
```

```python
import concourse.bass as bass
from concourse import mybir
from contextlib import ExitStack
import numpy as np

F32 = mybir.dt.float32
I32 = mybir.dt.int32
ALU = mybir.AluOpType
ACT = mybir.ActivationFunctionType
AX = mybir.AxisListType

P = 128
D = 1024
T = 1024
NT = T // P
META = 16
KD = D // P
C = 512
NC4 = C // P
TAPS = 31
CHUNK = 64
H = 8
NOPE, ROPE, VD = 64, 32, 64
QK = NOPE + ROPE
QL, KVL = 384, 256
ZR = QL + KVL + ROPE
G, EG, E = 4, 8, 32
F = 256
MAXB = E + 2 * T // P - 1
ALPHA = float(np.float32(2.0 ** 0.25))
EPS = 1e-5
NEG_INF = -1e30
PAD = TAPS - 1 - META
UW = PAD + META + T
WGU, WDN = KD * 2 * F, (F // P) * D
WE = WGU + WDN
WR = 96
RING = 4

CUTS = [0, META + 3 * P, META + 6 * P, META + T]
CHUNK_TAPS = [(n, c, k) for n in range(3) for c in range(2) for k in range(TAPS)]
EARLY_TAPS = 160

K_ID = 0
K_TRI = K_ID + P
K_ONE = K_TRI + P
K_COS = K_ONE + P
K_SIN = K_COS + (NT + 1) * ROPE
K_IOTA = K_SIN + (NT + 1) * ROPE
K_TOK = K_IOTA + P
K_DESC = K_TOK + NT
K_MH = K_DESC + EG
K_EPS = K_MH + NT
K_END = K_EPS + 1


def constants():
    t = np.zeros((P, K_END), np.float32)
    t[:, K_ID:K_ID + P] = np.eye(P)
    t[:, K_TRI:K_TRI + P] = np.triu(np.ones((P, P)), 1)
    t[:, K_ONE:K_ONE + P] = 1.0
    half = ROPE // 2
    freq = (np.float32(10000.0) ** (-np.arange(half, dtype=np.float32) / np.float32(half))).astype(np.float32)
    ang = np.arange(META + T, dtype=np.float32)[:, None] * freq[None, :]
    for name, f in ((K_COS, np.cos), (K_SIN, np.sin)):
        v = f(ang).astype(np.float32)
        v = np.concatenate([v, v], 1)
        t[:META, name:name + ROPE] = v[:META]
        t[:, name + ROPE:name + (NT + 1) * ROPE] = v[META:].reshape(NT, P, ROPE).transpose(1, 0, 2).reshape(P, -1)
    t[:, K_IOTA:K_IOTA + P] = np.arange(P)
    t[:, K_TOK:K_TOK + NT] = np.arange(T).reshape(NT, P).T
    t[:, K_DESC:K_DESC + EG] = np.arange(EG, 0, -1)
    t[:, K_MH:K_MH + NT] = -0.5
    t[:, K_EPS] = EPS
    return t


class Chain:

    def __init__(self, engine, semaphore):
        self.engine, self.semaphore, self.count = engine, semaphore, 0

    def __call__(self, instruction):
        self.count += 1
        instruction.then_inc(self.semaphore, 1)
        self.engine.wait_ge(self.semaphore, self.count)


def inverse_root(pool, chain, const, out, var, scale):
    r, n = out.shape
    chain(pool.tensor_scalar(out, var, scale, EPS, ALU.mult, ALU.add))
    return pool.tensor_tensor(out, out, const[:r, K_MH:K_MH + n], ALU.pow)


def rows(t):
    return META if t == 0 else P


def col(t):
    return 0 if t == 0 else META + P * (t - 1)


def chunk_tap(nc, chain, u, acc, cw, n, c, k):
    lo = max(CUTS[n] - META, 0)
    tap(nc, chain, u, acc, cw, c, k, lo, CUTS[n + 1] - META - lo)


def tap(nc, chain, u, acc, cw, c, k, lo=0, n=T):
    out, shifted = acc[:, c, lo:lo + n], u[:, c, lo + k:lo + k + n]
    if k == 0:
        chain(nc.vector.tensor_scalar(out, shifted, cw[:, c, 0:1], cw[:, c, TAPS:TAPS + 1], ALU.mult, ALU.add))
    else:
        chain(nc.vector.scalar_tensor_tensor(out, shifted, cw[:, c, k:k + 1], out, ALU.mult, ALU.add))


def input_block(nc, a, ps, chains, const, hT, u, acc, cw, h_dram):
    ctx = ExitStack()
    with ctx:
        sb = lambda n, s, d=F32: ctx.enter_context(nc.sbuf_tensor(n, s, d))
        sem = lambda n: ctx.enter_context(nc.semaphore(n))
        NS, NB = NT + 1, 4
        x_t = sb("x_t", [P, NB, D])
        h_t = sb("h_t", [P, NB, D])
        g_in = sb("g_in", [P, D])
        b_in = sb("b_in", [P, D])
        w_c = sb("w_c", [P, NC4, KD * 2 * P])
        sg = sb("sg", [P, 2, 512])
        stats = sb("stats", [P, 2, 12])
        mv = sb("mv", [P, NS, 2])
        rstd = sb("rstd", [P, NS, 1])
        ident = const[:, K_ID:K_ID + P]

        consts_in, gb_in, cw_in, w_in = sem("a_consts_in"), sem("a_gb_in"), sem("a_cw_in"), [sem(f"a_w_in{c}") for c in range(NC4)]
        x_in = [sem(f"a_x_in{b}") for b in range(NB)]
        stats_done, rstd_done, normed, scaled, h_done = (sem("a_" + n) for n in ("stats", "rstd", "normed", "scaled", "h"))
        h_out = [sem(f"a_h_out{b}") for b in range(NB)]
        transposed, hT_act, hT_dve = (sem("a_" + n) for n in ("transposed", "hT_act", "hT_dve"))
        gate_done, sig_done, u_done = (sem("a_" + n) for n in ("gate", "sig", "u"))
        block = ctx.enter_context(nc.Block())
        units = [(n, c) for n in range(3) for c in range(NC4)]
        NU = len(units)

        @block.sync
        def _(sp):
            def load(t):
                if t >= NB:
                    sp.wait_ge(normed, t - NB + 1)
                src = a["meta_tokens"] if t == 0 else a["x"][0, P * (t - 1):P * t, :]
                sp.dma_start(x_t[:rows(t), t % NB, :], src).then_inc(x_in[t % NB], 16)

            def store(t):
                sp.wait_ge(h_done, t + 1)
                sp.dma_start(h_dram[P * (t - 1):P * t, :], h_t[:, t % NB, :]).then_inc(h_out[t % NB], 16)

            load(0)
            load(1)
            sp.dma_start(const[:, :], a["consts"]).then_inc(consts_in, 16)
            sp.dma_start(g_in[:, :], a["ln_in_g"].rearrange("(a n) -> a n", a=1).broadcast_to([P, D])).then_inc(gb_in, 16)
            sp.dma_start(b_in[:, :], a["ln_in_b"].rearrange("(a n) -> a n", a=1).broadcast_to([P, D])).then_inc(gb_in, 16)
            for t in range(2, NS):
                load(t)
                if t == 4:
                    for c in range(NC4):
                        sp.dma_start(w_c[:, c, :], a["w_conv_in"][:, c, :]).then_inc(w_in[c], 16)
                    sp.dma_start(cw[:, :, :], a["conv_wb"]).then_inc(cw_in, 16)
                if t > NB:
                    store(t - NB)
            for t in range(NS - NB, NS):
                store(t)
            for b in range(NB):
                sp.wait_ge(h_out[b], 16 * (NT // NB))

        def add_bias(pool, t):
            r = rows(t)
            pool.wait_ge(scaled, t + 1)
            pool.tensor_tensor(h_t[:r, t % NB, :], h_t[:r, t % NB, :], b_in[:r, :], ALU.add).then_inc(h_done, 1)

        @block.gpsimd
        def _(pool):
            chain = chains["gpsimd"]
            pool.memset(u[:, :, 0:PAD], 0.0)
            pool.wait_ge(consts_in, 16)
            for t in range(NS):
                r = rows(t)
                pool.wait_ge(stats_done, t + 1)
                inverse_root(pool, chain, const, rstd[:r, t, :], mv[:r, t, 1:2], 1.0).then_inc(rstd_done, 1)
                if t >= 1:
                    add_bias(pool, t - 1)
            add_bias(pool, NS - 1)

        def take(eng, ns, t, half, done):
            r = rows(t)
            eng.wait_ge(transposed, t + 1)
            src = ps[:, half, :].rearrange("p (k t) -> p k t", t=P)[:, :, 0:r]
            dst = hT[:, 4 * half:4 * half + 4, col(t):col(t) + r]
            if half:
                ns.tensor_copy(dst, src).then_inc(done, 1)
            else:
                ns.activation(dst, src, ACT.Copy).then_inc(done, 1)

        @block.vector
        def _(dve):
            chain = chains["vector"]

            def statistics(t):
                r = rows(t)
                dve.wait_ge(x_in[t % NB], 16 * (t // NB + 1))
                if t >= 2:
                    dve.wait_ge(stats_done, t - 1)
                nc.vector.bn_stats(stats[:r, t % 2, 0:6], x_t[:r, t % NB, 0:512])
                chain(nc.vector.bn_stats(stats[:r, t % 2, 6:12], x_t[:r, t % NB, 512:1024]))
                nc.vector.bn_aggr(mv[:r, t, :], stats[:r, t % 2, :]).then_inc(stats_done, 1)

            def gated(j):
                n, c = units[j]
                lo, hi = CUTS[n], CUTS[n + 1]
                dve.wait_ge(sig_done, j + 1)
                nc.vector.tensor_tensor(u[:, c, PAD + lo:PAD + hi], ps[:, 2 + 2 * (j % 2), 0:hi - lo], sg[:, j % 2, 0:hi - lo],
                                        ALU.mult).then_inc(u_done, 1)

            statistics(0)
            for t in range(NS):
                r = rows(t)
                if t + 1 < NS:
                    statistics(t + 1)
                dve.wait_ge(rstd_done, t + 1)
                if t >= NB:
                    if t > NB:
                        dve.wait_ge(h_out[t % NB], 16 * ((t - 1) // NB))
                    dve.wait_ge(transposed, t - NB + 1)
                nc.vector.tensor_scalar(h_t[:r, t % NB, :], x_t[:r, t % NB, :], mv[:r, t, 0:1], rstd[:r, t, :],
                                        ALU.subtract, ALU.mult).then_inc(normed, 1)
                if t == 0:
                    dve.wait_ge(gb_in, 32)
                dve.wait_ge(normed, t + 1)
                nc.vector.tensor_tensor(h_t[:r, t % NB, :], h_t[:r, t % NB, :], g_in[:r, :], ALU.mult).then_inc(scaled, 1)
                if 1 <= t <= 4:
                    take(dve, nc.vector, t - 1, 1, hT_dve)
            done = 0
            for j, (n, _) in enumerate(units):
                gated(j)
                if j < 5:
                    take(dve, nc.vector, 4 + j, 1, hT_dve)
                if j == 0:
                    dve.wait_ge(cw_in, 16)
                dve.wait_ge(u_done, j + 1)
                ready = sum(m[0:2] in units[:j + 1] for m in CHUNK_TAPS)
                upto = min(ready, done + (16 if n < 2 else 12), EARLY_TAPS)
                while done < upto:
                    chunk_tap(nc, chain, u, acc, cw, *CHUNK_TAPS[done])
                    done += 1
            assert done == EARLY_TAPS

        @block.scalar
        def _(act):
            def sigmoid(j):
                act.wait_ge(gate_done, j + 1)
                if j >= 2:
                    act.wait_ge(u_done, j - 1)
                n = CUTS[units[j][0] + 1] - CUTS[units[j][0]]
                nc.scalar.activation(sg[:, j % 2, 0:n], ps[:, 3 + 2 * (j % 2), 0:n], ACT.Sigmoid).then_inc(sig_done, 1)

            for t in range(4):
                take(act, nc.scalar, t, 0, hT_act)
            for j in range(NU):
                sigmoid(j)
                if j < 5:
                    take(act, nc.scalar, 4 + j, 0, hT_act)

        @block.tensor
        def _(pe):
            def turn(t):
                r = rows(t)
                pe.wait_ge(h_done, t + 1)
                if t >= 1:
                    pe.wait_ge(hT_act, t)
                    pe.wait_ge(hT_dve, t)
                for k in range(KD):
                    last = nc.tensor.transpose(ps[:, k // 4, (k % 4) * P:(k % 4) * P + r], h_t[:r, t % NB, k * P:(k + 1) * P],
                                               ident[:r, :r])
                last.then_inc(transposed, 1)

            pe.wait_ge(consts_in, 16)
            for t in range(4):
                turn(t)
            for j, (n, c) in enumerate(units):
                lo, hi = CUTS[n], CUTS[n + 1]
                if c == 0:
                    pe.wait_ge(hT_act, (4, 7, NS)[n])
                    pe.wait_ge(hT_dve, (4, 7, NS)[n])
                if n == 0:
                    pe.wait_ge(w_in[c], 16)
                if j >= 2:
                    pe.wait_ge(u_done, j - 1)
                for part in range(2):
                    for k in range(KD):
                        w = w_c[:, c, k * 2 * P + part * P:k * 2 * P + (part + 1) * P]
                        last = nc.tensor.matmul(ps[:, 2 + 2 * (j % 2) + part, 0:hi - lo], w, hT[:, k, lo:hi],
                                                start=(k == 0), stop=(k == KD - 1))
                last.then_inc(gate_done, 1)
                if j < 5:
                    turn(4 + j)


def mixer_block(nc, a, ps, chains, const, hT, u, acc, cw, qT, kT, v_all, v_meta, z, zT, q_t, k_t, w_z_q):
    ctx = ExitStack()
    with ctx:
        sb = lambda n, s, d=F32: ctx.enter_context(nc.sbuf_tensor(n, s, d))
        sem = lambda n: ctx.enter_context(nc.semaphore(n))
        w_z = w_z_q[:, 0:KD * ZR].rearrange("p (k n) -> p k n", k=KD)
        w_q = w_z_q[:, KD * ZR:KD * ZR + 3 * H * QK].rearrange("p (k n) -> p k n", k=3)
        w_kv1 = sb("w_kv1", [P, 2 * H * NOPE])
        w_kv = [acc[:, 3, :], w_kv1[:, :]]
        qg = sb("qg", [P, 5])
        ssq = sb("ssq", [P, 2, 2])
        rr = sb("rr", [P, 2, 2])
        ra = sb("ra", [P, H, ROPE])
        rb = sb("rb", [P, H, ROPE])
        ka = sb("ka", [P, ROPE])
        kb = sb("kb", [P, ROPE])
        ident = const[:, K_ID:K_ID + P]

        w_ready, wz_ready, vm_in = sem("b_w"), sem("b_wz"), sem("b_vm")
        folded, z_mm, z_sq, z_copied, z_cp2, r_done = (sem("b_" + n) for n in ("folded", "z", "z_sq", "z_cp", "z_cp2", "r"))
        zT_mm, zT_a, zT_d = (sem("b_" + n) for n in ("zT_mm", "zT_a", "zT_d"))
        q_mm, kv_mm, q_ev, k_ev, v_ev, roped = (sem("b_" + n) for n in ("q_mm", "kv_mm", "q_ev", "k_ev", "v_ev", "roped"))
        kr_used = sem("b_kr_used")
        tq_mm, tk_mm, tq_ev, tk_ev = (sem("b_" + n) for n in ("tq_mm", "tk_mm", "tq_ev", "tk_ev"))
        block = ctx.enter_context(nc.Block())
        NS = NT + 1

        @block.sync
        def _(sp):
            sp.dma_start(w_z[:, :, :], a["w_z"]).then_inc(wz_ready, 16)
            sp.dma_start(w_q[:, :, :], a["w_q"]).then_inc(w_ready, 16)
            for k in range(2):
                sp.dma_start(w_kv[k], a["w_kv"][:, k, :]).then_inc(w_ready, 16)
            sp.dma_start(qg[:, :], a["qkv_g"]).then_inc(w_ready, 16)
            for h in range(H):
                if h == 0:
                    sp.wait_ge(v_ev, 1)
                    sp.wait_ge(folded, 6)
                sp.dma_start(v_meta[META * h:META * (h + 1), VD * h:VD * (h + 1)],
                             v_all[:META, 0, VD * h:VD * (h + 1)]).then_inc(vm_in, 16)
            sp.wait_ge(vm_in, 16 * H)

        @block.gpsimd
        def _(pool):
            pool.wait_ge(w_ready, 64)
            for k in range(3):
                pool.tensor_scalar(w_q[:, k, :], w_q[:, k, :], qg[:, k:k + 1], None, ALU.mult).then_inc(folded, 1)
            for k in range(2):
                pool.tensor_scalar(w_kv[k], w_kv[k], qg[:, 3 + k:4 + k], None, ALU.mult).then_inc(folded, 1)
            pool.memset(v_meta[:, :], 0.0).then_inc(folded, 1)
            chain = chains["gpsimd"]
            halves = lambda x, t, half: x[QK:QK + 1, :, t + CHUNK * half:t + CHUNK * (half + 1)]
            for t in range(NS):
                r = rows(t)
                c2 = const[:r, K_COS + ROPE * t:K_COS + ROPE * (t + 1)]
                s2 = const[:r, K_SIN + ROPE * t:K_SIN + ROPE * (t + 1)]
                half = ROPE // 2
                if t:
                    pool.wait_ge(roped, 2 * t - 1)
                    for half_tile, queries, keys in ((0, 1.0, 0.0), (1, 0.0, NEG_INF)):
                        pool.memset(halves(qT, P * (t - 1), half_tile), queries)
                        ins = pool.memset(halves(kT, col(t), half_tile), keys)
                    chain(ins)
                pool.wait_ge(z_sq, t + 1)
                for part, width in ((0, QL), (1, KVL)):
                    if part or t:
                        ins = inverse_root(pool, chain, const, rr[:r, t % 2, part:part + 1], ssq[:r, t % 2, part:part + 1], 1.0 / width)
                ins.then_inc(r_done, 1)
                pool.wait_ge(z_cp2, t + 1)
                kr = z[:r, QL + KVL:ZR]
                pool.tensor_tensor(ka[:r, :], kr, c2, ALU.mult)
                pool.tensor_tensor(kb[:r, :], kr, s2, ALU.mult).then_inc(kr_used, 1)
                pool.wait_ge(kr_used, t + 1)
                if t >= 1:
                    pool.wait_ge(tk_mm, t)
                one = lambda x, lo: x[:r, lo:lo + half].unsqueeze(1).broadcast_to([r, H, half])
                pool.tensor_tensor(k_t[:r, :, NOPE:NOPE + half], one(ka, 0), one(kb, half), ALU.subtract)
                pool.tensor_tensor(k_t[:r, :, NOPE + half:QK], one(kb, 0), one(ka, half), ALU.add).then_inc(roped, 1)
                if t >= 1:
                    pool.wait_ge(q_ev, 2 * t)
                    qr = q_t[:r, :, NOPE:QK]
                    many = lambda x: x.unsqueeze(1).broadcast_to([r, H, ROPE])
                    pool.tensor_tensor(ra[:r, :, :], qr, many(c2), ALU.mult)
                    chain(pool.tensor_tensor(rb[:r, :, :], qr, many(s2), ALU.mult))
                    pool.tensor_tensor(q_t[:r, :, NOPE:NOPE + half], ra[:r, :, 0:half], rb[:r, :, half:ROPE], ALU.subtract)
                    pool.tensor_tensor(q_t[:r, :, NOPE + half:QK], rb[:r, :, 0:half], ra[:r, :, half:ROPE], ALU.add).then_inc(roped, 1)

        @block.scalar
        def _(act):
            for t in range(NS + 1):
                if t < NS:
                    r = rows(t)
                    act.wait_ge(z_mm, t + 1)
                    if t:
                        act.wait_ge(zT_mm, t)
                        act.wait_ge(kr_used, t)
                        nc.scalar.activation(z[:r, 0:QL], ps[:r, 0, 0:QL], ACT.Copy).then_inc(z_copied, 1)
                        act.wait_ge(z_copied, t)
                        nc.scalar.activation(ps[:r, 0, 0:QL], ps[:r, 0, 0:QL], ACT.Square, accum_out=ssq[:r, t % 2, 0:1])
                    nc.scalar.activation(z[:r, QL:ZR], ps[:r, 1, 0:KVL + ROPE], ACT.Copy).then_inc(z_cp2, 1)
                    act.wait_ge(z_cp2, t + 1)
                    nc.scalar.activation(ps[:r, 1, 0:KVL], ps[:r, 1, 0:KVL], ACT.Square, accum_out=ssq[:r, t % 2, 1:2]).then_inc(z_sq, 1)
                if t >= 1:
                    e = t - 1
                    r = rows(e)
                    act.wait_ge(r_done, e + 1)
                    if e:
                        act.wait_ge(q_mm, e)
                        if e >= 2:
                            act.wait_ge(tq_mm, e - 1)
                        for b in range(2):
                            nc.scalar.activation(q_t[:r, 4 * b:4 * b + 4, :].rearrange("p h d -> p (h d)"), ps[:r, 4 + b, 0:4 * QK],
                                                 ACT.Copy, scale=rr[:r, e % 2, 0:1]).then_inc(q_ev, 1)
                    act.wait_ge(kv_mm, e + 1)
                    if e:
                        act.wait_ge(tk_mm, e)
                    nc.scalar.activation(k_t[:r, :, 0:NOPE], ps[:r, 6, :].rearrange("p (h d) -> p h d", d=NOPE), ACT.Copy,
                                         scale=rr[:r, e % 2, 1:2]).then_inc(k_ev, 1)
                    nc.scalar.activation(v_all[:r, e, :], ps[:r, 7, :], ACT.Copy, scale=rr[:r, e % 2, 1:2]).then_inc(v_ev, 1)

        taps = CHUNK_TAPS[EARLY_TAPS:] + [(2, k) for k in range(TAPS)]

        @block.vector
        def _(dve):
            done = 0
            dve.wait_ge(w_ready, 64)
            dve.wait_ge(wz_ready, 16)
            chain = chains["vector"]
            for t in range(NS + 2):
                if t >= 2:
                    e = t - 2
                    r = rows(e)
                    if e:
                        dve.wait_ge(tq_mm, e)
                        for b in range(2):
                            nc.vector.tensor_copy(qT[:QK, 4 * b:4 * b + 4, P * (e - 1):P * e],
                                                  ps[:QK, 2 + b, :].rearrange("p (h t) -> p h t", t=P)).then_inc(tq_ev, 1)
                    dve.wait_ge(tk_mm, e + 1)
                    for b in range(2):
                        nc.vector.tensor_copy(kT[:QK, 4 * b:4 * b + 4, col(e):col(e) + r],
                                              ps[:QK, 6 + b, :].rearrange("p (h t) -> p h t", t=P)[:, :, 0:r]).then_inc(tk_ev, 1)
                if t < NS:
                    r = rows(t)
                    dve.wait_ge(zT_mm, t + 1)
                    if t >= 1:
                        dve.wait_ge(kv_mm, t)
                        nc.vector.tensor_copy(zT[:, 0:3, 0:r], ps[:, 2, 0:3 * P].rearrange("p (k t) -> p k t", t=P)[:, :, 0:r]).then_inc(zT_d, 1)
                    nc.vector.tensor_copy(zT[:, 3:5, 0:r], ps[:, 3, 0:2 * P].rearrange("p (k t) -> p k t", t=P)[:, :, 0:r]).then_inc(zT_a, 1)
                upto = min(len(taps), len(taps) * (t + 1) // NS)
                while done < upto:
                    (chunk_tap if len(taps[done]) == 3 else tap)(nc, chain, u, acc, cw, *taps[done])
                    done += 1

        @block.tensor
        def _(pe):
            def latents(t):
                r, lo = rows(t), col(t)
                if t:
                    pe.wait_ge(z_sq, t)
                    for k in range(KD):
                        nc.tensor.matmul(ps[:r, 0, 0:QL], hT[:, k, lo:lo + r], w_z[:, k, 0:QL], start=(k == 0), stop=(k == KD - 1))
                for k in range(KD):
                    last = nc.tensor.matmul(ps[:r, 1, 0:KVL + ROPE], hT[:, k, lo:lo + r], w_z[:, k, QL:ZR],
                                            start=(k == 0), stop=(k == KD - 1))
                last.then_inc(z_mm, 1)

            def heads_turned(t):
                r = rows(t)
                pe.wait_ge(roped, 2 * t + 1)
                pe.wait_ge(zT_d, min(t + 1, NT))
                pe.wait_ge(zT_a, min(t + 2, NS))
                if t:
                    pe.wait_ge(q_ev, 2 * t)
                    for h in range(H):
                        last = nc.tensor.transpose(ps[:QK, 2 + h // 4, (h % 4) * P:(h % 4 + 1) * P], q_t[:r, h, :], ident[:r, :r])
                    last.then_inc(tq_mm, 1)
                pe.wait_ge(k_ev, t + 1)
                pe.wait_ge(v_ev, t + 1)
                for h in range(H):
                    last = nc.tensor.transpose(ps[:QK, 6 + h // 4, (h % 4) * P:(h % 4) * P + r], k_t[:r, h, :], ident[:r, :r])
                last.then_inc(tk_mm, 1)

            def project(t):
                r = rows(t)
                if t == 0:
                    pe.wait_ge(folded, 5)
                else:
                    pe.wait_ge(zT_d, t)
                    if t >= 2:
                        pe.wait_ge(q_ev, 2 * (t - 1))
                    for b in range(2):
                        for k in range(3):
                            last = nc.tensor.matmul(ps[:r, 4 + b, 0:4 * QK], zT[:, k, 0:r], w_q[:, k, 4 * QK * b:4 * QK * (b + 1)],
                                                    start=(k == 0), stop=(k == 2))
                    last.then_inc(q_mm, 1)
                pe.wait_ge(zT_a, t + 1)
                if t:
                    pe.wait_ge(tk_ev, 2 * t)
                for b in range(2):
                    for k in range(2):
                        last = nc.tensor.matmul(ps[:r, 6 + b, :], zT[:, 3 + k, 0:r], w_kv[k][:, 512 * b:512 * (b + 1)],
                                                start=(k == 0), stop=(k == 1))
                last.then_inc(kv_mm, 1)

            def latents_turned(t):
                r = rows(t)
                if t >= 3:
                    pe.wait_ge(tq_ev, 2 * (t - 2))
                if t:
                    pe.wait_ge(z_copied, t)
                    for k in range(3):
                        nc.tensor.transpose(ps[:, 2, k * P:k * P + r], z[:r, k * P:(k + 1) * P], ident[:r, :r])
                pe.wait_ge(z_cp2, t + 1)
                if t >= 1:
                    pe.wait_ge(zT_a, t)
                for k in range(2):
                    last = nc.tensor.transpose(ps[:, 3, k * P:k * P + r], z[:r, QL + k * P:QL + (k + 1) * P], ident[:r, :r])
                last.then_inc(zT_mm, 1)

            pe.wait_ge(wz_ready, 16)
            for s in range(NS + 2):
                if s < NS:
                    latents(s)
                if s >= 2:
                    heads_turned(s - 2)
                if 1 <= s <= NS:
                    project(s - 1)
                if s < NS:
                    latents_turned(s)


def attention_units():
    units = []
    for i in range(NT):
        heads = 1024 // (P * (i + 1)) if i != 2 else 2
        units += [(i, h, heads) for h in range(0, H, heads)]
    return units


def attention_block(nc, a, ps, chains, const, u, acc, cw, qT, kT, v_all, v_meta, o_all, p, pT, w_o, g_o):
    ctx = ExitStack()
    with ctx:
        sb = lambda n, s, d=F32: ctx.enter_context(nc.sbuf_tensor(n, s, d))
        sem = lambda n: ctx.enter_context(nc.semaphore(n))
        m_s = sb("m_s", [P, NT, H, META])
        m_p = sb("m_p", [P, H, META])
        m_pT = sb("m_pT", [P, P])
        m_neg = sb("m_neg", [P, NT, H])
        r_max = sb("r_max", [P, 2, H])
        bias = sb("bias", [P, 2, H])
        sums = sb("sums", [P, 2, H])
        m_sums = sb("m_sums", [P, H])
        inv = sb("inv", [P, H])
        scale = float(np.float32(QK ** -0.5))
        ident = const[:, K_ID:K_ID + P]
        units = attention_units()
        NU = len(units)
        first = [n for n, (i, h, _) in enumerate(units) if h == 0] + [NU]

        (m_mm, m_copied, s_mm, biased, exp_done, t_mm, ev_act, ev_dve, pv_mm, m_arg, m_exp, m_t, m_tc, o_mm,
         o_done, sums_done) = (sem("c_" + n) for n in ("m_mm", "m_copied", "s_mm", "biased", "exp", "t_mm", "ev_act",
                                                             "ev_dve", "pv_mm", "m_arg", "m_exp", "m_t", "m_tc", "o_mm",
                                                             "o_done", "sums_done"))
        wo_in = sem("c_wo_in")
        block = ctx.enter_context(nc.Block())
        at = lambda i, h: h * (512 if i == 2 else P * (i + 1))
        pair = lambda n: ps[:, 2 * (n % 3):2 * (n % 3) + 2, :].rearrange("p b n -> p (b n)")

        def blocks_of(n):
            i, _, heads = units[n]
            return [(h, k) for h in range(heads) for k in range(i + 1)]

        m_tiles = [range(0, 3), range(3, 6), range(6, NT)]
        two_banks = lambda n: len(blocks_of(n)) > 4
        dve_evacs = lambda n: sum(two_banks(m) for m in range(n))

        @block.sync
        def _(sp):
            sp.dma_start(g_o[:, :], a["out_g"]).then_inc(wo_in, 16)
            sp.dma_start(w_o[:, :, :], a["w_o"]).then_inc(wo_in, 16)

        @block.gpsimd
        def _(pool):
            pool.wait_ge(wo_in, 32)
            for k in range(KD):
                pool.tensor_scalar(w_o[:, k, :], w_o[:, k, :], g_o[:, k:k + 1], None, ALU.mult)

        @block.tensor
        def _(pe):
            def scores(n):
                i, h0, heads = units[n]
                if n >= 3:
                    pe.wait_ge(ev_act, n - 2)
                    if dve_evacs(n - 2):
                        pe.wait_ge(ev_dve, dve_evacs(n - 2))
                keys = P * i
                for h in range(heads):
                    for lo in range(0, keys, 512):
                        hi = min(lo + 512, keys)
                        nc.tensor.matmul(pair(n)[:, at(i, h) + lo:at(i, h) + hi], qT[:QK, h0 + h, P * i:P * (i + 1)],
                                         kT[:QK, h0 + h, META + lo:META + hi], start=True, stop=True)
                    last = nc.tensor.matmul(pair(n)[:, at(i, h) + keys:at(i, h) + keys + P], qT[:, h0 + h, P * i:P * (i + 1)],
                                            kT[:, h0 + h, META + keys:META + keys + P], start=True, stop=True)
                last.then_inc(s_mm, 1)

            def transposes(n):
                i, _, _ = units[n]
                pe.wait_ge(exp_done, n + 1)
                for b, (h, k) in enumerate(blocks_of(n)):
                    last = nc.tensor.transpose(pair(n)[:, b * P:(b + 1) * P], p[:, n % 2, at(i, h) + k * P:at(i, h) + (k + 1) * P], ident)
                last.then_inc(t_mm, 1)

            def values(n):
                i, h0, heads = units[n]
                if h0 == 0 and i >= 1:
                    meta_values(i - 1)
                pe.wait_ge(ev_act, n + 1)
                if two_banks(n):
                    pe.wait_ge(ev_dve, dve_evacs(n + 1))
                for b, (h, k) in enumerate(blocks_of(n)):
                    at_v = slice(VD * (h0 + h), VD * (h0 + h + 1))
                    last = nc.tensor.matmul(ps[:, 6 + i % 2, at_v], pT[:, n % 2, b, :], v_all[:, k + 1, at_v],
                                            start=(h0 == 0 and b == 0), stop=False, skip_group_check=True)
                last.then_inc(pv_mm, 1)
                if h0 + heads == H:
                    pe.wait_ge(m_exp, i + 1)
                    if i >= 1:
                        pe.wait_ge(o_done, i)
                    nc.tensor.transpose(ps[:, 6 + (i + 1) % 2, 0:P], m_p[:, :, :].rearrange("p h k -> p (h k)"), ident).then_inc(m_t, 1)

            def meta_values(i):
                pe.wait_ge(m_tc, i + 1)
                nc.tensor.matmul(ps[:, 6 + i % 2, :], m_pT[:, :], v_meta[:, :], start=False, stop=True,
                                 skip_group_check=True).then_inc(o_mm, 1)

            def meta_scores(g):
                for i in m_tiles[g]:
                    for h in range(H):
                        c = P * (i - m_tiles[g][0]) + META * h
                        last = nc.tensor.matmul(ps[:, 5 + g, c:c + WR], qT[:QK, h, P * i:P * (i + 1)], kT[:QK, h, 0:WR], start=True, stop=True)
                last.then_inc(m_mm, 1)

            scores(0)
            meta_scores(0)
            scores(1)
            meta_scores(1)
            meta_scores(2)
            pe.wait_ge(m_copied, 3)
            for n in range(NU):
                transposes(n)
                if n + 2 < NU:
                    scores(n + 2)
                if n >= 1:
                    values(n - 1)
            values(NU - 1)
            meta_values(NT - 1)

        @block.scalar
        def _(act):
            def exps(n):
                i, h0, heads = units[n]
                if h0 == 0 and i >= 2:
                    act.wait_ge(o_done, i - 1)
                act.wait_ge(biased, n + 1)
                if n >= 2:
                    act.wait_ge(t_mm, n - 1)
                keys = P * (i + 1)
                for h in range(heads):
                    last = nc.scalar.activation(p[:, n % 2, at(i, h):at(i, h) + keys], pair(n)[:, at(i, h):at(i, h) + keys], ACT.Exp,
                                                bias=bias[:, i % 2, h0 + h:h0 + h + 1], scale=scale,
                                                accum_out=sums[:, i % 2, h0 + h:h0 + h + 1])
                last.then_inc(exp_done, 1)
                if h0 + heads == H:
                    act.wait_ge(m_arg, i + 1)
                    nc.scalar.activation(m_p[:, :, :], m_p[:, :, :], ACT.Exp).then_inc(m_exp, 1)

            def meta_copy(i):
                act.wait_ge(m_t, i + 1)
                if i >= 1:
                    act.wait_ge(o_mm, i)
                nc.scalar.activation(m_pT[:, :], ps[:, 6 + (i + 1) % 2, 0:P], ACT.Copy).then_inc(m_tc, 1)

            for g, tiles in enumerate(m_tiles):
                act.wait_ge(m_mm, g + 1)
                nc.scalar.activation(m_s[:, tiles[0]:tiles[-1] + 1, :, :].rearrange("p t h k -> p (t h k)"), ps[:, 5 + g, 0:P * len(tiles)],
                                     ACT.Copy).then_inc(m_copied, 1)
            exps(0)
            for n, (i, h0, _) in enumerate(units):
                if n + 1 < NU:
                    exps(n + 1)
                act.wait_ge(t_mm, n + 1)
                if n >= 2:
                    act.wait_ge(pv_mm, n - 1)
                m = min(4, len(blocks_of(n)))
                nc.scalar.activation(pT[:, n % 2, 0:m, :].rearrange("p k t -> p (k t)"), pair(n)[:, 0:m * P], ACT.Copy).then_inc(ev_act, 1)
                if h0 == 0 and i >= 1:
                    meta_copy(i - 1)
            meta_copy(NT - 1)

        taps = [(3, k) for k in range(TAPS)]

        @block.vector
        def _(dve):
            chain = chains["vector"]

            def maxima(n):
                i, h0, heads = units[n]
                dve.wait_ge(s_mm, n + 1)
                keys = P * (i + 1)
                if heads == 1:
                    src = pair(n)[:, 0:keys].unsqueeze(1)
                else:
                    src = pair(n).rearrange("p (h k) -> p h k", k=at(i, 1))[:, 0:heads, 0:keys]
                chain(nc.vector.reduce_max(r_max[:, n % 2, 0:heads], src, AX.X))
                if h0 == 0 and i >= 2:
                    dve.wait_ge(exp_done, first[i - 1])
                hs = slice(h0, h0 + heads)
                nc.vector.scalar_tensor_tensor(bias[:, i % 2, hs], r_max[:, n % 2, 0:heads], -scale, m_neg[:, i, hs],
                                               ALU.mult, ALU.min).then_inc(biased, 1)
                if h0 + heads == H:
                    dve.wait_ge(biased, n + 1)
                    if i >= 1:
                        dve.wait_ge(m_t, i)
                        dve.wait_ge(sums_done, i)
                    nc.vector.scalar_tensor_tensor(m_p[:, :, :], m_s[:, i, :, :], scale,
                                                   bias[:, i % 2, :].unsqueeze(2).broadcast_to([P, H, META]),
                                                   ALU.mult, ALU.add).then_inc(m_arg, 1)

            def finish(i):
                dve.wait_ge(sums_done, i + 1)
                chain(nc.vector.tensor_tensor(m_sums[:, :], m_sums[:, :], sums[:, i % 2, :], ALU.add))
                chain(nc.vector.reciprocal(inv[:, :], m_sums[:, :]))
                dve.wait_ge(o_mm, i + 1)
                nc.vector.tensor_tensor(o_all[:, i, :].rearrange("p (h d) -> p h d", d=VD),
                                        ps[:, 6 + i % 2, :].rearrange("p (h d) -> p h d", d=VD),
                                        inv[:, :].unsqueeze(2).broadcast_to([P, H, VD]), ALU.mult).then_inc(o_done, 1)

            def meta_sums(i):
                dve.wait_ge(m_exp, i + 1)
                if i >= 1:
                    dve.wait_ge(o_done, i)
                nc.vector.reduce_sum(m_sums[:, :], m_p[:, :, :], AX.X).then_inc(sums_done, 1)

            for g, tiles in enumerate(m_tiles):
                at_t = slice(tiles[0], tiles[-1] + 1)
                dve.wait_ge(m_copied, g + 1)
                chain(nc.vector.reduce_max(m_neg[:, at_t, :], m_s[:, at_t, :, :], AX.X))
                chain(nc.vector.tensor_scalar(m_neg[:, at_t, :], m_neg[:, at_t, :], -scale, None, ALU.mult))
                if g == 0:
                    maxima(0)
            done = 0
            for n, (i, h0, heads) in enumerate(units):
                if i >= 1 and h0 == 0:
                    meta_sums(i - 1)
                if n + 1 < NU:
                    maxima(n + 1)
                if two_banks(n):
                    dve.wait_ge(t_mm, n + 1)
                    if n >= 2:
                        dve.wait_ge(pv_mm, n - 1)
                    m = len(blocks_of(n))
                    nc.vector.tensor_copy(pT[:, n % 2, 4:m, :].rearrange("p k t -> p (k t)"), pair(n)[:, 512:m * P]).then_inc(ev_dve, 1)
                if i >= 1 and n == first[i] + 1:
                    finish(i - 1)
                upto = len(taps) * (n + 1) // NU
                while done < upto:
                    tap(nc, chain, u, acc, cw, *taps[done])
                    done += 1
            meta_sums(NT - 1)
            finish(NT - 1)


def merge_block(nc, a, ps, chains, const, acc, o_all, scratch, w_o, h_dram, h1, h1_dram, logits):
    ctx = ExitStack()
    with ctx:
        sb = lambda n, s, d=F32: ctx.enter_context(nc.sbuf_tensor(n, s, d))
        sem = lambda n: ctx.enter_context(nc.semaphore(n))
        cg = sb("cg", [P, 2, NC4])
        w_r = sb("w_r", [P, KD, WR])
        g1 = sb("g1", [P, D])
        b1 = sb("b1", [P, D])
        sq = sb("sq", [P, 2, NC4, 512])
        rs = sb("rs", [P, 2, 512])
        rc = sb("rc", [P, NT])
        ra = sb("ra_o", [P, NT])
        oT = sb("oT", [P, 2, NC4, P])
        hT1 = sb("hT1", [P, KD, P])
        stats = sb("stats1", [P, 12])
        mv = sb("mv1", [P, 2])
        rstd = sb("rstd1", [P, 1])
        ident, ones = const[:, K_ID:K_ID + P], const[:, K_ONE:K_ONE + P]

        (sum_mm, centred, squared, var_mm, var_ev, rs_done, scaled, silu, c_sq, csum_mm, rc_ev, ra_done, rc_done, o_sq,
         oT_mm, oT_ev, yc_mm, ya_mm, res_done, ya_done, yc_done, stats_done, rstd_done, normed, gained, h1_done, hT_mm,
         hT_a, hT_d, lg_mm, lg_ev) = (sem("d_" + n) for n in
                                ("sum_mm", "centred", "squared", "var_mm", "var_ev", "rs", "scaled", "silu", "c_sq", "csum_mm",
                                 "rc_ev", "ra", "rc", "o_sq", "oT_mm", "oT_ev", "yc_mm", "ya_mm", "res", "ya", "yc", "stats",
                                 "rstd", "normed", "gained", "h1", "hT_mm", "hT_a", "hT_d", "lg_mm", "lg_ev"))
        w_in, cg_in, h1_out, padded = sem("d_w"), sem("d_cg"), sem("d_h1_out"), sem("d_padded")
        h_in = [sem(f"d_h_in{t}") for t in range(NT)]
        block = ctx.enter_context(nc.Block())
        token_halves = [slice(0, 512), slice(512, 1024)]

        @block.sync
        def _(sp):
            sp.dma_start(cg[:, :, :], a["conv_ln"]).then_inc(cg_in, 16)
            for t in range(NT):
                sp.dma_start(h1[:, t, :], h_dram[P * t:P * (t + 1), :]).then_inc(h_in[t], 16)
                if t == 1:
                    sp.wait_ge(padded, 1)
                    sp.dma_start(w_r[:, :, 0:G + E], a["w_r"]).then_inc(w_in, 16)
                    sp.dma_start(g1[:, :], a["ln1_g"].broadcast_to([P, D])).then_inc(w_in, 16)
                    sp.dma_start(b1[:, :], a["ln1_b"].broadcast_to([P, D])).then_inc(w_in, 16)
            for t in range(NT):
                sp.wait_ge(h1_done, t + 1)
                sp.dma_start(h1_dram[P * t:P * (t + 1), :], h1[:, t, :]).then_inc(h1_out, 16)
            sp.wait_ge(h1_out, 16 * NT)

        @block.gpsimd
        def _(pool):
            chain = chains["gpsimd"]
            pool.memset(w_r[:, :, :], 0.0).then_inc(padded, 1)
            for t in range(NT):
                pool.wait_ge(h_in[t], 16)
                pool.tensor_scalar(h1[:, t, :], h1[:, t, :], ALPHA, None, ALU.mult).then_inc(res_done, 1)
                if t == 0:
                    pool.wait_ge(o_sq, NT)
                    inverse_root(pool, chain, const, ra[:, :], ra[:, :], 1.0 / C).then_inc(ra_done, 1)
            pool.wait_ge(rc_ev, 1)
            inverse_root(pool, chain, const, rc[:, :], rc[:, :], 1.0 / C).then_inc(rc_done, 1)
            for t in range(NT):
                pool.wait_ge(stats_done, t + 1)
                inverse_root(pool, chain, const, rstd[:, :], mv[:, 1:2], 1.0).then_inc(rstd_done, 1)
                pool.wait_ge(gained, t + 1)
                pool.tensor_tensor(h1[:, t, :], h1[:, t, :], b1[:, :], ALU.add).then_inc(h1_done, 1)

        @block.vector
        def _(dve):
            chain = chains["vector"]

            def attention_part(t):
                if t == 0:
                    dve.wait_ge(ra_done, 1)
                dve.wait_ge(ya_mm, t + 1)
                dve.wait_ge(res_done, t + 1)
                nc.vector.scalar_tensor_tensor(h1[:, t, :], ps[:, 2 * (t % 2):2 * (t % 2) + 2, :].rearrange("p b n -> p (b n)"),
                                               ra[:, t:t + 1], h1[:, t, :], ALU.mult, ALU.add).then_inc(ya_done, 1)

            def normalise(n):
                dve.wait_ge(var_ev, n + 1)
                nc.vector.reciprocal(rs[:, n, :], rs[:, n, :]).then_inc(rs_done, 1)
                dve.wait_ge(rs_done, n + 1)
                for c in range(NC4):
                    nc.vector.tensor_tensor(acc[:, c, token_halves[n]], acc[:, c, token_halves[n]], rs[:, n, :], ALU.mult).then_inc(scaled, 1)

            for n in range(2):
                dve.wait_ge(sum_mm, n + 1)
                for c in range(NC4):
                    nc.vector.scalar_tensor_tensor(acc[:, c, token_halves[n]], ps[:, 6 + n, :], -1.0 / C, acc[:, c, token_halves[n]],
                                                   ALU.mult, ALU.add).then_inc(centred, 1)
            dve.wait_ge(centred, 2 * NC4)
            for t in range(NT):
                attention_part(t)
                if t < 2:
                    normalise(t)
                if t == 4:
                    dve.wait_ge(csum_mm, 1)
                    nc.vector.tensor_copy(rc[:, :], ps[:, 5, 0:NT]).then_inc(rc_ev, 1)

            def take_logits(t):
                dve.wait_ge(lg_mm, t + 1)
                nc.vector.tensor_copy(logits[:, t, :], ps[:, 7, 0:G + E]).then_inc(lg_ev, 1)

            dve.wait_ge(rc_done, 1)
            dve.wait_ge(w_in, 48)
            for t in range(NT + 1):
                if t < NT:
                    dve.wait_ge(yc_mm, t + 1)
                    dve.wait_ge(ya_done, NT)
                    nc.vector.scalar_tensor_tensor(h1[:, t, :], ps[:, 2 * (t % 2):2 * (t % 2) + 2, :].rearrange("p b n -> p (b n)"),
                                                   rc[:, t:t + 1], h1[:, t, :], ALU.mult, ALU.add).then_inc(yc_done, 1)
                    dve.wait_ge(yc_done, t + 1)
                    for b in range(2):
                        chain(nc.vector.bn_stats(stats[:, 6 * b:6 * b + 6], h1[:, t, 512 * b:512 * (b + 1)]))
                    nc.vector.bn_aggr(mv[:, :], stats[:, :]).then_inc(stats_done, 1)
                if t >= 2:
                    take_logits(t - 2)
                if t < NT:
                    dve.wait_ge(rstd_done, t + 1)
                    nc.vector.tensor_scalar(h1[:, t, :], h1[:, t, :], mv[:, 0:1], rstd[:, :], ALU.subtract, ALU.mult).then_inc(normed, 1)
                    dve.wait_ge(normed, t + 1)
                    nc.vector.tensor_tensor(h1[:, t, :], h1[:, t, :], g1[:, :], ALU.mult).then_inc(gained, 1)
                if t >= 1:
                    dve.wait_ge(hT_mm, t)
                    nc.vector.tensor_copy(hT1[:, 4:8, :].rearrange("p k t -> p (k t)"), ps[:, 5, :]).then_inc(hT_d, 1)
            take_logits(NT - 1)

        @block.scalar
        def _(act):
            def take_oT(t):
                act.wait_ge(oT_mm, t + 1)
                if t >= 2:
                    act.wait_ge(ya_mm, t - 1)
                nc.scalar.activation(oT[:, t % 2, :, :].rearrange("p k t -> p (k t)"), ps[:, 4, :], ACT.Copy).then_inc(oT_ev, 1)

            def shape(n):
                for c in range(NC4):
                    act.wait_ge(scaled, NC4 * n + c + 1)
                    nc.scalar.activation(acc[:, c, token_halves[n]], acc[:, c, token_halves[n]], ACT.Silu,
                                         scale=cg[:, 0, c:c + 1], bias=cg[:, 1, c:c + 1]).then_inc(silu, 1)
                for c in range(NC4):
                    act.wait_ge(silu, NC4 * n + c + 1)
                    nc.scalar.activation(sq[:, n, c, :], acc[:, c, token_halves[n]], ACT.Square).then_inc(c_sq, 1)

            for t in range(NT):
                nc.scalar.activation(scratch[:, t, :], o_all[:, t, :], ACT.Square, accum_out=ra[:, t:t + 1]).then_inc(o_sq, 1)
                if t < 2:
                    take_oT(t)
            for n in range(2):
                for c in range(NC4):
                    act.wait_ge(centred, NC4 * n + c + 1)
                    nc.scalar.activation(sq[:, n, c, :], acc[:, c, token_halves[n]], ACT.Square).then_inc(squared, 1)
            act.wait_ge(cg_in, 16)
            for n in range(2):
                act.wait_ge(var_mm, n + 1)
                nc.scalar.activation(rs[:, n, :], ps[:, 6 + n, :], ACT.Sqrt, scale=1.0 / C,
                                     bias=const[:, K_EPS:K_EPS + 1]).then_inc(var_ev, 1)
            take_oT(2)
            shape(0)
            take_oT(3)
            shape(1)
            for t in range(4, NT):
                take_oT(t)
            for t in range(NT):
                act.wait_ge(hT_mm, t + 1)
                nc.scalar.activation(hT1[:, 0:4, :].rearrange("p k t -> p (k t)"), ps[:, 4, :], ACT.Copy).then_inc(hT_a, 1)

        @block.tensor
        def _(pe):
            def turn_o(t):
                if t >= 1:
                    pe.wait_ge(oT_ev, t)
                for k in range(NC4):
                    last = nc.tensor.transpose(ps[:, 4, k * P:(k + 1) * P], o_all[:, t, k * P:(k + 1) * P], ident)
                last.then_inc(oT_mm, 1)

            def attention_part(t):
                pe.wait_ge(oT_ev, t + 1)
                if t >= 2:
                    pe.wait_ge(ya_done, t - 1)
                for b in range(2):
                    for k in range(NC4):
                        last = nc.tensor.matmul(ps[:, 2 * (t % 2) + b, :], oT[:, t % 2, k, :], w_o[:, NC4 + k, 512 * b:512 * (b + 1)],
                                                start=(k == 0), stop=(k == NC4 - 1))
                last.then_inc(ya_mm, 1)

            def conv_part(t):
                if t >= 2:
                    pe.wait_ge(yc_done, t - 1)
                else:
                    pe.wait_ge(ya_done, NT - 1 + t)
                for b in range(2):
                    for k in range(NC4):
                        last = nc.tensor.matmul(ps[:, 2 * (t % 2) + b, :], acc[:, k, P * t:P * (t + 1)], w_o[:, k, 512 * b:512 * (b + 1)],
                                                start=(k == 0), stop=(k == NC4 - 1))
                last.then_inc(yc_mm, 1)

            def router(t):
                pe.wait_ge(hT_a, t + 1)
                pe.wait_ge(hT_d, t + 1)
                if t >= 1:
                    pe.wait_ge(lg_ev, t)
                for k in range(KD):
                    last = nc.tensor.matmul(ps[:, 7, 0:WR], hT1[:, k, :], w_r[:, k, :], start=(k == 0), stop=(k == KD - 1))
                last.then_inc(lg_mm, 1)

            def turn_h(t):
                pe.wait_ge(h1_done, t + 1)
                for k in range(KD):
                    last = nc.tensor.transpose(ps[:, 4 + k // 4, (k % 4) * P:(k % 4 + 1) * P], h1[:, t, k * P:(k + 1) * P], ident)
                last.then_inc(hT_mm, 1)

            for n in range(2):
                for c in range(NC4):
                    last = nc.tensor.matmul(ps[:, 6 + n, :], ones, acc[:, c, token_halves[n]], start=(c == 0), stop=(c == NC4 - 1))
                last.then_inc(sum_mm, 1)
                turn_o(n)
            attention_part(0)
            pe.wait_ge(centred, 2 * NC4)
            for n in range(2):
                for c in range(NC4):
                    pe.wait_ge(squared, NC4 * n + c + 1)
                    last = nc.tensor.matmul(ps[:, 6 + n, :], ones, sq[:, n, c, :], start=(c == 0), stop=(c == NC4 - 1))
                last.then_inc(var_mm, 1)
            for t in range(1, NT):
                if t + 1 < NT:
                    turn_o(t + 1)
                attention_part(t)
                if t == 4:
                    pe.wait_ge(c_sq, 2 * NC4)
                    for j in range(NT):
                        for c in range(NC4):
                            last = nc.tensor.matmul(ps[:, 5, j:j + WR], sq[:, j // 4, c, P * (j % 4):P * (j % 4 + 1)], ones[:, 0:WR],
                                                    start=(c == 0), stop=(c == NC4 - 1))
                    last.then_inc(csum_mm, 1)
            pe.wait_ge(w_in, 48)
            pe.wait_ge(var_ev, 2)
            for t in range(NT + 2):
                if t < NT:
                    conv_part(t)
                if t >= 2:
                    router(t - 2)
                if t == 1:
                    pe.wait_ge(rc_ev, 1)
                    pe.wait_ge(oT_ev, NT)
                if 1 <= t <= NT:
                    turn_h(t - 1)


def route_block(nc, a, ps, chains, const, y_dram, logits, comb, dest, token_of, expert_of, n_blocks):
    ctx = ExitStack()
    with ctx:
        sb = lambda n, s, d=F32: ctx.enter_context(nc.sbuf_tensor(n, s, d))
        sem = lambda n: ctx.enter_context(nc.semaphore(n))
        rb = sb("rb_", [P, G + E])
        w1 = sb("w1", [P, NT])
        gmax = sb("gmax", [P, NT])
        keyg = sb("keyg", [P, NT, G])
        ohg = sb("ohg", [P, NT, G])
        expo = sb("expo", [P, NT, G + 1])
        gsum = sb("gsum", [P, NT])
        pick = sb("pick", [P, NT, G, EG])
        e_in = sb("e_in", [P, NT, EG])
        key = sb("key", [P, NT, EG])
        oh = sb("oh", [P, 2, NT, EG])
        v12 = sb("v12", [P, 2, NT])
        A = sb("A", [P, 2, NT, G, EG])
        M = sb("M", [P, NT, E])
        rank = sb("rank", [P, NT, E])
        base = sb("base", [P, NT + 1, E])
        over = sb("over", [P, E, 7])
        nover = sb("nover", [P, E])
        pre = sb("pre", [P, 2, E])
        excl = sb("excl", [P, E])
        tmp = sb("tmp", [P, NT, E])
        stat = sb("stat", [P, 3, NT])
        q7 = sb("q7", [P, NT, 7])
        qq = sb("qq", [P, NT])
        pp = sb("pp", [P, 2, NT])
        bb = sb("bb", [P, 2, NT])
        sel = sb("sel", [P, 2, P])
        blk = sb("blk", [P, 2, MAXB + 1])
        of = sb("of", [1, 16, E])
        of1 = sb("of1", [1, MAXB + 1])
        zeros = sb("zeros", [P, D])
        zeroed, zeros_out = sem("e_zeroed"), sem("e_zeros_out")

        bias_in, args, exps, mset, counted, made, used = (sem("e_" + n) for n in
            ("bias", "args", "exps", "M", "counted", "made", "used"))
        block = ctx.enter_context(nc.Block())
        io = lambda n: const[:, K_IOTA:K_IOTA + n]

        @block.sync
        def _(sp):
            sp.dma_start(rb[:, :], a["b_r"].broadcast_to([P, G + E])).then_inc(bias_in, 16)
            sp.wait_ge(bias_in, 16)
            sp.wait_ge(zeroed, 1)
            sp.dma_start(y_dram[E * P:MAXB * P, :].rearrange("(b p) d -> p b d", p=P),
                         zeros[:, :].unsqueeze(1).broadcast_to([P, MAXB - E, D])).then_inc(zeros_out, 16)
            sp.wait_ge(zeros_out, 16)

        @block.gpsimd
        def _(pool):
            pool.memset(zeros[:, :], 0.0).then_inc(zeroed, 1)

        @block.scalar
        def _(act):
            act.wait_ge(args, 2)
            nc.scalar.activation(expo[:, :, :], expo[:, :, :], ACT.Exp).then_inc(exps, 1)

        @block.tensor
        def _(pe):
            pe.wait_ge(mset, 1)
            flat = M[:, :, :].rearrange("p t e -> p (t e)")
            nc.tensor.matmul(ps[:, 0, 0:NT * E], const[:, K_TRI:K_TRI + P], flat, start=True, stop=True)
            nc.tensor.matmul(ps[:, 1, 0:NT * E], const[:, K_ONE:K_ONE + P], flat, start=True, stop=True).then_inc(counted, 1)
            for n in range(2 * NT):
                pe.wait_ge(made, n + 1)
                last = nc.tensor.matmul(ps[:, 2, 0:MAXB + 1], sel[:, n % 2, :], blk[:, n % 2, :], start=(n == 0), stop=(n == 2 * NT - 1))
                last.then_inc(used, 1)

        @block.vector
        def _(dve):
            v = nc.vector
            chain = chains["vector"]
            tt = lambda o, x, y, op: chain(v.tensor_tensor(o, x, y, op))
            one = lambda x, n: x.unsqueeze(len(x.shape)).broadcast_to(list(x.shape) + [n])
            dve.wait_ge(bias_in, 16)
            tt(logits[:, :, :], logits[:, :, :], rb[:, :].unsqueeze(1).broadcast_to([P, NT, G + E]), ALU.add)
            lg, le = logits[:, :, 0:G], logits[:, :, G:G + E].rearrange("p t (g e) -> p t g e", e=EG)

            def first_max(out_max, out_hot, x, keys, n):
                desc = const[:, K_DESC + EG - n:K_DESC + EG].unsqueeze(1).broadcast_to([P, NT, n])
                chain(v.reduce_max(out_max, x, AX.X))
                tt(keys, x, one(out_max, n), ALU.is_equal)
                tt(keys, keys, desc, ALU.mult)
                chain(v.reduce_max(w1[:, :], keys, AX.X))
                tt(out_hot, keys, one(w1[:, :], n), ALU.is_equal)

            first_max(gmax[:, :], ohg[:, :, :], lg, keyg[:, :, :], G)
            v.tensor_tensor(expo[:, :, 0:G], lg, one(gmax[:, :], G), ALU.subtract).then_inc(args, 1)
            tt(pick[:, :, :, :], le, one(ohg[:, :, :], EG), ALU.mult)
            chain(v.reduce_sum(e_in[:, :, :], pick[:, :, :, :].rearrange("p t g e -> p t e g"), AX.X))
            first_max(v12[:, 0, :], oh[:, 0, :, :], e_in[:, :, :], key[:, :, :], EG)
            chain(v.scalar_tensor_tensor(e_in[:, :, :], oh[:, 0, :, :], -1e30, e_in[:, :, :], ALU.mult, ALU.add))
            first_max(v12[:, 1, :], oh[:, 1, :, :], e_in[:, :, :], key[:, :, :], EG)
            v.tensor_tensor(expo[:, :, G], v12[:, 1, :], v12[:, 0, :], ALU.subtract).then_inc(args, 1)
            for j in range(2):
                for g in range(G):
                    tt(A[:, j, :, g, :], oh[:, j, :, :], ohg[:, :, g:g + 1].broadcast_to([P, NT, EG]), ALU.mult)
            Af = lambda j: A[:, j, :, :, :].rearrange("p t g e -> p t (g e)")
            v.tensor_tensor(M[:, :, :], Af(0), Af(1), ALU.add).then_inc(mset, 1)
            dve.wait_ge(exps, 1)
            chain(v.reduce_sum(gsum[:, :], expo[:, :, 0:G], AX.X))
            chain(v.tensor_scalar(qq[:, :], expo[:, :, G], 1.0, None, ALU.add))
            tt(gsum[:, :], gsum[:, :], qq[:, :], ALU.mult)
            chain(v.reciprocal(comb[:, 0, :], gsum[:, :]))
            tt(comb[:, 1, :], comb[:, 0, :], expo[:, :, G], ALU.mult)
            dve.wait_ge(counted, 1)
            chain(v.memset(base[:, 0, :], 0.0))
            for t in range(NT):
                tt(base[:, t + 1, :], base[:, t, :], ps[:, 1, E * t:E * (t + 1)], ALU.add)
            tt(rank[:, :, :], base[:, 0:NT, :], ps[:, 0, 0:NT * E].rearrange("p (t e) -> p t e", e=E), ALU.add)
            total = base[:, NT, :]
            chain(v.scalar_tensor_tensor(over[:, :, :], const[:, K_IOTA + 1:K_IOTA + 8].unsqueeze(1).broadcast_to([P, E, 7]), float(P),
                                         one(total, 7), ALU.mult, ALU.is_lt))
            chain(v.reduce_sum(nover[:, :], over[:, :, :], AX.X))
            cur = nover[:, :]
            step, n = 1, 0
            while step < E:
                nxt = pre[:, n % 2, :]
                chain(v.tensor_copy(nxt[:, 0:step], cur[:, 0:step]))
                tt(nxt[:, step:E], cur[:, step:E], cur[:, 0:E - step], ALU.add)
                cur, step, n = nxt, 2 * step, n + 1
            incl = cur
            tt(excl[:, :], incl, nover[:, :], ALU.subtract)
            for j in range(2):
                for m, table in enumerate((rank[:, :, :], excl[:, :].unsqueeze(1).broadcast_to([P, NT, E]),
                                           io(E).unsqueeze(1).broadcast_to([P, NT, E]))):
                    tt(tmp[:, :, :], Af(j), table, ALU.mult)
                    chain(v.reduce_sum(stat[:, m, :], tmp[:, :, :], AX.X))
                chain(v.scalar_tensor_tensor(q7[:, :, :], const[:, K_IOTA + 1:K_IOTA + 8].unsqueeze(1).broadcast_to([P, NT, 7]),
                                             float(P), one(stat[:, 0, :], 7), ALU.mult, ALU.is_le))
                chain(v.reduce_sum(qq[:, :], q7[:, :, :], AX.X))
                chain(v.scalar_tensor_tensor(pp[:, j, :], qq[:, :], -float(P), stat[:, 0, :], ALU.mult, ALU.add))
                tt(stat[:, 1, :], stat[:, 1, :], qq[:, :], ALU.add)
                tt(stat[:, 1, :], stat[:, 1, :], stat[:, 2, :], ALU.subtract)
                chain(v.tensor_scalar(qq[:, :], qq[:, :], 1.0, None, ALU.min))
                chain(v.scalar_tensor_tensor(stat[:, 1, :], stat[:, 1, :], float(E - 1), qq[:, :], ALU.add, ALU.mult))
                tt(bb[:, j, :], stat[:, 2, :], stat[:, 1, :], ALU.add)
                chain(v.scalar_tensor_tensor(dest[:, j, :], bb[:, j, :], float(P), pp[:, j, :], ALU.mult, ALU.add))
            for n in range(2 * NT):
                j, t = n // NT, n % NT
                if n >= 2:
                    dve.wait_ge(used, n - 1)
                v.tensor_scalar(sel[:, n % 2, :], io(P), pp[:, j, t:t + 1], None, ALU.is_equal)
                v.tensor_scalar(blk[:, n % 2, :], io(MAXB + 1), bb[:, j, t:t + 1], const[:, K_TOK + t:K_TOK + t + 1],
                                ALU.is_equal, ALU.mult).then_inc(made, 1)
            chain(v.tensor_copy(of1[0:1, 0:E], const[0:1, K_IOTA:K_IOTA + E]))
            tt(of[0:1, :, :], incl[0:1, :].unsqueeze(1).broadcast_to([1, 16, E]),
               const[0:1, K_IOTA:K_IOTA + 16].unsqueeze(2).broadcast_to([1, 16, E]), ALU.is_le)
            chain(v.reduce_sum(of1[0:1, E:E + 16], of[0:1, :, :], AX.X))
            chain(v.tensor_scalar(expert_of[0:1, :], of1[0:1, :], float(E - 1), None, ALU.min))
            chain(v.tensor_scalar(n_blocks[0:1, 0:1], incl[0:1, E - 1:E], float(E - 2), None, ALU.add))
            dve.wait_ge(used, 2 * NT)
            chain(v.tensor_copy(token_of[:, :], ps[:, 2, 0:MAXB + 1]))


def expert_block(nc, a, ps, chains, const, h1_dram, y_dram, token_of, expert_of, n_blocks):
    ctx = ExitStack()
    with ctx:
        sb = lambda n, s, d=F32: ctx.enter_context(nc.sbuf_tensor(n, s, d))
        sem = lambda n: ctx.enter_context(nc.semaphore(n))
        gu_w = sb("gu_w", [P, RING * WGU])
        dn_w = sb("dn_w", [P, RING * WDN])
        x = sb("x_rows", [P, D])
        xT = sb("xT", [P, KD, P])
        sg = sb("sg_e", [P, F])
        hh = sb("hh", [P, F])
        hT = sb("hT_e", [P, 2, P])
        y = sb("y_rows", [P, D])
        ident = const[:, K_ID:K_ID + P]
        (gu_in, dn_in, x_in, y_out, tx_mm, xT_a, xT_d, gu_mm, sg_done, hh_done, th_mm, hT_ev, dn_mm, y_a, y_d) = (
            sem("f_" + n) for n in ("gu_in", "dn_in", "x_in", "y_out", "tx_mm", "xT_a", "xT_d", "gu_mm", "sg", "hh", "th_mm",
                                    "hT_ev", "dn_mm", "y_a", "y_d"))
        block = ctx.enter_context(nc.Block())
        ds = bass.ds
        blocks = lambda eng: eng.value_load(n_blocks[0:1, 0:1], min_val=E - 2, max_val=MAXB - 2)

        @block.sync
        def _(sp):
            m = blocks(sp)

            def load(e, at):
                sp.dma_start(gu_w[:, ds(at, WGU)], a["w_gate_up"][ds(e, 1), :, :].rearrange("a p n -> p (a n)")).then_inc(gu_in, 16)

            def load_down(e, at):
                sp.dma_start(dn_w[:, ds(at, WDN)], a["w_down_t"][ds(e, 1), :, :].rearrange("a p n -> p (a n)")).then_inc(dn_in, 16)

            for b in range(RING):
                if b:
                    sp.wait_ge(gu_in, 16 * b)
                load(b, b * WGU)
                if b:
                    sp.wait_ge(dn_in, 16 * b)
                load_down(b, b * WDN)
            with sp.Fori(1, m + 2 - (RING - 1)) as used:
                b = used + (RING - 1)
                e = sp.value_load(expert_of[0:1, ds(b, 1)], min_val=0, max_val=E - 1)
                slot = sp.snap(b % RING)
                sp.wait_ge(gu_in, b * 16)
                sp.wait_ge(gu_mm, used)
                load(e, slot * WGU)
                sp.wait_ge(dn_in, b * 16)
                sp.wait_ge(dn_mm, used)
                load_down(e, slot * WDN)

        @block.gpsimd
        def _(pool):
            m = blocks(pool)

            def gather(b):
                if b:
                    pool.wait_ge(tx_mm, b)
                pool.indirect_dma_start(out=x[:, :], out_offset=None, in_=h1_dram,
                                        in_offset=bass.IndirectOffsetOnAxis(ap=token_of[:, b:b + 1], axis=0)).then_inc(x_in, 16)

            for b in range(E):
                gather(b)
            for b in range(E, MAXB):
                with pool.If(m > b - 2):
                    gather(b)
            pool.wait_ge(y_out, m * 16 + 32)

        @block.scalar
        def _(act):
            m = blocks(act)

            def x_part(b):
                act.wait_ge(tx_mm, b + 1)
                nc.scalar.activation(xT[:, 0:4, :].rearrange("p k t -> p (k t)"), ps[:, 1, :], ACT.Copy).then_inc(xT_a, 1)

            def h_part(b):
                act.wait_ge(th_mm, b + 1)
                nc.scalar.activation(hT[:, :, :].rearrange("p k t -> p (k t)"), ps[:, 3, 0:2 * P], ACT.Copy).then_inc(hT_ev, 1)

            def y_part(b, first):
                act.wait_ge(dn_mm, b + 1)
                if not first:
                    act.wait_ge(y_out, b * 16)
                nc.scalar.activation(y[:, 0:512], ps[:, 4, :], ACT.Copy).then_inc(y_a, 1)
                act.wait_ge(y_a, b + 1)
                act.wait_ge(y_d, b + 1)
                act.dma_start(y_dram[ds(b * P, P), :], y[:, :]).then_inc(y_out, 16)

            def silu(b):
                act.wait_ge(gu_mm, b + 1)
                nc.scalar.activation(sg[:, :], ps[:, 0, 0:F], ACT.Silu).then_inc(sg_done, 1)

            x_part(0)
            silu(0)
            x_part(1)
            h_part(0)
            act.wait_ge(hh_done, 1)
            silu(1)
            x_part(2)
            y_part(0, True)
            h_part(1)
            act.wait_ge(hh_done, 2)
            silu(2)
            with act.Fori(3, m + 2) as b:
                x_part(b)
                y_part(b - 2, False)
                h_part(b - 1)
                act.wait_ge(hh_done, b)
                silu(b)
            y_part(m, False)
            h_part(m + 1)
            y_part(m + 1, False)

        @block.vector
        def _(dve):
            m = blocks(dve)

            def x_part(b):
                dve.wait_ge(tx_mm, b + 1)
                nc.vector.tensor_copy(xT[:, 4:8, :].rearrange("p k t -> p (k t)"), ps[:, 2, :]).then_inc(xT_d, 1)

            def y_part(b, first):
                dve.wait_ge(dn_mm, b + 1)
                if not first:
                    dve.wait_ge(y_out, b * 16)
                nc.vector.tensor_copy(y[:, 512:1024], ps[:, 5, :]).then_inc(y_d, 1)

            def hidden(b, first):
                dve.wait_ge(sg_done, b + 1)
                if not first:
                    dve.wait_ge(th_mm, b)
                nc.vector.tensor_tensor(hh[:, :], sg[:, :], ps[:, 0, F:2 * F], ALU.mult).then_inc(hh_done, 1)

            x_part(0)
            hidden(0, True)
            x_part(1)
            hidden(1, False)
            x_part(2)
            y_part(0, True)
            hidden(2, False)
            with dve.Fori(3, m + 2) as b:
                x_part(b)
                y_part(b - 2, False)
                hidden(b, False)
            y_part(m, False)
            y_part(m + 1, False)

        @block.tensor
        def _(pe):
            m = blocks(pe)

            def turn_x(b):
                pe.wait_ge(x_in, b * 16 + 16)
                for k in range(KD):
                    last = nc.tensor.transpose(ps[:, 1 + k // 4, (k % 4) * P:(k % 4 + 1) * P], x[:, k * P:(k + 1) * P], ident)
                last.then_inc(tx_mm, 1)

            def gate_up(b, slot, first):
                pe.wait_ge(gu_in, b * 16 + 16)
                pe.wait_ge(xT_a, b + 1)
                pe.wait_ge(xT_d, b + 1)
                if not first:
                    pe.wait_ge(hh_done, b)
                for k in range(KD):
                    last = nc.tensor.matmul(ps[:, 0, :], xT[:, k, :], gu_w[:, ds(slot * WGU + k * 2 * F, 2 * F)],
                                            start=(k == 0), stop=(k == KD - 1))
                last.then_inc(gu_mm, 1)

            def turn_h(b):
                pe.wait_ge(hh_done, b + 1)
                for k in range(2):
                    last = nc.tensor.transpose(ps[:, 3, k * P:(k + 1) * P], hh[:, k * P:(k + 1) * P], ident)
                last.then_inc(th_mm, 1)

            def down(b, slot, first):
                pe.wait_ge(dn_in, b * 16 + 16)
                pe.wait_ge(hT_ev, b + 1)
                if not first:
                    pe.wait_ge(y_a, b)
                    pe.wait_ge(y_d, b)
                for half in range(2):
                    for k in range(2):
                        last = nc.tensor.matmul(ps[:, 4 + half, :], hT[:, k, :], dn_w[:, ds(slot * WDN + k * D + 512 * half, 512)],
                                                start=(k == 0), stop=(k == 1))
                last.then_inc(dn_mm, 1)

            turn_x(0)
            gate_up(0, 0, True)
            turn_x(1)
            turn_h(0)
            gate_up(1, 1, False)
            turn_x(2)
            down(0, 0, True)
            turn_h(1)
            gate_up(2, 2, False)
            with pe.Fori(3, m + 2) as b:
                turn_x(b)
                down(b - 2, (b - 2) % RING, False)
                turn_h(b - 1)
                gate_up(b, b % RING, False)
            down(m, m % RING, False)
            turn_h(m + 1)
            down(m + 1, (m + 1) % RING, False)


def final_block(nc, a, ps, chains, const, h1, y_dram, comb, dest, out):
    ctx = ExitStack()
    with ctx:
        sb = lambda n, s, d=F32: ctx.enter_context(nc.sbuf_tensor(n, s, d))
        sem = lambda n: ctx.enter_context(nc.semaphore(n))
        g2 = sb("g2", [P, D])
        b2 = sb("b2", [P, D])
        yy = sb("yy", [P, NT, 2, D])
        stats = sb("stats2", [P, 12])
        mv = sb("mv2", [P, 2])
        rstd = sb("rstd2", [P, 1])
        g_in, stats_done, rstd_done, gained, done, out_s, ah = (sem("g_" + n) for n in
            ("g_in", "stats", "rstd", "gained", "done", "out", "ah"))
        y_in = [sem(f"g_y{t}") for t in range(NT)]
        block = ctx.enter_context(nc.Block())

        @block.sync
        def _(sp):
            sp.dma_start(g2[:, :], a["ln2_g"].broadcast_to([P, D])).then_inc(g_in, 16)
            sp.dma_start(b2[:, :], a["ln2_b"].broadcast_to([P, D])).then_inc(g_in, 16)
            for t in range(NT):
                sp.wait_ge(done, t + 1)
                sp.dma_start(out[0, P * t:P * (t + 1), :], h1[:, t, :]).then_inc(out_s, 16)
            sp.wait_ge(out_s, 16 * NT)

        @block.gpsimd
        def _(pool):
            for t in range(NT):
                for j in range(2):
                    pool.indirect_dma_start(out=yy[:, t, j, :], out_offset=None, in_=y_dram,
                                            in_offset=bass.IndirectOffsetOnAxis(ap=dest[:, j, t:t + 1], axis=0)).then_inc(y_in[t], 16)
            chain = chains["gpsimd"]
            pool.wait_ge(g_in, 32)
            for t in range(NT):
                pool.wait_ge(stats_done, t + 1)
                inverse_root(pool, chain, const, rstd[:, :], mv[:, 1:2], 1.0).then_inc(rstd_done, 1)
                pool.wait_ge(gained, t + 1)
                pool.tensor_tensor(h1[:, t, :], h1[:, t, :], b2[:, :], ALU.add).then_inc(done, 1)

        @block.scalar
        def _(act):
            for t in range(NT):
                nc.scalar.activation(h1[:, t, :], h1[:, t, :], ACT.Copy, scale=ALPHA).then_inc(ah, 1)

        @block.vector
        def _(dve):
            v = nc.vector
            chain = chains["vector"]
            dve.wait_ge(g_in, 32)
            for t in range(NT):
                dve.wait_ge(y_in[t], 32)
                dve.wait_ge(ah, t + 1)
                chain(v.scalar_tensor_tensor(h1[:, t, :], yy[:, t, 0, :], comb[:, 0, t:t + 1], h1[:, t, :], ALU.mult, ALU.add))
                chain(v.scalar_tensor_tensor(h1[:, t, :], yy[:, t, 1, :], comb[:, 1, t:t + 1], h1[:, t, :], ALU.mult, ALU.add))
                for b in range(2):
                    chain(v.bn_stats(stats[:, 6 * b:6 * b + 6], h1[:, t, 512 * b:512 * (b + 1)]))
                v.bn_aggr(mv[:, :], stats[:, :]).then_inc(stats_done, 1)
                dve.wait_ge(rstd_done, t + 1)
                chain(v.tensor_scalar(h1[:, t, :], h1[:, t, :], mv[:, 0:1], rstd[:, :], ALU.subtract, ALU.mult))
                v.tensor_tensor(h1[:, t, :], h1[:, t, :], g2[:, :], ALU.mult).then_inc(gained, 1)


def program(nc, a, out):
    h_dram = nc.dram_tensor("h_dram", [T, D], F32, kind="Internal").ap()
    h1_dram = nc.dram_tensor("h1_dram", [T, D], F32, kind="Internal").ap()
    y_dram = nc.dram_tensor("y_dram", [MAXB * P, D], F32, kind="Internal").ap()
    ps = nc.alloc_psum_tensor("ps", [P, 8, 512], F32)
    chains = {"vector": Chain(nc.vector, nc.alloc_semaphore("vector_link")), "gpsimd": Chain(nc.gpsimd, nc.alloc_semaphore("gpsimd_link"))}
    with (nc.sbuf_tensor("const", [P, K_END], F32) as const, nc.sbuf_tensor("logits", [P, NT, G + E], F32) as logits,
          nc.sbuf_tensor("h1", [P, NT, D], F32) as h1):
        early, at = h1[:, :, :].rearrange("p t d -> p (t d)"), 0

        def piece(*dims):
            nonlocal at
            size = int(np.prod(dims))
            v = early[:, at:at + size]
            at += size
            if len(dims) == 2:
                v = v.rearrange("p (a b) -> p a b", a=dims[0])
            return v

        u, cw, v_meta = piece(NC4, UW), piece(NC4, TAPS + 1), piece(H * VD)
        z, zT, q_t, k_t = piece(ZR), piece(5, P), piece(H, QK), piece(H, QK)
        assert at <= NT * D
        with nc.sbuf_tensor("acc", [P, NC4, T], F32) as acc, nc.sbuf_tensor("hT", [P, KD, META + T], F32) as hT:
            flat = hT[:, :, :].rearrange("p k t -> p (k t)")
            o_all = flat[:, 0:NT * C].rearrange("p (t c) -> p t c", c=C)
            p = flat[:, NT * C:NT * C + 2 * T].rearrange("p (b n) -> p b n", b=2)
            pT = flat[:, NT * C + 2 * T:NT * C + 4 * T].rearrange("p (b k n) -> p b k n", b=2, n=P)
            scratch = flat[:, NT * C:2 * NT * C].rearrange("p (t c) -> p t c", c=C)
            input_block(nc, a, ps, chains, const, hT, u, acc, cw, h_dram)
            with nc.sbuf_tensor("wo", [P, KD, D], F32) as w_o, nc.sbuf_tensor("g_o", [P, KD], F32) as g_o:
                with (nc.sbuf_tensor("qT", [QK + 1, H, T], F32) as qT, nc.sbuf_tensor("kT", [QK + 1, H, META + T], F32) as kT,
                      nc.sbuf_tensor("v_all", [P, NT + 1, H * VD], F32) as v_all):
                    w_z_q = w_o[:, :, :].rearrange("p k d -> p (k d)")
                    mixer_block(nc, a, ps, chains, const, hT, u, acc, cw, qT, kT, v_all, v_meta, z, zT, q_t, k_t, w_z_q)
                    attention_block(nc, a, ps, chains, const, u, acc, cw, qT, kT, v_all, v_meta, o_all, p, pT, w_o, g_o)
                merge_block(nc, a, ps, chains, const, acc, o_all, scratch, w_o, h_dram, h1, h1_dram, logits)
        with (nc.sbuf_tensor("comb", [P, 2, NT], F32) as comb,
              nc.sbuf_tensor("dest", [P, 2, NT], I32) as dest, nc.sbuf_tensor("token_of", [P, MAXB + 1], I32) as token_of,
              nc.sbuf_tensor("expert_of", [1, MAXB + 1], I32) as expert_of, nc.sbuf_tensor("n_blocks", [1, 1], I32) as n_blocks):
            route_block(nc, a, ps, chains, const, y_dram, logits, comb, dest, token_of, expert_of, n_blocks)
            expert_block(nc, a, ps, chains, const, h1_dram, y_dram, token_of, expert_of, n_blocks)
            final_block(nc, a, ps, chains, const, h1, y_dram, comb, dest, out)


def kernel(**inputs):
    import numpy as _np
    import concourse.bacc as _bacc
    from concourse import mybir as _mybir
    from concourse.bass_utils import run_bass_kernel_spmd as _run

    i = {k: _np.asarray(v) for k, v in inputs.items()}
    tile = lambda w: w.reshape(w.shape[0] // P, P, -1).transpose(1, 0, 2)
    w_in = i["w_in"][0]
    conv = tile(w_in[:, :2 * C]).reshape(P, KD, 2, NC4, P).transpose(0, 3, 1, 2, 4).reshape(P, NC4, KD * 2 * P)
    kv = i["w_ukv"][0].reshape(KVL, H, 2, NOPE).transpose(0, 2, 1, 3).reshape(KVL, 2 * H * NOPE)
    experts = lambda w: w.reshape(E, w.shape[1] // P, P, w.shape[2]).transpose(0, 2, 1, 3)
    arrays = {
        "x": i["x"], "meta_tokens": i["meta_tokens"], "ln_in_g": i["ln_in_g"], "ln_in_b": i["ln_in_b"],
        "ln1_g": i["ln1_g"], "ln1_b": i["ln1_b"], "ln2_g": i["ln2_g"], "ln2_b": i["ln2_b"],
        "consts": constants(),
        "w_conv_in": conv,
        "w_z": tile(w_in[:, 2 * C:]),
        "w_q": tile(i["w_uq"][0]),
        "w_kv": tile(kv),
        "qkv_g": _np.concatenate([i["q_norm_g"][0].reshape(3, P).T, i["kv_norm_g"][0].reshape(2, P).T], 1),
        "conv_wb": _np.concatenate([i["conv_w"][0].reshape(TAPS, NC4, P), i["conv_b"][0].reshape(1, NC4, P)]).transpose(2, 1, 0),
        "conv_ln": _np.stack([i["conv_ln_g"][0].reshape(NC4, P), i["conv_ln_b"][0].reshape(NC4, P)]).transpose(2, 0, 1),
        "out_g": _np.concatenate([i["conv_out_g"][0], i["attn_out_g"][0]]).reshape(KD, P).T,
        "w_o": tile(i["w_o"][0]),
        "w_r": tile(_np.concatenate([i["w_rg"][0], i["w_re"][0]], 1)),
        "b_r": _np.concatenate([i["b_rg"], i["b_re"]], 1),
        "w_gate_up": _np.concatenate([experts(i["w_gate"][0]), experts(i["w_up"][0])], 3).reshape(E, P, WGU),
        "w_down_t": experts(i["w_down"][0]).reshape(E, P, WDN),
    }
    arrays = {k + "_in": _np.ascontiguousarray(v) for k, v in arrays.items()}
    nc = _bacc.Bacc("TRN2", target_bir_lowering=False, num_devices=1)
    aps = {k[:-3]: nc.dram_tensor(k, v.shape, _mybir.dt.from_np(v.dtype), kind="ExternalInput").ap() for k, v in arrays.items()}
    out = nc.dram_tensor("out_0", (1, T, D), _mybir.dt.float32, kind="ExternalOutput").ap()
    program(nc, aps, out)
    r = _run(nc, [arrays], core_ids=[0])
    return r.results[0]["out_0"]
```

```python
import concourse.bass as bass
from concourse import mybir
from contextlib import ExitStack
import numpy as np

F32 = mybir.dt.float32
F32R = mybir.dt.float32r
I32 = mybir.dt.int32
ALU = mybir.AluOpType
ACT = mybir.ActivationFunctionType
AX = mybir.AxisListType

P = 128
D = 1024
T = 1024
NT = T // P
META = 16
KD = D // P
C = 512
NC4 = C // P
TAPS = 31
CHUNK = 64
H = 8
NOPE, ROPE, VD = 64, 32, 64
QK = NOPE + ROPE
QL, KVL = 384, 256
ZR = QL + KVL + ROPE
G, EG, E = 4, 8, 32
F = 256
MAXB = E + 2 * T // P - 1
ALPHA = float(np.float32(2.0 ** 0.25))
EPS = 1e-5
NEG_INF = -1e30
PAD = TAPS - 1 - META
UW = PAD + META + T
WGU, WDN = KD * 2 * F, (F // P) * D
WE = WGU + WDN
WR = 96
RING = 4

CUTS = [0, META + 3 * P, META + 6 * P, META + T]
CHUNK_TAPS = [(n, c, k) for n in range(3) for c in range(2) for k in range(TAPS)]
EARLY_TAPS = 160

K_ID = 0
K_TRI = K_ID + P
K_ONE = K_TRI + P
K_COS = K_ONE + P
K_SIN = K_COS + (NT + 1) * ROPE
K_IOTA = K_SIN + (NT + 1) * ROPE
K_ROW = K_IOTA + P
K_DESC = K_ROW + 2 * NT
K_MH = K_DESC + EG
K_EPS = K_MH + NT
K_END = K_EPS + 1


def constants():
    t = np.zeros((P, K_END), np.float32)
    t[:, K_ID:K_ID + P] = np.eye(P)
    t[:, K_TRI:K_TRI + P] = np.triu(np.ones((P, P)), 1)
    t[:, K_ONE:K_ONE + P] = 1.0
    half = ROPE // 2
    freq = (np.float32(10000.0) ** (-np.arange(half, dtype=np.float32) / np.float32(half))).astype(np.float32)
    ang = np.arange(META + T, dtype=np.float32)[:, None] * freq[None, :]
    for name, f in ((K_COS, np.cos), (K_SIN, np.sin)):
        v = f(ang).astype(np.float32)
        v = np.concatenate([v, v], 1)
        t[:META, name:name + ROPE] = v[:META]
        t[:, name + ROPE:name + (NT + 1) * ROPE] = v[META:].reshape(NT, P, ROPE).transpose(1, 0, 2).reshape(P, -1)
    t[:, K_IOTA:K_IOTA + P] = np.arange(P)
    t[:, K_ROW:K_ROW + 2 * NT] = 1 + np.arange(2 * T).reshape(2 * NT, P).T
    t[:, K_DESC:K_DESC + EG] = np.arange(EG, 0, -1)
    t[:, K_MH:K_MH + NT] = -0.5
    t[:, K_EPS] = EPS
    return t


def split_product(nc, out, pairs, start=True):
    terms = [(x[i], w[j]) for x, w in pairs for i, j in ((0, 0), (0, 1), (1, 0))]
    for n, (x, w) in enumerate(terms):
        last = nc.tensor.matmul(out, x, w, start=(start and n == 0), stop=(n == len(terms) - 1))
    return last


class Chain:

    def __init__(self, engine, semaphore):
        self.engine, self.semaphore, self.count = engine, semaphore, 0

    def __call__(self, instruction):
        self.count += 1
        instruction.then_inc(self.semaphore, 1)
        self.engine.wait_ge(self.semaphore, self.count)


def inverse_root(pool, chain, const, out, var, scale):
    r, n = out.shape
    chain(pool.tensor_scalar(out, var, scale, EPS, ALU.mult, ALU.add))
    return pool.tensor_tensor(out, out, const[:r, K_MH:K_MH + n], ALU.pow)


def rows(t):
    return META if t == 0 else P


def col(t):
    return 0 if t == 0 else META + P * (t - 1)


def chunk_tap(nc, chain, u, acc, cw, n, c, k):
    lo = max(CUTS[n] - META, 0)
    tap(nc, chain, u, acc, cw, c, k, lo, CUTS[n + 1] - META - lo)


def tap(nc, chain, u, acc, cw, c, k, lo=0, n=T):
    out, shifted = acc[:, c, lo:lo + n], u[:, c, lo + k:lo + k + n]
    if k == 0:
        chain(nc.vector.tensor_scalar(out, shifted, cw[:, c, 0:1], cw[:, c, TAPS:TAPS + 1], ALU.mult, ALU.add))
    else:
        chain(nc.vector.scalar_tensor_tensor(out, shifted, cw[:, c, k:k + 1], out, ALU.mult, ALU.add))


def input_block(nc, a, ps, chains, const, hT, u, acc, cw, h_dram, early, w_z, w_q, w_kv0, qg):
    ctx = ExitStack()
    with ctx:
        sb = lambda n, s, d=F32: ctx.enter_context(nc.sbuf_tensor(n, s, d))
        sem = lambda n: ctx.enter_context(nc.semaphore(n))
        NS, NB = NT + 1, 4
        x_t = early[:, 0:NB * D].rearrange("p (b d) -> p b d", d=D)
        g_in, b_in = early[:, NB * D:(NB + 1) * D], early[:, (NB + 1) * D:(NB + 2) * D]
        h_t = sb("h_t", [P, NB, D])
        w_c = sb("w_c", [P, NC4, KD * 2 * P])
        sg = sb("sg", [P, 2, 512])
        stats = sb("stats", [P, 2, 12])
        mv = sb("mv", [P, NS, 2])
        rstd = sb("rstd", [P, NS, 1])
        ident = const[:, K_ID:K_ID + P]

        consts_in, gb_in, cw_in, w_in = sem("a_consts_in"), sem("a_gb_in"), sem("a_cw_in"), [sem(f"a_w_in{c}") for c in range(NC4)]
        x_in = [sem(f"a_x_in{b}") for b in range(NB)]
        stats_done, rstd_done, normed, scaled, h_done = (sem("a_" + n) for n in ("stats", "rstd", "normed", "scaled", "h"))
        h_out = [sem(f"a_h_out{b}") for b in range(NB)]
        transposed, hT_act, hT_dve = (sem("a_" + n) for n in ("transposed", "hT_act", "hT_dve"))
        gate_done, sig_done, u_done = (sem("a_" + n) for n in ("gate", "sig", "u"))
        next_in = sem("a_next_in")
        block = ctx.enter_context(nc.Block())
        units = [(n, c) for n in range(3) for c in range(NC4)]
        NU = len(units)

        @block.sync
        def _(sp):
            def load(t):
                if t >= NB:
                    sp.wait_ge(normed, t - NB + 1)
                src = a["meta_tokens"] if t == 0 else a["x"][0, P * (t - 1):P * t, :]
                sp.dma_start(x_t[:rows(t), t % NB, :], src).then_inc(x_in[t % NB], 16)

            def store(t):
                sp.wait_ge(h_done, t + 1)
                sp.dma_start(h_dram[P * (t - 1):P * t, :], h_t[:, t % NB, :]).then_inc(h_out[t % NB], 16)

            load(0)
            load(1)
            sp.dma_start(const[:, :], a["consts"]).then_inc(consts_in, 16)
            sp.dma_start(g_in[:, :], a["ln_in_g"].rearrange("(a n) -> a n", a=1).broadcast_to([P, D])).then_inc(gb_in, 16)
            sp.dma_start(b_in[:, :], a["ln_in_b"].rearrange("(a n) -> a n", a=1).broadcast_to([P, D])).then_inc(gb_in, 16)
            for t in range(2, NS):
                load(t)
                if t == 4:
                    for c in range(NC4):
                        sp.dma_start(w_c[:, c, :], a["w_conv_in"][:, c, :]).then_inc(w_in[c], 16)
                    sp.dma_start(cw[:, :, :], a["conv_wb"]).then_inc(cw_in, 16)
                if t > NB:
                    store(t - NB)
            sp.wait_ge(normed, NS)
            sp.wait_ge(h_done, NS)
            sp.dma_start(w_z, a["w_z"]).then_inc(next_in, 16)
            sp.dma_start(w_q, a["w_q"]).then_inc(next_in, 16)
            sp.dma_start(w_kv0, a["w_kv"][:, 0, :]).then_inc(next_in, 16)
            sp.dma_start(qg, a["qkv_g"]).then_inc(next_in, 16)
            for t in range(NS - NB, NS):
                store(t)
            for b in range(NB):
                sp.wait_ge(h_out[b], 16 * (NT // NB))

        def add_bias(pool, t):
            r = rows(t)
            pool.wait_ge(scaled, t + 1)
            pool.tensor_tensor(h_t[:r, t % NB, :], h_t[:r, t % NB, :], b_in[:r, :], ALU.add).then_inc(h_done, 1)

        @block.gpsimd
        def _(pool):
            chain = chains["gpsimd"]
            pool.memset(u[:, :, 0:PAD], 0.0)
            pool.wait_ge(consts_in, 16)
            for t in range(NS):
                r = rows(t)
                pool.wait_ge(stats_done, t + 1)
                inverse_root(pool, chain, const, rstd[:r, t, :], mv[:r, t, 1:2], 1.0).then_inc(rstd_done, 1)
                if t >= 1:
                    add_bias(pool, t - 1)
            add_bias(pool, NS - 1)
            pool.wait_ge(next_in, 64)
            for k in range(3):
                pool.tensor_scalar(w_q[:, k, :], w_q[:, k, :], qg[:, k:k + 1], None, ALU.mult)
            pool.tensor_scalar(w_kv0, w_kv0, qg[:, 3:4], None, ALU.mult)

        def take(eng, ns, t, half, done):
            r = rows(t)
            eng.wait_ge(transposed, t + 1)
            src = ps[:, half, :].rearrange("p (k t) -> p k t", t=P)[:, :, 0:r]
            dst = hT[:, 4 * half:4 * half + 4, col(t):col(t) + r]
            if half:
                ns.tensor_copy(dst, src).then_inc(done, 1)
            else:
                ns.activation(dst, src, ACT.Copy).then_inc(done, 1)

        @block.vector
        def _(dve):
            chain = chains["vector"]

            def statistics(t):
                r = rows(t)
                dve.wait_ge(x_in[t % NB], 16 * (t // NB + 1))
                if t >= 2:
                    dve.wait_ge(stats_done, t - 1)
                nc.vector.bn_stats(stats[:r, t % 2, 0:6], x_t[:r, t % NB, 0:512])
                chain(nc.vector.bn_stats(stats[:r, t % 2, 6:12], x_t[:r, t % NB, 512:1024]))
                nc.vector.bn_aggr(mv[:r, t, :], stats[:r, t % 2, :]).then_inc(stats_done, 1)

            def gated(j):
                n, c = units[j]
                lo, hi = CUTS[n], CUTS[n + 1]
                dve.wait_ge(sig_done, j + 1)
                nc.vector.tensor_tensor(u[:, c, PAD + lo:PAD + hi], ps[:, 2 + 2 * (j % 2), 0:hi - lo], sg[:, j % 2, 0:hi - lo],
                                        ALU.mult).then_inc(u_done, 1)

            statistics(0)
            for t in range(NS):
                r = rows(t)
                if t + 1 < NS:
                    statistics(t + 1)
                dve.wait_ge(rstd_done, t + 1)
                if t >= NB:
                    if t > NB:
                        dve.wait_ge(h_out[t % NB], 16 * ((t - 1) // NB))
                    dve.wait_ge(transposed, t - NB + 1)
                nc.vector.tensor_scalar(h_t[:r, t % NB, :], x_t[:r, t % NB, :], mv[:r, t, 0:1], rstd[:r, t, :],
                                        ALU.subtract, ALU.mult).then_inc(normed, 1)
                if t == 0:
                    dve.wait_ge(gb_in, 32)
                dve.wait_ge(normed, t + 1)
                nc.vector.tensor_tensor(h_t[:r, t % NB, :], h_t[:r, t % NB, :], g_in[:r, :], ALU.mult).then_inc(scaled, 1)
                if 1 <= t <= 4:
                    take(dve, nc.vector, t - 1, 1, hT_dve)
            done = 0
            for j, (n, _) in enumerate(units):
                gated(j)
                if j < 5:
                    take(dve, nc.vector, 4 + j, 1, hT_dve)
                if j == 0:
                    dve.wait_ge(cw_in, 16)
                dve.wait_ge(u_done, j + 1)
                ready = sum(m[0:2] in units[:j + 1] for m in CHUNK_TAPS)
                upto = min(ready, done + (16 if n < 2 else 12), EARLY_TAPS)
                while done < upto:
                    chunk_tap(nc, chain, u, acc, cw, *CHUNK_TAPS[done])
                    done += 1
            assert done == EARLY_TAPS

        @block.scalar
        def _(act):
            def sigmoid(j):
                act.wait_ge(gate_done, j + 1)
                if j >= 2:
                    act.wait_ge(u_done, j - 1)
                n = CUTS[units[j][0] + 1] - CUTS[units[j][0]]
                nc.scalar.activation(sg[:, j % 2, 0:n], ps[:, 3 + 2 * (j % 2), 0:n], ACT.Sigmoid).then_inc(sig_done, 1)

            for t in range(4):
                take(act, nc.scalar, t, 0, hT_act)
            for j in range(NU):
                sigmoid(j)
                if j < 5:
                    take(act, nc.scalar, 4 + j, 0, hT_act)

        @block.tensor
        def _(pe):
            def turn(t):
                r = rows(t)
                pe.wait_ge(h_done, t + 1)
                if t >= 1:
                    pe.wait_ge(hT_act, t)
                    pe.wait_ge(hT_dve, t)
                for k in range(KD):
                    last = nc.tensor.transpose(ps[:, k // 4, (k % 4) * P:(k % 4) * P + r], h_t[:r, t % NB, k * P:(k + 1) * P],
                                               ident[:r, :r])
                last.then_inc(transposed, 1)

            pe.wait_ge(consts_in, 16)
            for t in range(4):
                turn(t)
            for j, (n, c) in enumerate(units):
                lo, hi = CUTS[n], CUTS[n + 1]
                if c == 0:
                    pe.wait_ge(hT_act, (4, 7, NS)[n])
                    pe.wait_ge(hT_dve, (4, 7, NS)[n])
                if n == 0:
                    pe.wait_ge(w_in[c], 16)
                if j >= 2:
                    pe.wait_ge(u_done, j - 1)
                for part in range(2):
                    for k in range(KD):
                        w = w_c[:, c, k * 2 * P + part * P:k * 2 * P + (part + 1) * P]
                        last = nc.tensor.matmul(ps[:, 2 + 2 * (j % 2) + part, 0:hi - lo], w, hT[:, k, lo:hi],
                                                start=(k == 0), stop=(k == KD - 1))
                last.then_inc(gate_done, 1)
                if j < 5:
                    turn(4 + j)


def mixer_block(nc, a, ps, chains, const, hT, u, acc, cw, qT, kT, v_all, v_meta, z, zT, q_t, k_t, w_z, w_q, w_kv0, qg):
    ctx = ExitStack()
    with ctx:
        sb = lambda n, s, d=F32: ctx.enter_context(nc.sbuf_tensor(n, s, d))
        sem = lambda n: ctx.enter_context(nc.semaphore(n))
        w_kv1 = sb("w_kv1", [P, 2 * H * NOPE])
        w_kv = [w_kv0, w_kv1[:, :]]
        ssq = sb("ssq", [P, 2, 2])
        rr = sb("rr", [P, 2, 2])
        ra = sb("ra", [P, H, ROPE])
        rb = sb("rb", [P, H, ROPE])
        ka = sb("ka", [P, ROPE])
        kb = sb("kb", [P, ROPE])
        ident = const[:, K_ID:K_ID + P]

        w_ready, vm_in = sem("b_w"), sem("b_vm")
        folded, z_mm, z_sq, z_copied, z_cp2, r_done = (sem("b_" + n) for n in ("folded", "z", "z_sq", "z_cp", "z_cp2", "r"))
        zT_mm, zT_a, zT_d = (sem("b_" + n) for n in ("zT_mm", "zT_a", "zT_d"))
        q_mm, kv_mm, q_ev, k_ev, v_ev, roped = (sem("b_" + n) for n in ("q_mm", "kv_mm", "q_ev", "k_ev", "v_ev", "roped"))
        kr_used = sem("b_kr_used")
        tq_mm, tk_mm, tq_ev, tk_ev = (sem("b_" + n) for n in ("tq_mm", "tk_mm", "tq_ev", "tk_ev"))
        block = ctx.enter_context(nc.Block())
        NS = NT + 1

        @block.sync
        def _(sp):
            sp.dma_start(w_kv1[:, :], a["w_kv"][:, 1, :]).then_inc(w_ready, 16)
            for h in range(H):
                if h == 0:
                    sp.wait_ge(v_ev, 1)
                    sp.wait_ge(folded, 2)
                sp.dma_start(v_meta[META * h:META * (h + 1), VD * h:VD * (h + 1)],
                             v_all[:META, 0, VD * h:VD * (h + 1)]).then_inc(vm_in, 16)
            sp.wait_ge(vm_in, 16 * H)

        @block.gpsimd
        def _(pool):
            pool.wait_ge(w_ready, 16)
            pool.tensor_scalar(w_kv1[:, :], w_kv1[:, :], qg[:, 4:5], None, ALU.mult).then_inc(folded, 1)
            pool.memset(v_meta[:, :], 0.0).then_inc(folded, 1)
            chain = chains["gpsimd"]
            halves = lambda x, t, half: x[QK:QK + 1, :, t + CHUNK * half:t + CHUNK * (half + 1)]
            for t in range(NS):
                r = rows(t)
                c2 = const[:r, K_COS + ROPE * t:K_COS + ROPE * (t + 1)]
                s2 = const[:r, K_SIN + ROPE * t:K_SIN + ROPE * (t + 1)]
                half = ROPE // 2
                if t:
                    pool.wait_ge(roped, 2 * t - 1)
                    for half_tile, queries, keys in ((0, 1.0, 0.0), (1, 0.0, NEG_INF)):
                        pool.memset(halves(qT, P * (t - 1), half_tile), queries)
                        ins = pool.memset(halves(kT, col(t), half_tile), keys)
                    chain(ins)
                pool.wait_ge(z_sq, t + 1)
                for part, width in ((0, QL), (1, KVL)):
                    if part or t:
                        ins = inverse_root(pool, chain, const, rr[:r, t % 2, part:part + 1], ssq[:r, t % 2, part:part + 1], 1.0 / width)
                ins.then_inc(r_done, 1)
                pool.wait_ge(z_cp2, t + 1)
                kr = z[:r, QL + KVL:ZR]
                pool.tensor_tensor(ka[:r, :], kr, c2, ALU.mult)
                pool.tensor_tensor(kb[:r, :], kr, s2, ALU.mult).then_inc(kr_used, 1)
                pool.wait_ge(kr_used, t + 1)
                if t >= 1:
                    pool.wait_ge(tk_mm, t)
                one = lambda x, lo: x[:r, lo:lo + half].unsqueeze(1).broadcast_to([r, H, half])
                pool.tensor_tensor(k_t[:r, :, NOPE:NOPE + half], one(ka, 0), one(kb, half), ALU.subtract)
                pool.tensor_tensor(k_t[:r, :, NOPE + half:QK], one(kb, 0), one(ka, half), ALU.add).then_inc(roped, 1)
                if t >= 1:
                    pool.wait_ge(q_ev, 2 * t)
                    qr = q_t[:r, :, NOPE:QK]
                    many = lambda x: x.unsqueeze(1).broadcast_to([r, H, ROPE])
                    pool.tensor_tensor(ra[:r, :, :], qr, many(c2), ALU.mult)
                    chain(pool.tensor_tensor(rb[:r, :, :], qr, many(s2), ALU.mult))
                    pool.tensor_tensor(q_t[:r, :, NOPE:NOPE + half], ra[:r, :, 0:half], rb[:r, :, half:ROPE], ALU.subtract)
                    pool.tensor_tensor(q_t[:r, :, NOPE + half:QK], rb[:r, :, 0:half], ra[:r, :, half:ROPE], ALU.add).then_inc(roped, 1)

        @block.scalar
        def _(act):
            for t in range(NS + 1):
                if t < NS:
                    r = rows(t)
                    act.wait_ge(z_mm, t + 1)
                    if t:
                        act.wait_ge(zT_mm, t)
                        act.wait_ge(kr_used, t)
                        nc.scalar.activation(z[:r, 0:QL], ps[:r, 0, 0:QL], ACT.Copy).then_inc(z_copied, 1)
                        act.wait_ge(z_copied, t)
                        nc.scalar.activation(ps[:r, 0, 0:QL], ps[:r, 0, 0:QL], ACT.Square, accum_out=ssq[:r, t % 2, 0:1])
                    nc.scalar.activation(z[:r, QL:ZR], ps[:r, 1, 0:KVL + ROPE], ACT.Copy).then_inc(z_cp2, 1)
                    act.wait_ge(z_cp2, t + 1)
                    nc.scalar.activation(ps[:r, 1, 0:KVL], ps[:r, 1, 0:KVL], ACT.Square, accum_out=ssq[:r, t % 2, 1:2]).then_inc(z_sq, 1)
                if t >= 1:
                    e = t - 1
                    r = rows(e)
                    act.wait_ge(r_done, e + 1)
                    if e:
                        act.wait_ge(q_mm, e)
                        if e >= 2:
                            act.wait_ge(tq_mm, e - 1)
                        for b in range(2):
                            nc.scalar.activation(q_t[:r, 4 * b:4 * b + 4, :].rearrange("p h d -> p (h d)"), ps[:r, 4 + b, 0:4 * QK],
                                                 ACT.Copy, scale=rr[:r, e % 2, 0:1]).then_inc(q_ev, 1)
                    act.wait_ge(kv_mm, e + 1)
                    if e:
                        act.wait_ge(tk_mm, e)
                    nc.scalar.activation(k_t[:r, :, 0:NOPE], ps[:r, 6, :].rearrange("p (h d) -> p h d", d=NOPE), ACT.Copy,
                                         scale=rr[:r, e % 2, 1:2]).then_inc(k_ev, 1)
                    nc.scalar.activation(v_all[:r, e, :], ps[:r, 7, :], ACT.Copy, scale=rr[:r, e % 2, 1:2]).then_inc(v_ev, 1)

        taps = CHUNK_TAPS[EARLY_TAPS:] + [(2, k) for k in range(TAPS)]

        @block.vector
        def _(dve):
            done = 0
            chain = chains["vector"]
            for t in range(NS + 2):
                if t >= 2:
                    e = t - 2
                    r = rows(e)
                    if e:
                        dve.wait_ge(tq_mm, e)
                        for b in range(2):
                            nc.vector.tensor_copy(qT[:QK, 4 * b:4 * b + 4, P * (e - 1):P * e],
                                                  ps[:QK, 2 + b, :].rearrange("p (h t) -> p h t", t=P)).then_inc(tq_ev, 1)
                    dve.wait_ge(tk_mm, e + 1)
                    for b in range(2):
                        nc.vector.tensor_copy(kT[:QK, 4 * b:4 * b + 4, col(e):col(e) + r],
                                              ps[:QK, 6 + b, :].rearrange("p (h t) -> p h t", t=P)[:, :, 0:r]).then_inc(tk_ev, 1)
                if t < NS:
                    r = rows(t)
                    dve.wait_ge(zT_mm, t + 1)
                    if t >= 1:
                        dve.wait_ge(kv_mm, t)
                        nc.vector.tensor_copy(zT[:, 0:3, 0:r], ps[:, 2, 0:3 * P].rearrange("p (k t) -> p k t", t=P)[:, :, 0:r]).then_inc(zT_d, 1)
                    nc.vector.tensor_copy(zT[:, 3:5, 0:r], ps[:, 3, 0:2 * P].rearrange("p (k t) -> p k t", t=P)[:, :, 0:r]).then_inc(zT_a, 1)
                upto = min(len(taps), len(taps) * (t + 1) // NS)
                while done < upto:
                    (chunk_tap if len(taps[done]) == 3 else tap)(nc, chain, u, acc, cw, *taps[done])
                    done += 1

        @block.tensor
        def _(pe):
            def latents(t):
                r, lo = rows(t), col(t)
                if t:
                    pe.wait_ge(z_sq, t)
                    for k in range(KD):
                        nc.tensor.matmul(ps[:r, 0, 0:QL], hT[:, k, lo:lo + r], w_z[:, k, 0:QL], start=(k == 0), stop=(k == KD - 1))
                for k in range(KD):
                    last = nc.tensor.matmul(ps[:r, 1, 0:KVL + ROPE], hT[:, k, lo:lo + r], w_z[:, k, QL:ZR],
                                            start=(k == 0), stop=(k == KD - 1))
                last.then_inc(z_mm, 1)

            def heads_turned(t):
                r = rows(t)
                pe.wait_ge(roped, 2 * t + 1)
                pe.wait_ge(zT_d, min(t + 1, NT))
                pe.wait_ge(zT_a, min(t + 2, NS))
                if t:
                    pe.wait_ge(q_ev, 2 * t)
                    for h in range(H):
                        last = nc.tensor.transpose(ps[:QK, 2 + h // 4, (h % 4) * P:(h % 4 + 1) * P], q_t[:r, h, :], ident[:r, :r])
                    last.then_inc(tq_mm, 1)
                pe.wait_ge(k_ev, t + 1)
                pe.wait_ge(v_ev, t + 1)
                for h in range(H):
                    last = nc.tensor.transpose(ps[:QK, 6 + h // 4, (h % 4) * P:(h % 4) * P + r], k_t[:r, h, :], ident[:r, :r])
                last.then_inc(tk_mm, 1)

            def project(t):
                r = rows(t)
                if t == 0:
                    pe.wait_ge(folded, 1)
                else:
                    pe.wait_ge(zT_d, t)
                    if t >= 2:
                        pe.wait_ge(q_ev, 2 * (t - 1))
                    for b in range(2):
                        for k in range(3):
                            last = nc.tensor.matmul(ps[:r, 4 + b, 0:4 * QK], zT[:, k, 0:r], w_q[:, k, 4 * QK * b:4 * QK * (b + 1)],
                                                    start=(k == 0), stop=(k == 2))
                    last.then_inc(q_mm, 1)
                pe.wait_ge(zT_a, t + 1)
                if t:
                    pe.wait_ge(tk_ev, 2 * t)
                for b in range(2):
                    for k in range(2):
                        last = nc.tensor.matmul(ps[:r, 6 + b, :], zT[:, 3 + k, 0:r], w_kv[k][:, 512 * b:512 * (b + 1)],
                                                start=(k == 0), stop=(k == 1))
                last.then_inc(kv_mm, 1)

            def latents_turned(t):
                r = rows(t)
                if t >= 3:
                    pe.wait_ge(tq_ev, 2 * (t - 2))
                if t:
                    pe.wait_ge(z_copied, t)
                    for k in range(3):
                        nc.tensor.transpose(ps[:, 2, k * P:k * P + r], z[:r, k * P:(k + 1) * P], ident[:r, :r])
                pe.wait_ge(z_cp2, t + 1)
                if t >= 1:
                    pe.wait_ge(zT_a, t)
                for k in range(2):
                    last = nc.tensor.transpose(ps[:, 3, k * P:k * P + r], z[:r, QL + k * P:QL + (k + 1) * P], ident[:r, :r])
                last.then_inc(zT_mm, 1)

            for s in range(NS + 2):
                if s < NS:
                    latents(s)
                if s >= 2:
                    heads_turned(s - 2)
                if 1 <= s <= NS:
                    project(s - 1)
                if s < NS:
                    latents_turned(s)


def attention_units():
    units = []
    for i in range(NT):
        heads = 1024 // (P * (i + 1)) if i != 2 else 2
        units += [(i, h, heads) for h in range(0, H, heads)]
    return units


def attention_block(nc, a, ps, chains, const, u, acc, cw, qT, kT, v_all, v_meta, o_all, p, pT, w_o, g_o):
    ctx = ExitStack()
    with ctx:
        sb = lambda n, s, d=F32: ctx.enter_context(nc.sbuf_tensor(n, s, d))
        sem = lambda n: ctx.enter_context(nc.semaphore(n))
        m_s = sb("m_s", [P, NT, H, META])
        m_p = sb("m_p", [P, H, META])
        m_pT = sb("m_pT", [P, P])
        m_neg = sb("m_neg", [P, NT, H])
        r_max = sb("r_max", [P, 2, H])
        bias = sb("bias", [P, 2, H])
        sums = sb("sums", [P, 2, H])
        m_sums = sb("m_sums", [P, H])
        inv = sb("inv", [P, H])
        scale = float(np.float32(QK ** -0.5))
        ident = const[:, K_ID:K_ID + P]
        units = attention_units()
        NU = len(units)
        first = [n for n, (i, h, _) in enumerate(units) if h == 0] + [NU]

        (m_mm, m_copied, s_mm, biased, exp_done, t_mm, ev_act, ev_dve, pv_mm, m_arg, m_exp, m_t, m_tc, o_mm,
         o_done, sums_done) = (sem("c_" + n) for n in ("m_mm", "m_copied", "s_mm", "biased", "exp", "t_mm", "ev_act",
                                                             "ev_dve", "pv_mm", "m_arg", "m_exp", "m_t", "m_tc", "o_mm",
                                                             "o_done", "sums_done"))
        wo_in = sem("c_wo_in")
        block = ctx.enter_context(nc.Block())
        at = lambda i, h: h * (512 if i == 2 else P * (i + 1))
        pair = lambda n: ps[:, 2 * (n % 3):2 * (n % 3) + 2, :].rearrange("p b n -> p (b n)")

        def blocks_of(n):
            i, _, heads = units[n]
            return [(h, k) for h in range(heads) for k in range(i + 1)]

        m_tiles = [range(0, 3), range(3, 6), range(6, NT)]
        two_banks = lambda n: len(blocks_of(n)) > 4
        dve_evacs = lambda n: sum(two_banks(m) for m in range(n))

        @block.sync
        def _(sp):
            sp.dma_start(g_o[:, :], a["out_g"]).then_inc(wo_in, 16)
            sp.dma_start(w_o[:, :, :], a["w_o"]).then_inc(wo_in, 16)

        @block.gpsimd
        def _(pool):
            pool.wait_ge(wo_in, 32)
            for k in range(KD):
                pool.tensor_scalar(w_o[:, k, :], w_o[:, k, :], g_o[:, k:k + 1], None, ALU.mult)

        @block.tensor
        def _(pe):
            def scores(n):
                i, h0, heads = units[n]
                if n >= 3:
                    pe.wait_ge(ev_act, n - 2)
                    if dve_evacs(n - 2):
                        pe.wait_ge(ev_dve, dve_evacs(n - 2))
                keys = P * i
                for h in range(heads):
                    for lo in range(0, keys, 512):
                        hi = min(lo + 512, keys)
                        nc.tensor.matmul(pair(n)[:, at(i, h) + lo:at(i, h) + hi], qT[:QK, h0 + h, P * i:P * (i + 1)],
                                         kT[:QK, h0 + h, META + lo:META + hi], start=True, stop=True)
                    last = nc.tensor.matmul(pair(n)[:, at(i, h) + keys:at(i, h) + keys + P], qT[:, h0 + h, P * i:P * (i + 1)],
                                            kT[:, h0 + h, META + keys:META + keys + P], start=True, stop=True)
                last.then_inc(s_mm, 1)

            def transposes(n):
                i, _, _ = units[n]
                pe.wait_ge(exp_done, n + 1)
                for b, (h, k) in enumerate(blocks_of(n)):
                    last = nc.tensor.transpose(pair(n)[:, b * P:(b + 1) * P], p[:, n % 2, at(i, h) + k * P:at(i, h) + (k + 1) * P], ident)
                last.then_inc(t_mm, 1)

            def values(n):
                i, h0, heads = units[n]
                if h0 == 0 and i >= 1:
                    meta_values(i - 1)
                pe.wait_ge(ev_act, n + 1)
                if two_banks(n):
                    pe.wait_ge(ev_dve, dve_evacs(n + 1))
                for b, (h, k) in enumerate(blocks_of(n)):
                    at_v = slice(VD * (h0 + h), VD * (h0 + h + 1))
                    last = nc.tensor.matmul(ps[:, 6 + i % 2, at_v], pT[:, n % 2, b, :], v_all[:, k + 1, at_v],
                                            start=(h0 == 0 and b == 0), stop=False, skip_group_check=True)
                last.then_inc(pv_mm, 1)
                if h0 + heads == H:
                    pe.wait_ge(m_exp, i + 1)
                    if i >= 1:
                        pe.wait_ge(o_done, i)
                    nc.tensor.transpose(ps[:, 6 + (i + 1) % 2, 0:P], m_p[:, :, :].rearrange("p h k -> p (h k)"), ident).then_inc(m_t, 1)

            def meta_values(i):
                pe.wait_ge(m_tc, i + 1)
                nc.tensor.matmul(ps[:, 6 + i % 2, :], m_pT[:, :], v_meta[:, :], start=False, stop=True,
                                 skip_group_check=True).then_inc(o_mm, 1)

            def meta_scores(g):
                for i in m_tiles[g]:
                    for h in range(H):
                        c = P * (i - m_tiles[g][0]) + META * h
                        last = nc.tensor.matmul(ps[:, 5 + g, c:c + WR], qT[:QK, h, P * i:P * (i + 1)], kT[:QK, h, 0:WR], start=True, stop=True)
                last.then_inc(m_mm, 1)

            scores(0)
            meta_scores(0)
            scores(1)
            meta_scores(1)
            meta_scores(2)
            pe.wait_ge(m_copied, 3)
            for n in range(NU):
                transposes(n)
                if n + 2 < NU:
                    scores(n + 2)
                if n >= 1:
                    values(n - 1)
            values(NU - 1)
            meta_values(NT - 1)

        @block.scalar
        def _(act):
            def exps(n):
                i, h0, heads = units[n]
                if h0 == 0 and i >= 2:
                    act.wait_ge(o_done, i - 1)
                act.wait_ge(biased, n + 1)
                if n >= 2:
                    act.wait_ge(t_mm, n - 1)
                keys = P * (i + 1)
                for h in range(heads):
                    last = nc.scalar.activation(p[:, n % 2, at(i, h):at(i, h) + keys], pair(n)[:, at(i, h):at(i, h) + keys], ACT.Exp,
                                                bias=bias[:, i % 2, h0 + h:h0 + h + 1], scale=scale,
                                                accum_out=sums[:, i % 2, h0 + h:h0 + h + 1])
                last.then_inc(exp_done, 1)
                if h0 + heads == H:
                    act.wait_ge(m_arg, i + 1)
                    nc.scalar.activation(m_p[:, :, :], m_p[:, :, :], ACT.Exp).then_inc(m_exp, 1)

            def meta_copy(i):
                act.wait_ge(m_t, i + 1)
                if i >= 1:
                    act.wait_ge(o_mm, i)
                nc.scalar.activation(m_pT[:, :], ps[:, 6 + (i + 1) % 2, 0:P], ACT.Copy).then_inc(m_tc, 1)

            for g, tiles in enumerate(m_tiles):
                act.wait_ge(m_mm, g + 1)
                nc.scalar.activation(m_s[:, tiles[0]:tiles[-1] + 1, :, :].rearrange("p t h k -> p (t h k)"), ps[:, 5 + g, 0:P * len(tiles)],
                                     ACT.Copy).then_inc(m_copied, 1)
            exps(0)
            for n, (i, h0, _) in enumerate(units):
                if n + 1 < NU:
                    exps(n + 1)
                act.wait_ge(t_mm, n + 1)
                if n >= 2:
                    act.wait_ge(pv_mm, n - 1)
                m = min(4, len(blocks_of(n)))
                nc.scalar.activation(pT[:, n % 2, 0:m, :].rearrange("p k t -> p (k t)"), pair(n)[:, 0:m * P], ACT.Copy).then_inc(ev_act, 1)
                if h0 == 0 and i >= 1:
                    meta_copy(i - 1)
            meta_copy(NT - 1)

        taps = [(3, k) for k in range(TAPS)]

        @block.vector
        def _(dve):
            chain = chains["vector"]

            def maxima(n):
                i, h0, heads = units[n]
                dve.wait_ge(s_mm, n + 1)
                keys = P * (i + 1)
                if heads == 1:
                    src = pair(n)[:, 0:keys].unsqueeze(1)
                else:
                    src = pair(n).rearrange("p (h k) -> p h k", k=at(i, 1))[:, 0:heads, 0:keys]
                chain(nc.vector.reduce_max(r_max[:, n % 2, 0:heads], src, AX.X))
                if h0 == 0 and i >= 2:
                    dve.wait_ge(exp_done, first[i - 1])
                hs = slice(h0, h0 + heads)
                nc.vector.scalar_tensor_tensor(bias[:, i % 2, hs], r_max[:, n % 2, 0:heads], -scale, m_neg[:, i, hs],
                                               ALU.mult, ALU.min).then_inc(biased, 1)
                if h0 + heads == H:
                    dve.wait_ge(biased, n + 1)
                    if i >= 1:
                        dve.wait_ge(m_t, i)
                        dve.wait_ge(sums_done, i)
                    nc.vector.scalar_tensor_tensor(m_p[:, :, :], m_s[:, i, :, :], scale,
                                                   bias[:, i % 2, :].unsqueeze(2).broadcast_to([P, H, META]),
                                                   ALU.mult, ALU.add).then_inc(m_arg, 1)

            def finish(i):
                dve.wait_ge(sums_done, i + 1)
                chain(nc.vector.tensor_tensor(m_sums[:, :], m_sums[:, :], sums[:, i % 2, :], ALU.add))
                chain(nc.vector.reciprocal(inv[:, :], m_sums[:, :]))
                dve.wait_ge(o_mm, i + 1)
                nc.vector.tensor_tensor(o_all[:, i, :].rearrange("p (h d) -> p h d", d=VD),
                                        ps[:, 6 + i % 2, :].rearrange("p (h d) -> p h d", d=VD),
                                        inv[:, :].unsqueeze(2).broadcast_to([P, H, VD]), ALU.mult).then_inc(o_done, 1)

            def meta_sums(i):
                dve.wait_ge(m_exp, i + 1)
                if i >= 1:
                    dve.wait_ge(o_done, i)
                nc.vector.reduce_sum(m_sums[:, :], m_p[:, :, :], AX.X).then_inc(sums_done, 1)

            for g, tiles in enumerate(m_tiles):
                at_t = slice(tiles[0], tiles[-1] + 1)
                dve.wait_ge(m_copied, g + 1)
                chain(nc.vector.reduce_max(m_neg[:, at_t, :], m_s[:, at_t, :, :], AX.X))
                chain(nc.vector.tensor_scalar(m_neg[:, at_t, :], m_neg[:, at_t, :], -scale, None, ALU.mult))
                if g == 0:
                    maxima(0)
            done = 0
            for n, (i, h0, heads) in enumerate(units):
                if i >= 1 and h0 == 0:
                    meta_sums(i - 1)
                if n + 1 < NU:
                    maxima(n + 1)
                if two_banks(n):
                    dve.wait_ge(t_mm, n + 1)
                    if n >= 2:
                        dve.wait_ge(pv_mm, n - 1)
                    m = len(blocks_of(n))
                    nc.vector.tensor_copy(pT[:, n % 2, 4:m, :].rearrange("p k t -> p (k t)"), pair(n)[:, 512:m * P]).then_inc(ev_dve, 1)
                if i >= 1 and n == first[i] + 1:
                    finish(i - 1)
                upto = len(taps) * (n + 1) // NU
                while done < upto:
                    tap(nc, chain, u, acc, cw, *taps[done])
                    done += 1
            meta_sums(NT - 1)
            finish(NT - 1)


def merge_block(nc, a, ps, chains, rows_in, const, acc, o_all, junk, w_o, h_dram, h1, h1_dram, logits):
    ctx = ExitStack()
    with ctx:
        sb = lambda n, s, d=F32: ctx.enter_context(nc.sbuf_tensor(n, s, d))
        sem = lambda n: ctx.enter_context(nc.semaphore(n))
        cg = sb("cg", [P, 2, NC4])
        w_r = sb("w_r", [P, KD, WR])
        g1 = sb("g1", [P, D])
        b1 = sb("b1", [P, D])
        sq = sb("sq", [P, 2, NC4, 512])
        rs = sb("rs", [P, 2, 512])
        rc = sb("rc", [P, NT])
        ra = sb("ra_o", [P, NT])
        oT_hi = sb("oT_hi", [P, 2, NC4, P], F32R)
        oT_lo = sb("oT_lo", [P, 2, NC4, P], F32R)
        wo_hi = sb("wo_hi", [P, NC4, D], F32R)
        wo_lo = sb("wo_lo", [P, NC4, D], F32R)
        c_hi = sb("c_hi", [P, 2, NC4, P], F32R)
        c_lo = sb("c_lo", [P, 2, NC4, P], F32R)
        hT1 = sb("hT1", [P, KD, P])
        stats = sb("stats1", [P, 12])
        mv = sb("mv1", [P, 2])
        rstd = sb("rstd1", [P, 1])
        ident, ones = const[:, K_ID:K_ID + P], const[:, K_ONE:K_ONE + P]

        (sum_mm, centred, squared, var_mm, var_ev, rs_done, scaled, silu, c_sq, csum_mm, rc_ev, ra_done, rc_done, o_sq,
         oT_mm, oT_ev, yc_mm, ya_mm, res_done, ya_done, yc_done, stats_done, rstd_done, normed, gained, h1_done, hT_mm,
         hT_a, hT_d, lg_mm, lg_ev) = (sem("d_" + n) for n in
                                ("sum_mm", "centred", "squared", "var_mm", "var_ev", "rs", "scaled", "silu", "c_sq", "csum_mm",
                                 "rc_ev", "ra", "rc", "o_sq", "oT_mm", "oT_ev", "yc_mm", "ya_mm", "res", "ya", "yc", "stats",
                                 "rstd", "normed", "gained", "h1", "hT_mm", "hT_a", "hT_d", "lg_mm", "lg_ev"))
        wo_high, wo_low, c_high, c_low, oT_low = (sem("d_" + n) for n in ("wo_high", "wo_low", "c_high", "c_low", "oT_low"))
        w_in, cg_in, h1_out, padded = sem("d_w"), sem("d_cg"), sem("d_h1_out"), sem("d_padded")
        block = ctx.enter_context(nc.Block())
        WO_ORDER = [4, 5, 6, 7, 0, 1, 2, 3]
        token_halves = [slice(0, 512), slice(512, 1024)]

        @block.sync
        def _(sp):
            sp.dma_start(cg[:, :, :], a["conv_ln"]).then_inc(cg_in, 16)
            for t in range(NT):
                sp.dma_start(h1[:, t, :], h_dram[P * t:P * (t + 1), :]).then_inc(rows_in[t], 16)
                if t == 1:
                    sp.wait_ge(padded, 1)
                    sp.dma_start(w_r[:, :, 0:G + E], a["w_r"]).then_inc(w_in, 16)
                    sp.dma_start(g1[:, :], a["ln1_g"].broadcast_to([P, D])).then_inc(w_in, 16)
                    sp.dma_start(b1[:, :], a["ln1_b"].broadcast_to([P, D])).then_inc(w_in, 16)
            for t in range(NT):
                sp.wait_ge(h1_done, t + 1)
                sp.dma_start(h1_dram[P * t:P * (t + 1), :], h1[:, t, :]).then_inc(h1_out, 16)
            sp.wait_ge(h1_out, 16 * NT)

        @block.gpsimd
        def _(pool):
            chain = chains["gpsimd"]
            pool.memset(w_r[:, :, :], 0.0).then_inc(padded, 1)
            for t in range(NT):
                pool.wait_ge(rows_in[t], 16)
                pool.tensor_scalar(h1[:, t, :], h1[:, t, :], ALPHA, None, ALU.mult).then_inc(res_done, 1)
                if t == 0:
                    pool.wait_ge(o_sq, NT)
                    inverse_root(pool, chain, const, ra[:, :], ra[:, :], 1.0 / C).then_inc(ra_done, 1)
            pool.wait_ge(rc_ev, 1)
            inverse_root(pool, chain, const, rc[:, :], rc[:, :], 1.0 / C).then_inc(rc_done, 1)
            for t in range(NT):
                pool.wait_ge(stats_done, t + 1)
                inverse_root(pool, chain, const, rstd[:, :], mv[:, 1:2], 1.0).then_inc(rstd_done, 1)
                pool.wait_ge(gained, t + 1)
                pool.tensor_tensor(h1[:, t, :], h1[:, t, :], b1[:, :], ALU.add).then_inc(h1_done, 1)

        @block.vector
        def _(dve):
            chain = chains["vector"]

            def attention_part(t):
                if t == 0:
                    dve.wait_ge(ra_done, 1)
                dve.wait_ge(ya_mm, t + 1)
                dve.wait_ge(res_done, t + 1)
                nc.vector.scalar_tensor_tensor(h1[:, t, :], ps[:, 2 * (t % 2):2 * (t % 2) + 2, :].rearrange("p b n -> p (b n)"),
                                               ra[:, t:t + 1], h1[:, t, :], ALU.mult, ALU.add).then_inc(ya_done, 1)

            def low_weights(k):
                dve.wait_ge(wo_high, WO_ORDER.index(k) + 1)
                nc.vector.tensor_tensor(wo_lo[:, k % NC4, :], w_o[:, k, :], wo_hi[:, k % NC4, :], ALU.subtract).then_inc(wo_low, 1)

            def low_oT(t):
                dve.wait_ge(oT_ev, t + 1)
                if t >= 2:
                    dve.wait_ge(ya_mm, t - 1)
                nc.vector.tensor_tensor(oT_lo[:, t % 2, :, :].rearrange("p k t -> p (k t)"), ps[:, 4, :],
                                        oT_hi[:, t % 2, :, :].rearrange("p k t -> p (k t)"), ALU.subtract).then_inc(oT_low, 1)

            def low_conv(t):
                dve.wait_ge(c_high, t)
                nc.vector.tensor_tensor(c_lo[:, t % 2, :, :], acc[:, :, P * t:P * (t + 1)], c_hi[:, t % 2, :, :],
                                        ALU.subtract).then_inc(c_low, 1)

            def normalise(n):
                dve.wait_ge(var_ev, n + 1)
                nc.vector.reciprocal(rs[:, n, :], rs[:, n, :]).then_inc(rs_done, 1)
                dve.wait_ge(rs_done, n + 1)
                for c in range(NC4):
                    nc.vector.tensor_tensor(acc[:, c, token_halves[n]], acc[:, c, token_halves[n]], rs[:, n, :], ALU.mult).then_inc(scaled, 1)

            for k in WO_ORDER[0:NC4]:
                low_weights(k)
            low_oT(0)
            low_oT(1)
            for n in range(2):
                dve.wait_ge(sum_mm, n + 1)
                for c in range(NC4):
                    nc.vector.scalar_tensor_tensor(acc[:, c, token_halves[n]], ps[:, 6 + n, :], -1.0 / C, acc[:, c, token_halves[n]],
                                                   ALU.mult, ALU.add).then_inc(centred, 1)
            dve.wait_ge(centred, 2 * NC4)
            for t in range(NT):
                attention_part(t)
                if t < 2:
                    normalise(t)
                if 2 <= t + 2 < NT:
                    low_oT(t + 2)
                if t == 4:
                    dve.wait_ge(csum_mm, 1)
                    nc.vector.tensor_copy(rc[:, :], ps[:, 5, 0:NT]).then_inc(rc_ev, 1)

            def take_logits(t):
                dve.wait_ge(lg_mm, t + 1)
                nc.vector.tensor_copy(logits[:, t, :], ps[:, 7, 0:G + E]).then_inc(lg_ev, 1)

            for k in WO_ORDER[NC4:]:
                low_weights(k)
            low_conv(1)
            dve.wait_ge(rc_done, 1)
            dve.wait_ge(w_in, 48)
            for t in range(NT + 1):
                if t < NT:
                    dve.wait_ge(yc_mm, t + 1)
                    dve.wait_ge(ya_done, NT)
                    nc.vector.scalar_tensor_tensor(h1[:, t, :], ps[:, 2 * (t % 2):2 * (t % 2) + 2, :].rearrange("p b n -> p (b n)"),
                                                   rc[:, t:t + 1], h1[:, t, :], ALU.mult, ALU.add).then_inc(yc_done, 1)
                    dve.wait_ge(yc_done, t + 1)
                    for b in range(2):
                        chain(nc.vector.bn_stats(stats[:, 6 * b:6 * b + 6], h1[:, t, 512 * b:512 * (b + 1)]))
                    nc.vector.bn_aggr(mv[:, :], stats[:, :]).then_inc(stats_done, 1)
                    if t + 2 < NT:
                        low_conv(t + 2)
                if t >= 2:
                    take_logits(t - 2)
                if t < NT:
                    dve.wait_ge(rstd_done, t + 1)
                    nc.vector.tensor_scalar(h1[:, t, :], h1[:, t, :], mv[:, 0:1], rstd[:, :], ALU.subtract, ALU.mult).then_inc(normed, 1)
                    dve.wait_ge(normed, t + 1)
                    nc.vector.tensor_tensor(h1[:, t, :], h1[:, t, :], g1[:, :], ALU.mult).then_inc(gained, 1)
                if t >= 1:
                    dve.wait_ge(hT_mm, t)
                    nc.vector.tensor_copy(hT1[:, 4:8, :].rearrange("p k t -> p (k t)"), ps[:, 5, :]).then_inc(hT_d, 1)
            take_logits(NT - 1)

        @block.scalar
        def _(act):
            def take_oT(t):
                act.wait_ge(oT_mm, t + 1)
                if t >= 2:
                    act.wait_ge(ya_mm, t - 1)
                nc.scalar.activation(oT_hi[:, t % 2, :, :].rearrange("p k t -> p (k t)"), ps[:, 4, :], ACT.Copy).then_inc(oT_ev, 1)

            def high_conv(t):
                if t >= 3:
                    act.wait_ge(yc_mm, t - 1)
                nc.scalar.activation(c_hi[:, t % 2, :, :], acc[:, :, P * t:P * (t + 1)], ACT.Copy).then_inc(c_high, 1)

            def high_weights(k):
                nc.scalar.activation(wo_hi[:, k % NC4, :], w_o[:, k, :], ACT.Copy).then_inc(wo_high, 1)

            def shape(n):
                for c in range(NC4):
                    act.wait_ge(scaled, NC4 * n + c + 1)
                    nc.scalar.activation(acc[:, c, token_halves[n]], acc[:, c, token_halves[n]], ACT.Silu,
                                         scale=cg[:, 0, c:c + 1], bias=cg[:, 1, c:c + 1]).then_inc(silu, 1)
                for c in range(NC4):
                    act.wait_ge(silu, NC4 * n + c + 1)
                    nc.scalar.activation(sq[:, n, c, :], acc[:, c, token_halves[n]], ACT.Square).then_inc(c_sq, 1)

            for k in WO_ORDER[0:NC4]:
                high_weights(k)
            for t in range(NT):
                nc.scalar.activation(junk[:, t, :], o_all[:, t, :], ACT.Square, accum_out=ra[:, t:t + 1]).then_inc(o_sq, 1)
                if t < 2:
                    take_oT(t)
            for n in range(2):
                for c in range(NC4):
                    act.wait_ge(centred, NC4 * n + c + 1)
                    nc.scalar.activation(sq[:, n, c, :], acc[:, c, token_halves[n]], ACT.Square).then_inc(squared, 1)
            act.wait_ge(cg_in, 16)
            for n in range(2):
                act.wait_ge(var_mm, n + 1)
                nc.scalar.activation(rs[:, n, :], ps[:, 6 + n, :], ACT.Sqrt, scale=1.0 / C,
                                     bias=const[:, K_EPS:K_EPS + 1]).then_inc(var_ev, 1)
            take_oT(2)
            shape(0)
            take_oT(3)
            shape(1)
            for t in range(4, NT):
                take_oT(t)
            act.wait_ge(ya_mm, NT)
            act.wait_ge(wo_low, NC4)
            for k in WO_ORDER[NC4:]:
                high_weights(k)
            act.wait_ge(silu, 2 * NC4)
            high_conv(1)
            for t in range(NT):
                if t + 2 < NT:
                    high_conv(t + 2)
                act.wait_ge(hT_mm, t + 1)
                nc.scalar.activation(hT1[:, 0:4, :].rearrange("p k t -> p (k t)"), ps[:, 4, :], ACT.Copy).then_inc(hT_a, 1)

        @block.tensor
        def _(pe):
            def turn_o(t):
                if t >= 1:
                    pe.wait_ge(oT_ev, t)
                    pe.wait_ge(oT_low, t)
                for k in range(NC4):
                    last = nc.tensor.transpose(ps[:, 4, k * P:(k + 1) * P], o_all[:, t, k * P:(k + 1) * P], ident)
                last.then_inc(oT_mm, 1)

            def attention_part(t):
                pe.wait_ge(oT_low, t + 1)
                if t >= 2:
                    pe.wait_ge(ya_done, t - 1)
                for b in range(2):
                    at = slice(512 * b, 512 * (b + 1))
                    last = split_product(nc, ps[:, 2 * (t % 2) + b, :],
                                         [((oT_hi[:, t % 2, k, :], oT_lo[:, t % 2, k, :]), (wo_hi[:, k, at], wo_lo[:, k, at]))
                                          for k in range(NC4)])
                last.then_inc(ya_mm, 1)

            def conv_part(t):
                if t >= 2:
                    pe.wait_ge(yc_done, t - 1)
                else:
                    pe.wait_ge(ya_done, NT - 1 + t)
                for b in range(2):
                    at, out = slice(512 * b, 512 * (b + 1)), ps[:, 2 * (t % 2) + b, :]
                    if t:
                        pe.wait_ge(wo_low, KD)
                        pe.wait_ge(c_low, t)
                        last = split_product(nc, out, [((c_hi[:, t % 2, k, :], c_lo[:, t % 2, k, :]), (wo_hi[:, k, at], wo_lo[:, k, at]))
                                                       for k in range(NC4)])
                    else:
                        for k in range(NC4):
                            last = nc.tensor.matmul(out, acc[:, k, 0:P], w_o[:, k, at], start=(k == 0), stop=(k == NC4 - 1))
                last.then_inc(yc_mm, 1)

            def router(t):
                pe.wait_ge(hT_a, t + 1)
                pe.wait_ge(hT_d, t + 1)
                if t >= 1:
                    pe.wait_ge(lg_ev, t)
                for k in range(KD):
                    last = nc.tensor.matmul(ps[:, 7, 0:WR], hT1[:, k, :], w_r[:, k, :], start=(k == 0), stop=(k == KD - 1))
                last.then_inc(lg_mm, 1)

            def turn_h(t):
                pe.wait_ge(h1_done, t + 1)
                for k in range(KD):
                    last = nc.tensor.transpose(ps[:, 4 + k // 4, (k % 4) * P:(k % 4 + 1) * P], h1[:, t, k * P:(k + 1) * P], ident)
                last.then_inc(hT_mm, 1)

            for n in range(2):
                for c in range(NC4):
                    last = nc.tensor.matmul(ps[:, 6 + n, :], ones, acc[:, c, token_halves[n]], start=(c == 0), stop=(c == NC4 - 1))
                last.then_inc(sum_mm, 1)
                turn_o(n)
            pe.wait_ge(wo_low, NC4)
            attention_part(0)
            pe.wait_ge(centred, 2 * NC4)
            for n in range(2):
                for c in range(NC4):
                    pe.wait_ge(squared, NC4 * n + c + 1)
                    last = nc.tensor.matmul(ps[:, 6 + n, :], ones, sq[:, n, c, :], start=(c == 0), stop=(c == NC4 - 1))
                last.then_inc(var_mm, 1)
            for t in range(1, NT):
                if t + 1 < NT:
                    turn_o(t + 1)
                attention_part(t)
                if t == 4:
                    pe.wait_ge(c_sq, 2 * NC4)
                    for j in range(NT):
                        for c in range(NC4):
                            last = nc.tensor.matmul(ps[:, 5, j:j + WR], sq[:, j // 4, c, P * (j % 4):P * (j % 4 + 1)], ones[:, 0:WR],
                                                    start=(c == 0), stop=(c == NC4 - 1))
                    last.then_inc(csum_mm, 1)
            pe.wait_ge(w_in, 48)
            pe.wait_ge(var_ev, 2)
            pe.wait_ge(silu, 2 * NC4)
            for t in range(NT + 2):
                if t < NT:
                    conv_part(t)
                if t >= 2:
                    router(t - 2)
                if t == 1:
                    pe.wait_ge(rc_ev, 1)
                    pe.wait_ge(oT_ev, NT)
                if 1 <= t <= NT:
                    turn_h(t - 1)


def route_block(nc, a, ps, chains, const, logits, comb, row_of, token_of, expert_of, blocks_to, n_blocks, gu_w, dn_w, gu_in, dn_in):
    ctx = ExitStack()
    with ctx:
        sb = lambda n, s, d=F32: ctx.enter_context(nc.sbuf_tensor(n, s, d))
        sem = lambda n: ctx.enter_context(nc.semaphore(n))
        rb = sb("rb_", [P, G + E])
        w1 = sb("w1", [P, NT])
        gmax = sb("gmax", [P, NT])
        keyg = sb("keyg", [P, NT, G])
        ohg = sb("ohg", [P, NT, G])
        expo = sb("expo", [P, NT, G + 1])
        gsum = sb("gsum", [P, NT])
        pick = sb("pick", [P, NT, G, EG])
        e_in = sb("e_in", [P, NT, EG])
        key = sb("key", [P, NT, EG])
        oh = sb("oh", [P, 2, NT, EG])
        v12 = sb("v12", [P, 2, NT])
        A = sb("A", [P, 2, NT, G, EG])
        M = sb("M", [P, NT, E])
        rank = sb("rank", [P, NT, E])
        base = sb("base", [P, NT + 1, E])
        over = sb("over", [P, E, 7])
        nover = sb("nover", [P, E])
        pre = sb("pre", [P, 2, E])
        excl = sb("excl", [P, E])
        tmp = sb("tmp", [P, NT, E])
        stat = sb("stat", [P, 3, NT])
        q7 = sb("q7", [P, NT, 7])
        qq = sb("qq", [P, NT])
        pp = sb("pp", [P, 2, NT])
        bb = sb("bb", [P, 2, NT])
        sel = sb("sel", [P, 2, P])
        blk = sb("blk", [P, 2, MAXB + 1])
        of = sb("of", [1, MAXB + 1, E])
        last_of = sb("last_of", [1, E])
        of1 = sb("of1", [1, MAXB + 1])
        slot = sb("slot", [P, 2, MAXB + 1])

        bias_in, args, exps, mset, counted, made, used = (sem("e_" + n) for n in
            ("bias", "args", "exps", "M", "counted", "made", "used"))
        block = ctx.enter_context(nc.Block())
        io = lambda n: const[:, K_IOTA:K_IOTA + n]

        @block.sync
        def _(sp):
            sp.dma_start(rb[:, :], a["b_r"].broadcast_to([P, G + E])).then_inc(bias_in, 16)
            sp.wait_ge(bias_in, 16)
            for b in range(RING):
                if b:
                    sp.wait_ge(gu_in, 16 * b)
                sp.dma_start(gu_w[:, b * WGU:(b + 1) * WGU], a["w_gate_up"][b, :, :]).then_inc(gu_in, 16)
                if b:
                    sp.wait_ge(dn_in, 16 * b)
                sp.dma_start(dn_w[:, b * WDN:(b + 1) * WDN], a["w_down_t"][b, :, :]).then_inc(dn_in, 16)

        @block.scalar
        def _(act):
            act.wait_ge(args, 2)
            nc.scalar.activation(expo[:, :, :], expo[:, :, :], ACT.Exp).then_inc(exps, 1)

        @block.tensor
        def _(pe):
            pe.wait_ge(mset, 1)
            flat = M[:, :, :].rearrange("p t e -> p (t e)")
            nc.tensor.matmul(ps[:, 0, 0:NT * E], const[:, K_TRI:K_TRI + P], flat, start=True, stop=True)
            nc.tensor.matmul(ps[:, 1, 0:NT * E], const[:, K_ONE:K_ONE + P], flat, start=True, stop=True).then_inc(counted, 1)
            for n in range(2 * NT):
                pe.wait_ge(made, n + 1)
                last = nc.tensor.matmul(ps[:, 2, 0:MAXB + 1], sel[:, n % 2, :], blk[:, n % 2, :], start=(n == 0), stop=(n == 2 * NT - 1))
                last.then_inc(used, 1)

        @block.vector
        def _(dve):
            v = nc.vector
            chain = chains["vector"]
            tt = lambda o, x, y, op: chain(v.tensor_tensor(o, x, y, op))
            one = lambda x, n: x.unsqueeze(len(x.shape)).broadcast_to(list(x.shape) + [n])
            dve.wait_ge(bias_in, 16)
            tt(logits[:, :, :], logits[:, :, :], rb[:, :].unsqueeze(1).broadcast_to([P, NT, G + E]), ALU.add)
            lg, le = logits[:, :, 0:G], logits[:, :, G:G + E].rearrange("p t (g e) -> p t g e", e=EG)

            def first_max(out_max, out_hot, x, keys, n):
                desc = const[:, K_DESC + EG - n:K_DESC + EG].unsqueeze(1).broadcast_to([P, NT, n])
                chain(v.reduce_max(out_max, x, AX.X))
                tt(keys, x, one(out_max, n), ALU.is_equal)
                tt(keys, keys, desc, ALU.mult)
                chain(v.reduce_max(w1[:, :], keys, AX.X))
                tt(out_hot, keys, one(w1[:, :], n), ALU.is_equal)

            first_max(gmax[:, :], ohg[:, :, :], lg, keyg[:, :, :], G)
            v.tensor_tensor(expo[:, :, 0:G], lg, one(gmax[:, :], G), ALU.subtract).then_inc(args, 1)
            tt(pick[:, :, :, :], le, one(ohg[:, :, :], EG), ALU.mult)
            chain(v.reduce_sum(e_in[:, :, :], pick[:, :, :, :].rearrange("p t g e -> p t e g"), AX.X))
            first_max(v12[:, 0, :], oh[:, 0, :, :], e_in[:, :, :], key[:, :, :], EG)
            chain(v.scalar_tensor_tensor(e_in[:, :, :], oh[:, 0, :, :], -1e30, e_in[:, :, :], ALU.mult, ALU.add))
            first_max(v12[:, 1, :], oh[:, 1, :, :], e_in[:, :, :], key[:, :, :], EG)
            v.tensor_tensor(expo[:, :, G], v12[:, 1, :], v12[:, 0, :], ALU.subtract).then_inc(args, 1)
            for j in range(2):
                for g in range(G):
                    tt(A[:, j, :, g, :], oh[:, j, :, :], ohg[:, :, g:g + 1].broadcast_to([P, NT, EG]), ALU.mult)
            Af = lambda j: A[:, j, :, :, :].rearrange("p t g e -> p t (g e)")
            v.tensor_tensor(M[:, :, :], Af(0), Af(1), ALU.add).then_inc(mset, 1)
            dve.wait_ge(exps, 1)
            chain(v.reduce_sum(gsum[:, :], expo[:, :, 0:G], AX.X))
            chain(v.tensor_scalar(qq[:, :], expo[:, :, G], 1.0, None, ALU.add))
            tt(gsum[:, :], gsum[:, :], qq[:, :], ALU.mult)
            chain(v.reciprocal(comb[:, 0, :], gsum[:, :]))
            tt(comb[:, 1, :], comb[:, 0, :], expo[:, :, G], ALU.mult)
            dve.wait_ge(counted, 1)
            chain(v.memset(base[:, 0, :], 0.0))
            for t in range(NT):
                tt(base[:, t + 1, :], base[:, t, :], ps[:, 1, E * t:E * (t + 1)], ALU.add)
            tt(rank[:, :, :], base[:, 0:NT, :], ps[:, 0, 0:NT * E].rearrange("p (t e) -> p t e", e=E), ALU.add)
            total = base[:, NT, :]
            chain(v.scalar_tensor_tensor(over[:, :, :], const[:, K_IOTA + 1:K_IOTA + 8].unsqueeze(1).broadcast_to([P, E, 7]), float(P),
                                         one(total, 7), ALU.mult, ALU.is_lt))
            chain(v.reduce_sum(nover[:, :], over[:, :, :], AX.X))
            cur = nover[:, :]
            step, n = 1, 0
            while step < E:
                nxt = pre[:, n % 2, :]
                chain(v.tensor_copy(nxt[:, 0:step], cur[:, 0:step]))
                tt(nxt[:, step:E], cur[:, step:E], cur[:, 0:E - step], ALU.add)
                cur, step, n = nxt, 2 * step, n + 1
            incl = cur
            tt(excl[:, :], incl, nover[:, :], ALU.subtract)
            for j in range(2):
                for m, table in enumerate((rank[:, :, :], excl[:, :].unsqueeze(1).broadcast_to([P, NT, E]),
                                           io(E).unsqueeze(1).broadcast_to([P, NT, E]))):
                    tt(tmp[:, :, :], Af(j), table, ALU.mult)
                    chain(v.reduce_sum(stat[:, m, :], tmp[:, :, :], AX.X))
                chain(v.scalar_tensor_tensor(q7[:, :, :], const[:, K_IOTA + 1:K_IOTA + 8].unsqueeze(1).broadcast_to([P, NT, 7]),
                                             float(P), one(stat[:, 0, :], 7), ALU.mult, ALU.is_le))
                chain(v.reduce_sum(qq[:, :], q7[:, :, :], AX.X))
                chain(v.scalar_tensor_tensor(pp[:, j, :], qq[:, :], -float(P), stat[:, 0, :], ALU.mult, ALU.add))
                tt(stat[:, 1, :], stat[:, 1, :], qq[:, :], ALU.add)
                tt(bb[:, j, :], stat[:, 2, :], stat[:, 1, :], ALU.add)
            for n in range(2 * NT):
                j, t = n // NT, n % NT
                if n >= 2:
                    dve.wait_ge(used, n - 1)
                v.tensor_scalar(sel[:, n % 2, :], io(P), pp[:, j, t:t + 1], None, ALU.is_equal)
                v.tensor_scalar(blk[:, n % 2, :], io(MAXB + 1), bb[:, j, t:t + 1], const[:, K_ROW + n:K_ROW + n + 1],
                                ALU.is_equal, ALU.mult).then_inc(made, 1)
            chain(v.scalar_tensor_tensor(last_of[0:1, :], incl[0:1, :], 1.0, const[0:1, K_IOTA:K_IOTA + E], ALU.add, ALU.add))
            chain(v.tensor_copy(blocks_to[0:1, :], last_of[0:1, :]))
            tt(of[0:1, :, :], last_of[0:1, :].unsqueeze(1).broadcast_to([1, MAXB + 1, E]),
               const[0:1, K_IOTA:K_IOTA + MAXB + 1].unsqueeze(2).broadcast_to([1, MAXB + 1, E]), ALU.is_le)
            chain(v.reduce_sum(of1[0:1, :], of[0:1, :, :], AX.X))
            chain(v.tensor_scalar(expert_of[0:1, :], of1[0:1, :], float(E - 1), None, ALU.min))
            chain(v.tensor_scalar(n_blocks[0:1, 0:1], incl[0:1, E - 1:E], float(E - 2), None, ALU.add))
            dve.wait_ge(used, 2 * NT)
            found, nothing = slot[:, 0, :], slot[:, 1, :]
            chain(v.tensor_copy(found, ps[:, 2, 0:MAXB + 1]))
            chain(v.tensor_scalar(nothing, found, 0.0, float(4 * T), ALU.is_equal, ALU.mult))
            chain(v.scalar_tensor_tensor(row_of[:, :], found, -1.0, nothing, ALU.add, ALU.add))
            chain(v.tensor_scalar(found, found, float(T), -float(T), ALU.is_gt, ALU.mult))
            tt(token_of[:, :], row_of[:, :], found, ALU.add)


def expert_block(nc, a, ps, chains, const, h1, h1_dram, y_dram, row_of, token_of, expert_of, blocks_to, n_blocks, gu_w, dn_w, gu_in, dn_in, g2, b2):
    ctx = ExitStack()
    with ctx:
        sb = lambda n, s, d=F32: ctx.enter_context(nc.sbuf_tensor(n, s, d))
        sem = lambda n: ctx.enter_context(nc.semaphore(n))
        x = sb("x_rows", [P, D])
        x_hi = sb("x_hi", [P, KD // 2, P], F32R)
        x_lo = sb("x_lo", [P, KD // 2, P], F32R)
        xT = sb("xT", [P, KD // 2, P])
        gu_hi = sb("gu_hi", [P, WGU // 2], F32R)
        gu_lo = sb("gu_lo", [P, WGU // 2], F32R)
        dn_hi = sb("dn_hi", [P, WDN], F32R)
        dn_lo = sb("dn_lo", [P, WDN], F32R)
        sg = sb("sg_e", [P, F])
        hh = sb("hh", [P, F])
        h_hi = sb("h_hi", [P, 2, P], F32R)
        h_lo = sb("h_lo", [P, 2, P], F32R)
        y = sb("y_rows", [P, D])
        ident = const[:, K_ID:K_ID + P]
        (x_in, y_out, tx_mm, xT_a, xT_d, gu_mm, sg_done, hh_done, th_mm, hT_ev, dn_mm, y_a, y_d) = (
            sem("f_" + n) for n in ("x_in", "y_out", "tx_mm", "xT_a", "xT_d", "gu_mm", "sg", "hh", "th_mm",
                                    "hT_ev", "dn_mm", "y_a", "y_d"))
        ln_in = sem("f_ln_in")
        gu_high, gu_low, dn_high, dn_low, x_low, h_low = (sem("f_" + n) for n in ("gu_high", "gu_low", "dn_high", "dn_low", "x_low", "h_low"))
        block = ctx.enter_context(nc.Block())
        ds = bass.ds
        blocks = lambda eng: eng.value_load(n_blocks[0:1, 0:1], min_val=E - 2, max_val=MAXB - 2)

        PIECE = WGU // 4

        @block.sync
        def _(sp):
            sp.dma_start(g2[:, :], a["ln2_g"].broadcast_to([P, D])).then_inc(ln_in, 16)
            sp.dma_start(b2[:, :], a["ln2_b"].broadcast_to([P, D])).then_inc(ln_in, 16)
            with sp.Fori(RING, E) as e:
                slot = sp.snap(e % RING)
                blocks_done = sp.value_load(blocks_to[0:1, ds(e - RING, 1)], min_val=1, max_val=MAXB)
                sp.wait_ge(gu_in, e * 16)
                sp.wait_ge(gu_mm, blocks_done)
                sp.dma_start(gu_w[:, ds(slot * WGU, WGU)], a["w_gate_up"][ds(e, 1), :, :].rearrange("a p n -> p (a n)")).then_inc(gu_in, 16)
                sp.wait_ge(dn_in, e * 16)
                sp.wait_ge(dn_mm, blocks_done)
                sp.dma_start(dn_w[:, ds(slot * WDN, WDN)], a["w_down_t"][ds(e, 1), :, :].rearrange("a p n -> p (a n)")).then_inc(dn_in, 16)
            sp.wait_ge(ln_in, 32)

        @block.gpsimd
        def _(pool):
            m = blocks(pool)

            def gather(b):
                if b:
                    pool.wait_ge(tx_mm, b)
                pool.indirect_dma_start(out=x[:, :], out_offset=None, in_=h1_dram,
                                        in_offset=bass.IndirectOffsetOnAxis(ap=token_of[:, b:b + 1], axis=0),
                                        bounds_check=T - 1, oob_is_err=False).then_inc(x_in, 16)

            def scatter(b):
                pool.wait_ge(y_a, b + 1)
                pool.wait_ge(y_d, b + 1)
                pool.indirect_dma_start(out=y_dram, out_offset=bass.IndirectOffsetOnAxis(ap=row_of[:, b:b + 1], axis=0),
                                        in_=y[:, :], in_offset=None, bounds_check=2 * T - 1, oob_is_err=False).then_inc(y_out, 16)

            def step(b):
                if b + 1 < MAXB:
                    with pool.If(m > b - 1) if b + 1 >= E else ExitStack():
                        gather(b + 1)
                with pool.If(m > b - 4) if b - 2 >= E else ExitStack():
                    scatter(b - 2)

            chain = chains["gpsimd"]
            chain(pool.memset(x[:, :], 0.0))
            gather(0)
            gather(1)
            gather(2)
            for b in range(2, MAXB + 2):
                step(b)
                if 2 <= b < 2 + NT:
                    pool.tensor_scalar(h1[:, b - 2, :], h1[:, b - 2, :], ALPHA, None, ALU.mult)
            pool.wait_ge(y_out, m * 16 + 32)

        @block.scalar
        def _(act):
            m = blocks(act)

            def x_part(b):
                act.wait_ge(tx_mm, b + 1)
                nc.scalar.activation(x_hi[:, :, :].rearrange("p k t -> p (k t)"), ps[:, 1, :], ACT.Copy).then_inc(xT_a, 1)

            def slot_of(b):
                return act.value_load(expert_of[0:1, ds(b, 1)], min_val=0, max_val=E - 1) % RING

            def high_gate_up(b, slot, first):
                if not first:
                    act.wait_ge(gu_mm, b)
                for n in range(2):
                    nc.scalar.activation(gu_hi[:, PIECE * n:PIECE * (n + 1)], gu_w[:, ds(slot * WGU + PIECE * n, PIECE)], ACT.Copy).then_inc(gu_high, 1)

            def high_down(b, slot):
                for n in range(2):
                    nc.scalar.activation(dn_hi[:, PIECE * n:PIECE * (n + 1)], dn_w[:, ds(slot * WDN + PIECE * n, PIECE)], ACT.Copy).then_inc(dn_high, 1)

            def h_part(b):
                act.wait_ge(th_mm, b + 1)
                nc.scalar.activation(h_hi[:, :, :].rearrange("p k t -> p (k t)"), ps[:, 3, 0:2 * P], ACT.Copy).then_inc(hT_ev, 1)

            def y_part(b, first):
                act.wait_ge(dn_mm, b + 1)
                if not first:
                    act.wait_ge(y_out, b * 16)
                nc.scalar.activation(y[:, 0:512], ps[:, 4, :], ACT.Copy).then_inc(y_a, 1)

            def silu(b):
                act.wait_ge(gu_mm, b + 1)
                nc.scalar.activation(sg[:, :], ps[:, 0, 0:F], ACT.Silu).then_inc(sg_done, 1)

            first_slot, second_slot, third_slot = slot_of(0), slot_of(1), slot_of(2)
            x_part(0)
            high_gate_up(0, first_slot, True)
            silu(0)
            x_part(1)
            high_gate_up(1, second_slot, False)
            h_part(0)
            high_down(0, first_slot)
            act.wait_ge(hh_done, 1)
            silu(1)
            x_part(2)
            high_gate_up(2, third_slot, False)
            y_part(0, True)
            h_part(1)
            high_down(1, second_slot)
            act.wait_ge(hh_done, 2)
            silu(2)
            with act.Fori(3, m + 2) as b:
                slot, slot_before = slot_of(b), slot_of(b - 1)
                x_part(b)
                high_gate_up(b, slot, False)
                y_part(b - 2, False)
                h_part(b - 1)
                high_down(b - 1, slot_before)
                act.wait_ge(hh_done, b)
                silu(b)
            last_slot = slot_of(m + 1)
            y_part(m, False)
            h_part(m + 1)
            high_down(m + 1, last_slot)
            y_part(m + 1, False)

        @block.vector
        def _(dve):
            m = blocks(dve)

            def x_part(b):
                dve.wait_ge(tx_mm, b + 1)
                nc.vector.tensor_copy(xT[:, :, :].rearrange("p k t -> p (k t)"), ps[:, 2, :]).then_inc(xT_d, 1)
                dve.wait_ge(xT_a, b + 1)
                nc.vector.tensor_tensor(x_lo[:, :, :].rearrange("p k t -> p (k t)"), ps[:, 1, :],
                                        x_hi[:, :, :].rearrange("p k t -> p (k t)"), ALU.subtract).then_inc(x_low, 1)

            def slot_of(b):
                return dve.value_load(expert_of[0:1, ds(b, 1)], min_val=0, max_val=E - 1) % RING

            def low_gate_up(b, slot):
                for n in range(2):
                    dve.wait_ge(gu_high, 2 * b + n + 1)
                    nc.vector.tensor_tensor(gu_lo[:, PIECE * n:PIECE * (n + 1)], gu_w[:, ds(slot * WGU + PIECE * n, PIECE)],
                                            gu_hi[:, PIECE * n:PIECE * (n + 1)], ALU.subtract).then_inc(gu_low, 1)

            def h_part(b):
                dve.wait_ge(hT_ev, b + 1)
                nc.vector.tensor_tensor(h_lo[:, :, :].rearrange("p k t -> p (k t)"), ps[:, 3, 0:2 * P],
                                        h_hi[:, :, :].rearrange("p k t -> p (k t)"), ALU.subtract).then_inc(h_low, 1)

            def low_down(b, slot):
                for n in range(2):
                    dve.wait_ge(dn_high, 2 * b + n + 1)
                    nc.vector.tensor_tensor(dn_lo[:, PIECE * n:PIECE * (n + 1)], dn_w[:, ds(slot * WDN + PIECE * n, PIECE)],
                                            dn_hi[:, PIECE * n:PIECE * (n + 1)], ALU.subtract).then_inc(dn_low, 1)

            def y_part(b, first):
                dve.wait_ge(dn_mm, b + 1)
                if not first:
                    dve.wait_ge(y_out, b * 16)
                nc.vector.tensor_copy(y[:, 512:1024], ps[:, 5, :]).then_inc(y_d, 1)

            def hidden(b, first):
                dve.wait_ge(sg_done, b + 1)
                if not first:
                    dve.wait_ge(th_mm, b)
                nc.vector.tensor_tensor(hh[:, :], sg[:, :], ps[:, 0, F:2 * F], ALU.mult).then_inc(hh_done, 1)

            first_slot, second_slot, third_slot = slot_of(0), slot_of(1), slot_of(2)
            x_part(0)
            low_gate_up(0, first_slot)
            hidden(0, True)
            x_part(1)
            low_gate_up(1, second_slot)
            h_part(0)
            low_down(0, first_slot)
            hidden(1, False)
            x_part(2)
            low_gate_up(2, third_slot)
            y_part(0, True)
            h_part(1)
            low_down(1, second_slot)
            hidden(2, False)
            with dve.Fori(3, m + 2) as b:
                slot, slot_before = slot_of(b), slot_of(b - 1)
                x_part(b)
                low_gate_up(b, slot)
                y_part(b - 2, False)
                h_part(b - 1)
                low_down(b - 1, slot_before)
                hidden(b, False)
            last_slot = slot_of(m + 1)
            y_part(m, False)
            h_part(m + 1)
            low_down(m + 1, last_slot)
            y_part(m + 1, False)

        @block.tensor
        def _(pe):
            m = blocks(pe)

            def expert(b):
                return pe.value_load(expert_of[0:1, ds(b, 1)], min_val=0, max_val=E - 1)

            def turn_x(b):
                pe.wait_ge(gu_in, expert(b) * 16 + 16)
                pe.wait_ge(x_in, b * 16 + 16)
                for k in range(KD):
                    last = nc.tensor.transpose(ps[:, 1 + k // 4, (k % 4) * P:(k % 4 + 1) * P], x[:, k * P:(k + 1) * P], ident)
                last.then_inc(tx_mm, 1)

            def gate_up(b, first):
                at = expert(b) % RING * WGU
                pe.wait_ge(xT_d, b + 1)
                if not first:
                    pe.wait_ge(hh_done, b)
                half = KD // 2
                for k in range(half):
                    nc.tensor.matmul(ps[:, 0, :], xT[:, k, :], gu_w[:, ds(at + (half + k) * 2 * F, 2 * F)], start=(k == 0), stop=False)
                pe.wait_ge(x_low, b + 1)
                pe.wait_ge(gu_low, 2 * b + 2)
                cols = lambda k: slice(k * 2 * F, (k + 1) * 2 * F)
                split_product(nc, ps[:, 0, :], [((x_hi[:, k, :], x_lo[:, k, :]), (gu_hi[:, cols(k)], gu_lo[:, cols(k)])) for k in range(half)],
                              start=False).then_inc(gu_mm, 1)

            def turn_h(b):
                pe.wait_ge(dn_in, expert(b) * 16 + 16)
                pe.wait_ge(hh_done, b + 1)
                for k in range(2):
                    last = nc.tensor.transpose(ps[:, 3, k * P:(k + 1) * P], hh[:, k * P:(k + 1) * P], ident)
                last.then_inc(th_mm, 1)

            def down(b, first):
                pe.wait_ge(h_low, b + 1)
                pe.wait_ge(dn_low, 2 * b + 2)
                if not first:
                    pe.wait_ge(y_a, b)
                    pe.wait_ge(y_d, b)
                for half in range(2):
                    cols = lambda k: slice(k * D + 512 * half, k * D + 512 * (half + 1))
                    last = split_product(nc, ps[:, 4 + half, :], [((h_hi[:, k, :], h_lo[:, k, :]), (dn_hi[:, cols(k)], dn_lo[:, cols(k)]))
                                                                  for k in range(2)])
                last.then_inc(dn_mm, 1)

            turn_x(0)
            gate_up(0, True)
            turn_x(1)
            turn_h(0)
            gate_up(1, False)
            turn_x(2)
            down(0, True)
            turn_h(1)
            gate_up(2, False)
            with pe.Fori(3, m + 2) as b:
                turn_x(b)
                down(b - 2, False)
                turn_h(b - 1)
                gate_up(b, False)
            down(m, False)
            turn_h(m + 1)
            down(m + 1, False)


def final_block(nc, a, ps, chains, rows_in, const, h1, y_dram, comb, g2, b2, out):
    ctx = ExitStack()
    with ctx:
        sb = lambda n, s, d=F32: ctx.enter_context(nc.sbuf_tensor(n, s, d))
        sem = lambda n: ctx.enter_context(nc.semaphore(n))
        yy = sb("yy", [P, NT, 2, D])
        stats = sb("stats2", [P, 2, 12])
        mv = sb("mv2", [P, NT, 2])
        rstd = sb("rstd2", [P, NT])
        shift = sb("shift2", [P, NT])
        stats_done, rstd_done, shifted, normed, gained, done, out_s = (sem("g_" + n) for n in
            ("stats", "rstd", "shifted", "normed", "gained", "done", "out"))
        done_late = sem("g_done_late")
        POOL_TILES = NT - 2
        block = ctx.enter_context(nc.Block())

        @block.sync
        def _(sp):
            for t in range(NT):
                for j in range(2):
                    sp.dma_start(yy[:, t, j, :], y_dram[T * j + P * t:T * j + P * (t + 1), :]).then_inc(rows_in[t], 16)
            for t in range(NT):
                if t < POOL_TILES:
                    sp.wait_ge(done, t + 1)
                else:
                    sp.wait_ge(done_late, t + 1 - POOL_TILES)
                sp.dma_start(out[0, P * t:P * (t + 1), :], h1[:, t, :]).then_inc(out_s, 16)
            sp.wait_ge(out_s, 16 * NT)

        @block.gpsimd
        def _(pool):
            chain = chains["gpsimd"]

            def factors(t):
                pool.wait_ge(stats_done, t + 1)
                ins = inverse_root(pool, chain, const, rstd[:, t:t + 1], mv[:, t, 1:2], 1.0)
                ins.then_inc(rstd_done, 1)
                pool.wait_ge(rstd_done, t + 1)
                chain(pool.tensor_scalar(shift[:, t:t + 1], mv[:, t, 0:1], -1.0, None, ALU.mult))
                pool.tensor_tensor(shift[:, t:t + 1], shift[:, t:t + 1], rstd[:, t:t + 1], ALU.mult).then_inc(shifted, 1)

            factors(0)
            for t in range(NT):
                if t + 1 < NT:
                    factors(t + 1)
                if t < POOL_TILES:
                    pool.wait_ge(gained, t + 1)
                    pool.tensor_tensor(h1[:, t, :], h1[:, t, :], b2[:, :], ALU.add).then_inc(done, 1)

        @block.scalar
        def _(act):
            for t in range(NT):
                act.wait_ge(shifted, t + 1)
                nc.scalar.activation(h1[:, t, :], h1[:, t, :], ACT.Identity, scale=rstd[:, t:t + 1], bias=shift[:, t:t + 1]).then_inc(normed, 1)

        @block.vector
        def _(dve):
            v = nc.vector
            chain = chains["vector"]
            for t in range(NT + 2):
                if t < NT:
                    dve.wait_ge(rows_in[t], 48)
                    chain(v.scalar_tensor_tensor(h1[:, t, :], yy[:, t, 0, :], comb[:, 0, t:t + 1], h1[:, t, :], ALU.mult, ALU.add))
                    chain(v.scalar_tensor_tensor(h1[:, t, :], yy[:, t, 1, :], comb[:, 1, t:t + 1], h1[:, t, :], ALU.mult, ALU.add))
                    for b in range(2):
                        chain(v.bn_stats(stats[:, t % 2, 6 * b:6 * b + 6], h1[:, t, 512 * b:512 * (b + 1)]))
                    v.bn_aggr(mv[:, t, :], stats[:, t % 2, :]).then_inc(stats_done, 1)
                if t >= 2:
                    dve.wait_ge(normed, t - 1)
                    v.tensor_tensor(h1[:, t - 2, :], h1[:, t - 2, :], g2[:, :], ALU.mult).then_inc(gained, 1)
                    if t - 2 >= POOL_TILES:
                        dve.wait_ge(gained, t - 1)
                        v.tensor_tensor(h1[:, t - 2, :], h1[:, t - 2, :], b2[:, :], ALU.add).then_inc(done_late, 1)


def program(nc, a, out):
    h_dram = nc.dram_tensor("h_dram", [T, D], F32, kind="Internal").ap()
    h1_dram = nc.dram_tensor("h1_dram", [T, D], F32, kind="Internal").ap()
    y_dram = nc.dram_tensor("y_dram", [2 * T, D], F32, kind="Internal").ap()
    ps = nc.alloc_psum_tensor("ps", [P, 8, 512], F32)
    rows_in = [nc.alloc_semaphore(f"rows_in{t}") for t in range(NT)]
    chains = {"vector": Chain(nc.vector, nc.alloc_semaphore("vector_link")), "gpsimd": Chain(nc.gpsimd, nc.alloc_semaphore("gpsimd_link"))}
    with (nc.sbuf_tensor("const", [P, K_END], F32) as const, nc.sbuf_tensor("logits", [P, NT, G + E], F32) as logits,
          nc.sbuf_tensor("h1", [P, NT, D], F32) as h1):
        early, at = h1[:, :, :].rearrange("p t d -> p (t d)"), 0

        def piece(*dims):
            nonlocal at
            size = int(np.prod(dims))
            v = early[:, at:at + size]
            at += size
            if len(dims) == 2:
                v = v.rearrange("p (a b) -> p a b", a=dims[0])
            return v

        u, cw, v_meta = piece(NC4, UW), piece(NC4, TAPS + 1), piece(H * VD)
        z, zT, q_t, k_t = piece(ZR), piece(5, P), piece(H, QK), piece(H, QK)
        assert at <= NT * D
        with nc.sbuf_tensor("acc", [P, NC4, T], F32) as acc, nc.sbuf_tensor("hT", [P, KD, META + T], F32) as hT:
            flat = hT[:, :, :].rearrange("p k t -> p (k t)")
            o_all = flat[:, 0:NT * C].rearrange("p (t c) -> p t c", c=C)
            p = flat[:, NT * C:NT * C + 2 * T].rearrange("p (b n) -> p b n", b=2)
            pT = flat[:, NT * C + 2 * T:NT * C + 4 * T].rearrange("p (b k n) -> p b k n", b=2, n=P)
            junk = flat[:, NT * C:2 * NT * C].rearrange("p (t c) -> p t c", c=C)
            with (nc.sbuf_tensor("wo", [P, KD, D], F32) as w_o, nc.sbuf_tensor("g_o", [P, KD], F32) as g_o,
                  nc.sbuf_tensor("qg", [P, 5], F32) as qg):
                first = w_o[:, :, :].rearrange("p k d -> p (k d)")
                w_z = first[:, 0:KD * ZR].rearrange("p (k n) -> p k n", k=KD)
                w_q = first[:, KD * ZR:KD * ZR + 3 * H * QK].rearrange("p (k n) -> p k n", k=3)
                w_kv0 = acc[:, 3, :]
                input_block(nc, a, ps, chains, const, hT, u, acc, cw, h_dram, first, w_z, w_q, w_kv0, qg[:, :])
                with (nc.sbuf_tensor("qT", [QK + 1, H, T], F32) as qT, nc.sbuf_tensor("kT", [QK + 1, H, META + T], F32) as kT,
                      nc.sbuf_tensor("v_all", [P, NT + 1, H * VD], F32) as v_all):
                    mixer_block(nc, a, ps, chains, const, hT, u, acc, cw, qT, kT, v_all, v_meta, z, zT, q_t, k_t, w_z, w_q, w_kv0, qg)
                    attention_block(nc, a, ps, chains, const, u, acc, cw, qT, kT, v_all, v_meta, o_all, p, pT, w_o, g_o)
                merge_block(nc, a, ps, chains, rows_in, const, acc, o_all, junk, w_o, h_dram, h1, h1_dram, logits)
        with (nc.sbuf_tensor("comb", [P, 2, NT], F32) as comb, nc.sbuf_tensor("row_of", [P, MAXB + 1], I32) as row_of,
              nc.sbuf_tensor("token_of", [P, MAXB + 1], I32) as token_of, nc.sbuf_tensor("expert_of", [1, MAXB + 1], I32) as expert_of,
              nc.sbuf_tensor("g2", [P, D], F32) as g2, nc.sbuf_tensor("b2", [P, D], F32) as b2,
              nc.sbuf_tensor("blocks_to", [1, E], I32) as blocks_to, nc.sbuf_tensor("n_blocks", [1, 1], I32) as n_blocks):
            with (nc.sbuf_tensor("gu_w", [P, RING * WGU], F32) as gu_w, nc.sbuf_tensor("dn_w", [P, RING * WDN], F32) as dn_w,
                  nc.semaphore("gu_in") as gu_in, nc.semaphore("dn_in") as dn_in):
                route_block(nc, a, ps, chains, const, logits, comb, row_of, token_of, expert_of, blocks_to, n_blocks, gu_w, dn_w, gu_in, dn_in)
                expert_block(nc, a, ps, chains, const, h1, h1_dram, y_dram, row_of, token_of, expert_of, blocks_to, n_blocks, gu_w, dn_w, gu_in, dn_in, g2, b2)
            final_block(nc, a, ps, chains, rows_in, const, h1, y_dram, comb, g2, b2, out)


def kernel(**inputs):
    import numpy as _np
    import concourse.bacc as _bacc
    from concourse import mybir as _mybir
    from concourse.bass_utils import run_bass_kernel_spmd as _run

    i = {k: _np.asarray(v) for k, v in inputs.items()}
    tile = lambda w: w.reshape(w.shape[0] // P, P, -1).transpose(1, 0, 2)
    w_in = i["w_in"][0]
    conv = tile(w_in[:, :2 * C]).reshape(P, KD, 2, NC4, P).transpose(0, 3, 1, 2, 4).reshape(P, NC4, KD * 2 * P)
    kv = i["w_ukv"][0].reshape(KVL, H, 2, NOPE).transpose(0, 2, 1, 3).reshape(KVL, 2 * H * NOPE)
    experts = lambda w: w.reshape(E, w.shape[1] // P, P, w.shape[2]).transpose(0, 2, 1, 3)
    arrays = {
        "x": i["x"], "meta_tokens": i["meta_tokens"], "ln_in_g": i["ln_in_g"], "ln_in_b": i["ln_in_b"],
        "ln1_g": i["ln1_g"], "ln1_b": i["ln1_b"], "ln2_g": i["ln2_g"], "ln2_b": i["ln2_b"],
        "consts": constants(),
        "w_conv_in": conv,
        "w_z": tile(w_in[:, 2 * C:]),
        "w_q": tile(i["w_uq"][0]),
        "w_kv": tile(kv),
        "qkv_g": _np.concatenate([i["q_norm_g"][0].reshape(3, P).T, i["kv_norm_g"][0].reshape(2, P).T], 1),
        "conv_wb": _np.concatenate([i["conv_w"][0].reshape(TAPS, NC4, P), i["conv_b"][0].reshape(1, NC4, P)]).transpose(2, 1, 0),
        "conv_ln": _np.stack([i["conv_ln_g"][0].reshape(NC4, P), i["conv_ln_b"][0].reshape(NC4, P)]).transpose(2, 0, 1),
        "out_g": _np.concatenate([i["conv_out_g"][0], i["attn_out_g"][0]]).reshape(KD, P).T,
        "w_o": tile(i["w_o"][0]),
        "w_r": tile(_np.concatenate([i["w_rg"][0], i["w_re"][0]], 1)),
        "b_r": _np.concatenate([i["b_rg"], i["b_re"]], 1),
        "w_gate_up": _np.concatenate([experts(i["w_gate"][0]), experts(i["w_up"][0])], 3).reshape(E, P, WGU),
        "w_down_t": experts(i["w_down"][0]).reshape(E, P, WDN),
    }
    arrays = {k + "_in": _np.ascontiguousarray(v) for k, v in arrays.items()}
    nc = _bacc.Bacc("TRN2", target_bir_lowering=False, num_devices=1)
    aps = {k[:-3]: nc.dram_tensor(k, v.shape, _mybir.dt.from_np(v.dtype), kind="ExternalInput").ap() for k, v in arrays.items()}
    out = nc.dram_tensor("out_0", (1, T, D), _mybir.dt.float32, kind="ExternalOutput").ap()
    program(nc, aps, out)
    r = _run(nc, [arrays], core_ids=[0])
    return r.results[0]["out_0"]
```
